# Optimizing a Trainium2 kernel written in Bass

```python
import jax
import jax.numpy as jnp
from jax import lax
import numpy as np
import math
import jax, jax.numpy as jnp

D_MODEL = 1024
BATCH = 1
SEQ = 256
DEPTH = 2

GRID_W = 64
CTX_LEN = 256
NORM_EPS = 1e-6

MLA_HEADS = 8
MLA_Q_RANK = 256
MLA_KV_RANK = 128
MLA_NOPE = 64
MLA_ROPE = 32
MLA_V = 64
MLA_WIDTH = MLA_HEADS * MLA_V
ROPE_BASE = 10000.0
Q_BLOCK = 128

POOL_WINDOWS = (2, 4, 8, 16)
POOL_WIDTH = 512
POOL_GROUP = POOL_WIDTH // len(POOL_WINDOWS)

GLA_HEADS = 4
GLA_DK = 64
GLA_DV = 128
GLA_KW = GLA_HEADS * GLA_DK
GLA_WIDTH = GLA_HEADS * GLA_DV
GLA_GATE_RANK = 16
GLA_TAU = 16.0
GLA_CHUNK = 64

N_BRANCH = 3

IN_NAMES = ('mla_q', 'mla_kv', 'mla_kr', 'mla_gate', 'pool_x', 'pool_gate',
            'gla_q', 'gla_k', 'gla_v', 'gla_af', 'gla_ab', 'gla_gate', 'merge')
IN_SIZES = (MLA_Q_RANK, MLA_KV_RANK, MLA_ROPE, MLA_WIDTH, POOL_WIDTH, POOL_WIDTH,
            GLA_KW, GLA_KW, GLA_WIDTH, GLA_GATE_RANK, GLA_GATE_RANK, GLA_WIDTH, N_BRANCH * D_MODEL)
D_IN = sum(IN_SIZES)


def rmsnorm(x, g):
    xf = x.astype(jnp.float32)
    y = xf * lax.rsqrt(jnp.mean(xf * xf, axis=-1, keepdims=True) + NORM_EPS)
    return (y * g.astype(jnp.float32)).astype(x.dtype)

def split_columns(z):
    offsets = [int(o) for o in np.cumsum(IN_SIZES)[:-1]]
    return dict(zip(IN_NAMES, jnp.split(z, offsets, axis=-1)))

def flip(t):
    return t[:, ::-1]

def axial_rope_tables(row, col):
    half = MLA_ROPE // 2
    inv = ROPE_BASE ** (-jnp.arange(0, half, 2, dtype=jnp.float32) / half)
    ang_r = row.astype(jnp.float32)[:, None] * inv
    ang_c = col.astype(jnp.float32)[:, None] * inv
    ang = jnp.concatenate([ang_r, ang_r, ang_c, ang_c], axis=-1)
    return jnp.cos(ang), jnp.sin(ang)

def apply_rope(x, cos, sin):
    half = MLA_ROPE // 2
    quarter = half // 2

    def rot(v):
        return jnp.concatenate([-v[..., quarter:], v[..., :quarter]], axis=-1)

    rotated = jnp.concatenate([rot(x[..., :half]), rot(x[..., half:])], axis=-1)
    return (x * cos + rotated * sin).astype(x.dtype)

def softmax_attention(q, k, v, scale):
    s = jnp.einsum('bqhd,bkhd->bhqk', q, k).astype(jnp.float32) * scale
    p = jax.nn.softmax(s, axis=-1).astype(v.dtype)
    return jnp.einsum('bhqk,bkhd->bqhd', p, v)

def blocked_attention(q, k, v, scale):
    B, L, H, dk = q.shape
    nblk = L // Q_BLOCK
    qb = q.reshape(B, nblk, Q_BLOCK, H, dk).transpose(1, 0, 2, 3, 4)
    ob = lax.map(lambda qq: softmax_attention(qq, k, v, scale), qb)
    return ob.transpose(1, 0, 2, 3, 4).reshape(B, L, H, v.shape[-1])

def mla_queries(zz, q_norm, w_uq):
    B, L, _ = zz['mla_q'].shape
    q = (rmsnorm(zz['mla_q'], q_norm) @ w_uq).reshape(B, L, MLA_HEADS, MLA_NOPE + MLA_ROPE)
    return q[..., :MLA_NOPE], q[..., MLA_NOPE:]

def mla_keys_values(zz, kv_norm, w_ukv):
    B, L, _ = zz['mla_kv'].shape
    kv = (rmsnorm(zz['mla_kv'], kv_norm) @ w_ukv).reshape(B, L, MLA_HEADS, MLA_NOPE + MLA_V)
    return kv[..., :MLA_NOPE], kv[..., MLA_NOPE:]

def assemble_keys(k_nope, k_rope):
    B, L, H, _ = k_nope.shape
    return jnp.concatenate([k_nope, jnp.broadcast_to(k_rope[:, :, None, :], (B, L, H, MLA_ROPE))], axis=-1)

def mla_branch(z, zc, cos, sin, q_norm, w_uq, kv_norm, w_ukv, with_ctx_out):
    B, L, _ = z['mla_q'].shape
    scale = (MLA_NOPE + MLA_ROPE) ** -0.5
    q_nope, q_rope = mla_queries(z, q_norm, w_uq)
    q = jnp.concatenate([q_nope, apply_rope(q_rope, cos[:, None, :], sin[:, None, :])], axis=-1)
    k_nope, v = mla_keys_values(z, kv_norm, w_ukv)
    k = assemble_keys(k_nope, apply_rope(z['mla_kr'], cos, sin))
    kc_nope, vc = mla_keys_values(zc, kv_norm, w_ukv)
    kc = assemble_keys(kc_nope, zc['mla_kr'])
    k_all = jnp.concatenate([kc, k], axis=1)
    v_all = jnp.concatenate([vc, v], axis=1)
    y = blocked_attention(q, k_all, v_all, scale).reshape(B, L, MLA_WIDTH)
    y = y * jax.nn.silu(z['mla_gate'])
    if with_ctx_out:
        Bc, Lc, _ = zc['mla_q'].shape
        qc = jnp.concatenate(mla_queries(zc, q_norm, w_uq), axis=-1)
        yc = softmax_attention(qc, kc, vc, scale).reshape(Bc, Lc, MLA_WIDTH) * jax.nn.silu(zc['mla_gate'])
    else:
        yc = None
    return y, yc

def multiscale_pool(u):
    B, L, W = u.shape
    uf = u.astype(jnp.float32)
    csum = jnp.concatenate([jnp.zeros((B, 1, W), jnp.float32), jnp.cumsum(uf, axis=1)], axis=1)
    t = jnp.arange(L)
    outs = []
    for g, w in enumerate(POOL_WINDOWS):
        lo = jnp.clip(t - w // 2, 0, L)
        hi = jnp.clip(t + w // 2, 0, L)
        cs = csum[..., g * POOL_GROUP:(g + 1) * POOL_GROUP]
        count = (hi - lo).astype(jnp.float32)[None, :, None]
        outs.append((jnp.take(cs, hi, axis=1) - jnp.take(cs, lo, axis=1)) / count)
    return (jnp.concatenate(outs, axis=-1) - uf).astype(u.dtype)

def pool_branch(zz, pool_w, pool_scale):
    B, L, _ = zz['pool_x'].shape
    pooled = multiscale_pool(zz['pool_x']).reshape(B, L, len(POOL_WINDOWS), POOL_GROUP)
    mixed = jnp.einsum('blgi,gio->blgo', pooled, pool_w).reshape(B, L, POOL_WIDTH)
    return mixed * pool_scale * jax.nn.silu(zz['pool_gate'])

def gla_scan(q, k, v, log_a, s0, with_out):
    B, L, H, _ = q.shape
    n = L // GLA_CHUNK

    def to_chunks(t):
        return t.reshape(B, n, GLA_CHUNK, H, t.shape[-1]).transpose(1, 0, 3, 2, 4)

    mask = jnp.tril(jnp.ones((GLA_CHUNK, GLA_CHUNK), bool))[:, :, None]

    def step(s, inp):
        qq, kk, vv, aa = inp
        b = jnp.cumsum(aa, axis=2)
        b_last = b[:, :, -1:, :]
        s_new = jnp.exp(b_last)[:, :, 0, :, None] * s + jnp.einsum('bhcd,bhce->bhde', kk * jnp.exp(b_last - b), vv)
        if not with_out:
            return s_new, None
        inter = jnp.einsum('bhcd,bhde->bhce', qq * jnp.exp(b), s)
        decay = jnp.exp(jnp.where(mask, b[:, :, :, None, :] - b[:, :, None, :, :], -jnp.inf))
        attn = jnp.einsum('bhid,bhjd,bhijd->bhij', qq, kk, decay)
        intra = jnp.einsum('bhij,bhje->bhie', attn, vv)
        return s_new, inter + intra

    s_fin, out = lax.scan(step, s0, (to_chunks(q), to_chunks(k), to_chunks(v), to_chunks(log_a)))
    if with_out:
        out = out.transpose(1, 0, 3, 2, 4).reshape(B, L, H, v.shape[-1])
    return s_fin, out

def gla_inputs(zz, af_w2, af_b, ab_w2, ab_b):
    B, L, _ = zz['gla_v'].shape
    f32 = jnp.float32
    q = zz['gla_q'].astype(f32).reshape(B, L, GLA_HEADS, GLA_DK) * GLA_DK ** -0.5
    k = zz['gla_k'].astype(f32).reshape(B, L, GLA_HEADS, GLA_DK)
    v = zz['gla_v'].astype(f32).reshape(B, L, GLA_HEADS, GLA_DV)
    log_a_f = (jax.nn.log_sigmoid((zz['gla_af'] @ af_w2 + af_b).astype(f32)) / GLA_TAU).reshape(B, L, GLA_HEADS, GLA_DK)
    log_a_b = (jax.nn.log_sigmoid((zz['gla_ab'] @ ab_w2 + ab_b).astype(f32)) / GLA_TAU).reshape(B, L, GLA_HEADS, GLA_DK)
    return q, k, v, log_a_f, log_a_b

def gla_output(o, zz, g):
    B, L = o.shape[:2]
    o = rmsnorm(o, g).reshape(B, L, GLA_WIDTH).astype(zz['gla_gate'].dtype)
    return o * jax.nn.silu(zz['gla_gate'])

def gla_branch(z, zc, af_w2, af_b, ab_w2, ab_b, gla_norm, with_ctx_out):
    qc, kc, vc, afc, abc = gla_inputs(zc, af_w2, af_b, ab_w2, ab_b)
    s0 = jnp.zeros((qc.shape[0], GLA_HEADS, GLA_DK, GLA_DV), jnp.float32)
    sc_f, oc_f = gla_scan(qc, kc, vc, afc, s0, with_ctx_out)
    sc_b, oc_b = gla_scan(flip(qc), flip(kc), flip(vc), flip(abc), s0, with_ctx_out)
    q, k, v, af, ab = gla_inputs(z, af_w2, af_b, ab_w2, ab_b)
    _, o_f = gla_scan(q, k, v, af, sc_f, True)
    _, o_b = gla_scan(flip(q), flip(k), flip(v), flip(ab), sc_b, True)
    y = gla_output(o_f + flip(o_b), z, gla_norm)
    yc = gla_output(oc_f + flip(oc_b), zc, gla_norm) if with_ctx_out else None
    return y, yc

def merge_branches(zz, y_mla, y_pool, y_gla, w_bm, w_bp, w_bg, w_out):
    gates = jax.nn.sigmoid(zz['merge'].astype(jnp.float32)).astype(y_mla.dtype)
    g_mla, g_pool, g_gla = jnp.split(gates, N_BRANCH, axis=-1)
    merged = g_mla * (y_mla @ w_bm) + g_pool * (y_pool @ w_bp) + g_gla * (y_gla @ w_bg)
    return merged @ w_out

def trunk_layer(x, xc, mod, mod_c, cos, sin, pre_g, post_g, w_in, mla_q_norm, mla_w_uq, mla_kv_norm,
                mla_w_ukv, pool_w, pool_scale, gla_af_w2, gla_af_b, gla_ab_w2, gla_ab_b, gla_norm,
                w_branch_mla, w_branch_pool, w_branch_gla, w_out, with_ctx_out):
    shift, scale, gate = jnp.split(mod[:, None, :], 3, axis=-1)
    shift_c, scale_c, gate_c = jnp.split(mod_c[None, None, :], 3, axis=-1)
    z = split_columns((rmsnorm(x, pre_g) * (1 + scale) + shift) @ w_in)
    zc = split_columns((rmsnorm(xc, pre_g) * (1 + scale_c) + shift_c) @ w_in)
    y_mla, yc_mla = mla_branch(z, zc, cos, sin, mla_q_norm, mla_w_uq, mla_kv_norm, mla_w_ukv, with_ctx_out)
    y_pool = pool_branch(z, pool_w, pool_scale)
    y_gla, yc_gla = gla_branch(z, zc, gla_af_w2, gla_af_b, gla_ab_w2, gla_ab_b, gla_norm, with_ctx_out)
    out = merge_branches(z, y_mla, y_pool, y_gla, w_branch_mla, w_branch_pool, w_branch_gla, w_out)
    x = x + gate * rmsnorm(out, post_g)
    if with_ctx_out:
        yc_pool = pool_branch(zc, pool_w, pool_scale)
        out_c = merge_branches(zc, yc_mla, yc_pool, yc_gla, w_branch_mla, w_branch_pool, w_branch_gla, w_out)
        xc = xc + gate_c * rmsnorm(out_c, post_g)
    return x, xc

def first_inputs(seed: int = 0) -> dict:
    key = jax.random.key(seed)
    ks = jax.random.split(key, 24)
    f32 = jnp.float32

    def nrm(k, shape, s):
        return jax.random.normal(k, shape, f32) * s

    def gain(k, n):
        return 1.0 + 0.1 * jax.random.normal(k, (DEPTH, n), f32)

    return {
        'x': nrm(ks[0], (BATCH, SEQ, D_MODEL), 1.0),
        'c': nrm(ks[1], (BATCH, D_MODEL), 1.0),
        'ctx': nrm(ks[2], (BATCH, CTX_LEN, D_MODEL), 1.0),
        'c_ctx': nrm(ks[3], (D_MODEL,), 1.0),
        'mod_w': nrm(ks[4], (DEPTH, D_MODEL, 3 * D_MODEL), 0.5 * D_MODEL ** -0.5),
        'mod_b': nrm(ks[5], (DEPTH, 3 * D_MODEL), 0.02),
        'pre_norm': gain(ks[6], D_MODEL),
        'post_norm': gain(ks[7], D_MODEL),
        'w_in': nrm(ks[8], (DEPTH, D_MODEL, D_IN), D_MODEL ** -0.5),
        'mla_q_norm': gain(ks[9], MLA_Q_RANK),
        'mla_w_uq': nrm(ks[10], (DEPTH, MLA_Q_RANK, MLA_HEADS * (MLA_NOPE + MLA_ROPE)), MLA_Q_RANK ** -0.5),
        'mla_kv_norm': gain(ks[11], MLA_KV_RANK),
        'mla_w_ukv': nrm(ks[12], (DEPTH, MLA_KV_RANK, MLA_HEADS * (MLA_NOPE + MLA_V)), MLA_KV_RANK ** -0.5),
        'pool_w': nrm(ks[13], (DEPTH, len(POOL_WINDOWS), POOL_GROUP, POOL_GROUP), POOL_GROUP ** -0.5),
        'pool_scale': gain(ks[14], POOL_WIDTH),
        'gla_af_w2': nrm(ks[15], (DEPTH, GLA_GATE_RANK, GLA_KW), GLA_GATE_RANK ** -0.5),
        'gla_af_b': nrm(ks[16], (DEPTH, GLA_KW), 0.1),
        'gla_ab_w2': nrm(ks[17], (DEPTH, GLA_GATE_RANK, GLA_KW), GLA_GATE_RANK ** -0.5),
        'gla_ab_b': nrm(ks[18], (DEPTH, GLA_KW), 0.1),
        'gla_norm': gain(ks[19], GLA_DV),
        'w_branch_mla': nrm(ks[20], (DEPTH, MLA_WIDTH, D_MODEL), MLA_WIDTH ** -0.5),
        'w_branch_pool': nrm(ks[21], (DEPTH, POOL_WIDTH, D_MODEL), POOL_WIDTH ** -0.5),
        'w_branch_gla': nrm(ks[22], (DEPTH, GLA_WIDTH, D_MODEL), GLA_WIDTH ** -0.5),
        'w_out': nrm(ks[23], (DEPTH, D_MODEL, D_MODEL), D_MODEL ** -0.5),
    }

def first_block(x, c, ctx, c_ctx, mod_w, mod_b, pre_norm, post_norm, w_in, mla_q_norm, mla_w_uq,
              mla_kv_norm, mla_w_ukv, pool_w, pool_scale, gla_af_w2, gla_af_b, gla_ab_w2, gla_ab_b,
              gla_norm, w_branch_mla, w_branch_pool, w_branch_gla, w_out):
    n_tok = x.shape[1]
    rows = n_tok // GRID_W
    row = jnp.repeat(jnp.arange(rows), GRID_W)
    col = jnp.tile(jnp.arange(GRID_W), rows)
    cos, sin = axial_rope_tables(row, col)
    silu_c = jax.nn.silu(c)
    silu_cc = jax.nn.silu(c_ctx)
    xc = ctx
    for l in range(DEPTH):
        mod = silu_c @ mod_w[l] + mod_b[l]
        mod_c = silu_cc @ mod_w[l] + mod_b[l]
        x, xc = trunk_layer(x, xc, mod, mod_c, cos, sin, pre_norm[l], post_norm[l], w_in[l],
                            mla_q_norm[l], mla_w_uq[l], mla_kv_norm[l], mla_w_ukv[l], pool_w[l],
                            pool_scale[l], gla_af_w2[l], gla_af_b[l], gla_ab_w2[l], gla_ab_b[l],
                            gla_norm[l], w_branch_mla[l], w_branch_pool[l], w_branch_gla[l], w_out[l],
                            l < DEPTH - 1)
    return x


DEPTH_2 = 1

RWKV_WIDTH = D_MODEL // 2
RWKV_HEAD = 64
RWKV_HEADS = RWKV_WIDTH // RWKV_HEAD
DECAY_RANK = 64
AAA_RANK = 64
GATE_RANK = 128
RWKV_SPLITS = (RWKV_WIDTH, 2 * RWKV_WIDTH, 3 * RWKV_WIDTH,
               3 * RWKV_WIDTH + DECAY_RANK, 3 * RWKV_WIDTH + DECAY_RANK + AAA_RANK)
N_RWKV_COLS = 3 * RWKV_WIDTH + DECAY_RANK + AAA_RANK + GATE_RANK
LNX_EPS = 64e-5
S5_WIDTH = D_MODEL // 2
S5_GROUP = 16
S5_GROUPS = S5_WIDTH // S5_GROUP
S5_STATE = 64
STEP_MIN = 1e-3
STEP_MAX = 1e-1
N_IN_COLS = N_RWKV_COLS + S5_WIDTH + 2 * D_MODEL
D_FF = 256 * ((8 * D_MODEL // 3 + 255) // 256)
CONV_WIDTH = 3


def rms_norm(x, g):
    xf = x.astype(jnp.float32)
    y = xf * lax.rsqrt(jnp.mean(xf * xf, axis=-1, keepdims=True) + NORM_EPS)
    return y.astype(x.dtype) * g

def token_shift(p, mu):
    prev = jnp.pad(p, ((0, 0), (1, 0), (0, 0)))[:, :-1]
    return p + (prev - p) * mu

def wkv7_scan(r, decay, k, v, a_vec, b_vec):
    bsz, _, nh, n = r.shape

    def step(S, inp):
        r_t, w_t, k_t, v_t, a_t, b_t = inp
        sa = jnp.einsum('bhij,bhj->bhi', S, a_t)
        S = (S * w_t[:, :, None, :] + sa[..., None] * b_t[:, :, None, :]
             + v_t[..., None] * k_t[:, :, None, :])
        return S, jnp.einsum('bhij,bhj->bhi', S, r_t)

    xs = tuple(jnp.moveaxis(t, 1, 0) for t in (r, decay, k, v, a_vec, b_vec))
    S0 = jnp.zeros((bsz, nh, n, n), jnp.float32)
    _, ys = lax.scan(step, S0, xs)
    return jnp.moveaxis(ys, 0, 1)

def rwkv7_branch(p, mu, w0, w2, a0, a2, g2, k_k, k_a, r_k, lnx_w, lnx_b):
    dtype = p.dtype
    f32 = jnp.float32
    bsz, L, _ = p.shape
    p = token_shift(p.astype(f32), mu.astype(f32))
    r, k, v, wd, ad, gd = jnp.split(p, RWKV_SPLITS, axis=-1)
    w = -jax.nn.softplus(-(w0 + jnp.tanh(wd) @ w2)) - 0.5
    decay = jnp.exp(-jnp.exp(w))
    a = jax.nn.sigmoid(a0 + ad @ a2)
    g = jax.nn.sigmoid(gd) @ g2
    hs = (bsz, L, RWKV_HEADS, RWKV_HEAD)
    kk = (k * k_k).reshape(hs)
    kk = kk / jnp.maximum(jnp.linalg.norm(kk, axis=-1, keepdims=True), 1e-12)
    k = k * (1.0 + (a - 1.0) * k_a)
    rh, kh, vh = r.reshape(hs), k.reshape(hs), v.reshape(hs)
    ah = a.reshape(hs)
    y = wkv7_scan(rh, decay.reshape(hs), kh, vh, -kk, kk * ah)
    mean = jnp.mean(y, axis=-1, keepdims=True)
    var = jnp.mean(jnp.square(y - mean), axis=-1, keepdims=True)
    y = ((y - mean) * lax.rsqrt(var + LNX_EPS)).reshape(bsz, L, RWKV_WIDTH) * lnx_w + lnx_b
    bonus = jnp.sum(rh * kh * r_k, axis=-1, keepdims=True) * vh
    y = (y + bonus.reshape(bsz, L, RWKV_WIDTH)) * g
    return y.astype(dtype)

def s5_combine(left, right):
    a_i, b_i = left
    a_j, b_j = right
    return a_j * a_i, a_j * b_i + b_j

def s5_branch(u, a_re, a_im, b_re, b_im, c_re, c_im, d, log_step, w_glu, b_glu):
    f32 = jnp.float32
    bsz, L, _ = u.shape
    lam = lax.complex(a_re.astype(f32), a_im.astype(f32))
    dt = jnp.exp(log_step.astype(f32))[:, None]
    a_bar = jnp.exp(lam * dt)
    b_bar = ((a_bar - 1.0) / lam)[..., None] * lax.complex(b_re.astype(f32), b_im.astype(f32))
    c = lax.complex(c_re.astype(f32), c_im.astype(f32))
    ug = u.astype(f32).reshape(bsz, L, S5_GROUPS, S5_GROUP)
    bu = jnp.einsum('gpc,blgc->blgp', b_bar, ug.astype(jnp.complex64))
    a_elems = jnp.broadcast_to(a_bar, (1, L, S5_GROUPS, S5_STATE))
    _, states = lax.associative_scan(s5_combine, (a_elems, bu), axis=1)
    y = jnp.real(jnp.einsum('gcp,blgp->blgc', c, states)) + d.astype(f32).reshape(S5_GROUPS, S5_GROUP) * ug
    y = jax.nn.gelu(y.reshape(bsz, L, S5_WIDTH)).astype(u.dtype)
    return y * jax.nn.sigmoid(y @ w_glu + b_glu)

def conv_ffn(h, w_up, conv_w, conv_b, w_down):
    L = h.shape[1]
    z = h @ w_up
    zp = jnp.pad(z, ((0, 0), (CONV_WIDTH - 1, 0), (0, 0)))
    z = conv_b + sum(conv_w[j] * zp[:, j:j + L] for j in range(CONV_WIDTH))
    gate, val = jnp.split(z, 2, axis=-1)
    return (jax.nn.gelu(gate) * val) @ w_down

def second_inputs(seed: int = 0) -> dict:
    key = jax.random.key(seed)
    ks = jax.random.split(key, 40)
    f32 = jnp.float32
    Ld, W, G, P, C, F = DEPTH_2, RWKV_WIDTH, S5_GROUPS, S5_STATE, S5_GROUP, D_FF

    def nrm(k, shape, scale):
        return jax.random.normal(k, shape, f32) * scale

    def gain(k, shape):
        return 1.0 + 0.05 * jax.random.normal(k, shape, f32)

    n = jnp.arange(P, dtype=f32)
    return {
        'x': nrm(ks[0], (BATCH, SEQ, D_MODEL), 1.0),
        'norm_mix_pre': gain(ks[1], (Ld, D_MODEL)),
        'norm_mix_post': gain(ks[2], (Ld, D_MODEL)),
        'norm_ffn_pre': gain(ks[3], (Ld, D_MODEL)),
        'norm_ffn_post': gain(ks[4], (Ld, D_MODEL)),
        'w_in': nrm(ks[5], (Ld, D_MODEL, N_IN_COLS), D_MODEL ** -0.5),
        'b_gate': nrm(ks[6], (Ld, 2 * D_MODEL), 0.02),
        'rwkv_shift_mu': jax.random.uniform(ks[7], (Ld, N_RWKV_COLS), f32, 0.0, 1.0),
        'rwkv_w0': jax.random.uniform(ks[8], (Ld, W), f32, -6.0, -1.0),
        'rwkv_w2': nrm(ks[9], (Ld, DECAY_RANK, W), 0.1 * DECAY_RANK ** -0.5),
        'rwkv_a0': nrm(ks[10], (Ld, W), 0.1),
        'rwkv_a2': nrm(ks[11], (Ld, AAA_RANK, W), 0.1 * AAA_RANK ** -0.5),
        'rwkv_g2': nrm(ks[12], (Ld, GATE_RANK, W), GATE_RANK ** -0.5),
        'rwkv_k_k': 0.85 + 0.05 * jax.random.normal(ks[13], (Ld, W), f32),
        'rwkv_k_a': gain(ks[14], (Ld, W)),
        'rwkv_r_k': nrm(ks[15], (Ld, RWKV_HEADS, RWKV_HEAD), 0.3),
        'rwkv_lnx_w': gain(ks[16], (Ld, W)),
        'rwkv_lnx_b': nrm(ks[17], (Ld, W), 0.02),
        's5_a_re': -0.5 + 0.01 * jax.random.normal(ks[18], (Ld, G, P), f32),
        's5_a_im': math.pi * n + 0.01 * jax.random.normal(ks[19], (Ld, G, P), f32),
        's5_b_re': nrm(ks[20], (Ld, G, P, C), (2 * C) ** -0.5),
        's5_b_im': nrm(ks[21], (Ld, G, P, C), (2 * C) ** -0.5),
        's5_c_re': nrm(ks[22], (Ld, G, C, P), P ** -0.5),
        's5_c_im': nrm(ks[23], (Ld, G, C, P), P ** -0.5),
        's5_d': nrm(ks[24], (Ld, S5_WIDTH), 1.0),
        's5_log_step': jax.random.uniform(ks[25], (Ld, G), f32, math.log(STEP_MIN), math.log(STEP_MAX)),
        's5_w_glu': nrm(ks[26], (Ld, S5_WIDTH, S5_WIDTH), S5_WIDTH ** -0.5),
        's5_b_glu': nrm(ks[27], (Ld, S5_WIDTH), 0.02),
        'w_branch_rwkv': nrm(ks[28], (Ld, W, D_MODEL), W ** -0.5),
        'w_branch_s5': nrm(ks[29], (Ld, S5_WIDTH, D_MODEL), S5_WIDTH ** -0.5),
        'w_out': nrm(ks[30], (Ld, D_MODEL, D_MODEL), D_MODEL ** -0.5),
        'ffn_w_up': nrm(ks[31], (Ld, D_MODEL, 2 * F), D_MODEL ** -0.5),
        'ffn_conv_w': nrm(ks[32], (Ld, CONV_WIDTH, 2 * F), CONV_WIDTH ** -0.5),
        'ffn_conv_b': nrm(ks[33], (Ld, 2 * F), 0.02),
        'ffn_w_down': nrm(ks[34], (Ld, F, D_MODEL), F ** -0.5),
    }

def second_block(x, norm_mix_pre, norm_mix_post, norm_ffn_pre, norm_ffn_post, w_in, b_gate,
              rwkv_shift_mu, rwkv_w0, rwkv_w2, rwkv_a0, rwkv_a2, rwkv_g2, rwkv_k_k, rwkv_k_a,
              rwkv_r_k, rwkv_lnx_w, rwkv_lnx_b, s5_a_re, s5_a_im, s5_b_re, s5_b_im, s5_c_re,
              s5_c_im, s5_d, s5_log_step, s5_w_glu, s5_b_glu, w_branch_rwkv, w_branch_s5, w_out,
              ffn_w_up, ffn_conv_w, ffn_conv_b, ffn_w_down):
    for l in range(DEPTH_2):
        h = rms_norm(x, norm_mix_pre[l])
        proj = h @ w_in[l]
        p_rwkv = proj[..., :N_RWKV_COLS]
        u_s5 = proj[..., N_RWKV_COLS:N_RWKV_COLS + S5_WIDTH]
        gates = jax.nn.sigmoid(proj[..., N_RWKV_COLS + S5_WIDTH:] + b_gate[l])
        g_rwkv, g_s5 = jnp.split(gates, 2, axis=-1)
        o_rwkv = rwkv7_branch(p_rwkv, rwkv_shift_mu[l], rwkv_w0[l], rwkv_w2[l], rwkv_a0[l],
                              rwkv_a2[l], rwkv_g2[l], rwkv_k_k[l], rwkv_k_a[l], rwkv_r_k[l],
                              rwkv_lnx_w[l], rwkv_lnx_b[l]) @ w_branch_rwkv[l]
        o_s5 = s5_branch(u_s5, s5_a_re[l], s5_a_im[l], s5_b_re[l], s5_b_im[l], s5_c_re[l],
                         s5_c_im[l], s5_d[l], s5_log_step[l], s5_w_glu[l], s5_b_glu[l]) @ w_branch_s5[l]
        mixed = (g_rwkv * o_rwkv + g_s5 * o_s5) @ w_out[l]
        x = x + rms_norm(mixed, norm_mix_post[l])
        h = rms_norm(x, norm_ffn_pre[l])
        f = conv_ffn(h, ffn_w_up[l], ffn_conv_w[l], ffn_conv_b[l], ffn_w_down[l])
        x = x + rms_norm(f, norm_ffn_post[l])
    return x


def setup_inputs(seed=0):
    out = dict(first_inputs(seed))
    for name, value in second_inputs(seed + 1).items():
        if name != "x":
            out[name + "_2"] = value
    return out


def reference(
    x, c, ctx, c_ctx, mod_w, mod_b, pre_norm, post_norm, w_in, mla_q_norm, mla_w_uq,
    mla_kv_norm, mla_w_ukv, pool_w, pool_scale, gla_af_w2, gla_af_b, gla_ab_w2, gla_ab_b,
    gla_norm, w_branch_mla, w_branch_pool, w_branch_gla, w_out, norm_mix_pre_2, norm_mix_post_2,
    norm_ffn_pre_2, norm_ffn_post_2, w_in_2, b_gate_2, rwkv_shift_mu_2, rwkv_w0_2, rwkv_w2_2,
    rwkv_a0_2, rwkv_a2_2, rwkv_g2_2, rwkv_k_k_2, rwkv_k_a_2, rwkv_r_k_2, rwkv_lnx_w_2,
    rwkv_lnx_b_2, s5_a_re_2, s5_a_im_2, s5_b_re_2, s5_b_im_2, s5_c_re_2, s5_c_im_2, s5_d_2,
    s5_log_step_2, s5_w_glu_2, s5_b_glu_2, w_branch_rwkv_2, w_branch_s5_2, w_out_2, ffn_w_up_2,
    ffn_conv_w_2, ffn_conv_b_2, ffn_w_down_2,
):
    x = first_block(
        x, c, ctx, c_ctx, mod_w, mod_b, pre_norm, post_norm, w_in, mla_q_norm, mla_w_uq,
        mla_kv_norm, mla_w_ukv, pool_w, pool_scale, gla_af_w2, gla_af_b, gla_ab_w2, gla_ab_b,
        gla_norm, w_branch_mla, w_branch_pool, w_branch_gla, w_out,
    )
    return second_block(
        x, norm_mix_pre_2, norm_mix_post_2, norm_ffn_pre_2, norm_ffn_post_2, w_in_2, b_gate_2,
        rwkv_shift_mu_2, rwkv_w0_2, rwkv_w2_2, rwkv_a0_2, rwkv_a2_2, rwkv_g2_2, rwkv_k_k_2,
        rwkv_k_a_2, rwkv_r_k_2, rwkv_lnx_w_2, rwkv_lnx_b_2, s5_a_re_2, s5_a_im_2, s5_b_re_2,
        s5_b_im_2, s5_c_re_2, s5_c_im_2, s5_d_2, s5_log_step_2, s5_w_glu_2, s5_b_glu_2,
        w_branch_rwkv_2, w_branch_s5_2, w_out_2, ffn_w_up_2, ffn_conv_w_2, ffn_conv_b_2,
        ffn_w_down_2,
    )


_drawn_inputs = setup_inputs


def setup_inputs(seed=0):
    import zlib

    import numpy as np

    out = dict(_drawn_inputs(seed))
    spreads = {}
    factors = {'mla_q_norm': 8.0,
     'mla_kv_norm': 4.345,
     'gla_af_b': 3.654,
     'gla_ab_b': 3.695,
     'b_gate_2': 8.0,
     'rwkv_w2_2': 8.0,
     'rwkv_lnx_b_2': 4.798,
     's5_a_re_2': 200.0,
     's5_b_glu_2': 8.0,
     'ffn_conv_b_2': 3.582,
     's5_a_im_2': 36.768,
     's5_b_re_2': 50.632,
     's5_b_im_2': 51.384,
     's5_c_re_2': 50.936,
     's5_c_im_2': 50.888,
     's5_log_step_2': 39.232}
    for name, (base, spread) in spreads.items():
        noise = np.random.default_rng([zlib.crc32(name.encode()), seed]).standard_normal(out[name].shape)
        drawn = base * np.exp(spread * noise) if base else spread * noise
        out[name] = jnp.asarray(drawn.astype(out[name].dtype))
    for name, factor in factors.items():
        out[name] = (out[name] * factor).astype(out[name].dtype)
    return out
```

```python
from collections import namedtuple
from contextlib import ExitStack

import numpy as np

import concourse.bass as bass
from concourse import mybir

P = 128
D = 1024
KD = D // P
SEQ = 256
CTX = 256
TOK = SEQ + CTX
DEPTH = 2
HEADS, NOPE, ROPE, VDIM = 8, 64, 32, 64
QK = NOPE + ROPE
GRID_W = 64
ROPE_BASE = 10000.0
WINDOWS = (2, 4, 8, 16)
PAD = max(WINDOWS) // 2
CH = 64
NCH = TOK // CH
GLA_TAU = 16.0
GLA_LIMIT = 80.0
EPS = 1e-6
LNX_EPS = 64e-5
S5T = 16
FF = 2816
FT = FF // P
IN_SIZES = dict(mla_q=256, mla_kv=128, mla_kr=32, mla_gate=512, pool_x=512, pool_gate=512, gla_q=256,
                gla_k=256, gla_v=512, gla_af=16, gla_ab=16, gla_gate=512, merge=3 * D)
IN_AT = dict(zip(IN_SIZES, np.cumsum([0] + list(IN_SIZES.values()))[:-1].tolist()))
RW = 512
S5_AT = 3 * RW + 64 + 64 + 128
G2_AT = S5_AT + 512

PANEL = 16
SLOTS = 5

F32 = mybir.dt.float32
U32 = mybir.dt.uint32
ALU = mybir.AluOpType
ACT = mybir.ActivationFunctionType
AX = mybir.AxisListType

Piece = namedtuple("Piece", "array index turned row col")
Stage = namedtuple("Stage", "tensor scalar vector gpsimd", defaults=(None, None, None, None))
Tile = namedtuple("Tile", "products scalar vector", defaults=(None, None))



def part(array, l, r0, nr, c0, nc, row=0, col=0):
    return Piece(array, (l, slice(r0, r0 + nr), slice(c0, c0 + nc)), False, row, col)


def tiles_of(array, l, rows, c0, cols):
    return [[part(array, l, k * P, P, c0 + m * P, P)] for m in range(cols // P) for k in range(rows // P)]


def rotated(array, l, r0, c0, col):
    h, q = ROPE // 2, ROPE // 4
    return [part(array, l, r0, P, c0 + a * h + (1 - b) * q, q, 0, col + a * h + b * q) for a in range(2) for b in range(2)]


def stream_plan():
    plan, order = {}, []

    def add(name, blocks):
        plan[name] = len(order)
        order.extend(blocks)

    def mod(l):
        add(f"mod{l}", [[part("mod_w", l, k * P, P, n * 512 + q * P, P)] for n in range(6) for k in range(KD) for q in range(4)])

    mod(0)
    for l in range(DEPTH):
        z = lambda name: tiles_of("w_in", l, D, IN_AT[name], IN_SIZES[name])
        kr = [[part("w_in", l, k * P, P, IN_AT["mla_kr"], ROPE, 0, NOPE)]
              + rotated("w_in", l, k * P, IN_AT["mla_kr"], QK) for k in range(KD)]
        add(f"mla_in{l}", z("mla_q") + z("mla_kv") + kr + z("mla_gate"))
        q = [[part("mla_w_uq", l, k * P, P, h * QK, QK)] + rotated("mla_w_uq", l, k * P, h * QK + NOPE, QK)
             for h in range(HEADS) for k in range(2)]
        k = [[part("mla_w_ukv", l, 0, P, (h + j) * 128, NOPE, 0, j * NOPE) for j in range(2)] for h in range(0, HEADS, 2)]
        v = [[part("mla_w_ukv", l, 0, P, (h + j) * 128 + NOPE, VDIM, 0, j * VDIM) for j in range(2)]
             for h in range(0, HEADS, 2)]
        add(f"mla_up{l}", q + k + v)
        add(f"pool_in{l}", z("pool_x") + z("pool_gate"))
        a = [[part("w_in", l, k * P, P, IN_AT["gla_af"], 32)] for k in range(KD)]
        add(f"gla_in{l}", z("gla_q") + z("gla_k") + a + z("gla_gate"))
        add(f"gla_v{l}", [[part("w_in", l, k * P, P, IN_AT["gla_v"] + n * P, P)] for k in range(KD) for n in range(4)])
        add(f"pool_w{l}", [[Piece("pool_w", (l, g), False, 0, 0)] for g in range(len(WINDOWS))])
        add(f"gla_w{l}", [[part("gla_af_w2", l, 0, 16, m * P, P)] for m in range(2)]
            + [[part("gla_ab_w2", l, 0, 16, m * P, P, 16)] for m in range(2)])
        if l + 1 < DEPTH:
            mod(l + 1)
        merge = []
        for m in range(KD):
            for b, name in enumerate(("w_branch_mla", "w_branch_pool", "w_branch_gla")):
                merge += tiles_of("w_in", l, D, IN_AT["merge"] + b * D + m * P, P) + tiles_of(name, l, 512, m * P, P)
        add(f"merge{l}", merge)
        add(f"out{l}", tiles_of("w_out", l, D, 0, D))
    add("rw_in", tiles_of("w_in_2", 0, D, 0, S5_AT))
    add("rw_w", [[part("rwkv_w2_2", 0, 0, 64, m * P, P)] for m in range(4)]
        + [[part("rwkv_a2_2", 0, 0, 64, m * P, P, 64)] for m in range(4)] + tiles_of("rwkv_g2_2", 0, P, 0, RW))
    add("s5_in", tiles_of("w_in_2", 0, D, S5_AT, 512))
    for name in ("s5_b_re_2", "s5_b_im_2"):
        add(name, [[Piece(name, (0, 2 * i + j), True, 32 * (i % 4) + 16 * j, 64 * j) for j in range(2)] for i in range(S5T)])
    add("s5_glu", tiles_of("s5_w_glu_2", 0, 512, 0, 512))
    merge = []
    for m in range(KD):
        for b, name in enumerate(("w_branch_rwkv_2", "w_branch_s5_2")):
            merge += tiles_of("w_in_2", 0, D, G2_AT + b * D + m * P, P) + tiles_of(name, 0, 512, m * P, P)
    add("merge2", merge)
    add("out2", tiles_of("w_out_2", 0, D, 0, D))
    up = []
    for j in range(FT):
        up += tiles_of("ffn_w_up_2", 0, D, j * P, P) + tiles_of("ffn_w_up_2", 0, D, FF + j * P, P)
    add("ff_up", up)
    add("ff_down", tiles_of("ffn_w_down_2", 0, FF, 0, D))
    return plan, order


def vector_plan():
    at, src, n = {}, [], 0

    def add(name, array, l, cols):
        nonlocal n
        at[name] = (n, cols)
        src.append((n, cols, array, l))
        n += cols

    for l in range(DEPTH):
        for name, array, cols in (("pre", "pre_norm", 8), ("post", "post_norm", 8), ("mod_b", "mod_b", 24),
                                  ("q_norm", "mla_q_norm", 2), ("kv_norm", "mla_kv_norm", 1),
                                  ("pool_scale", "pool_scale", 4), ("af_b", "gla_af_b", 2), ("ab_b", "gla_ab_b", 2),
                                  ("gla_norm", "gla_norm", 1)):
            add(f"{name}{l}", array, l, cols)
    for name, array, cols in (("mix_pre", "norm_mix_pre_2", 8), ("mix_post", "norm_mix_post_2", 8),
                              ("ffn_pre", "norm_ffn_pre_2", 8), ("ffn_post", "norm_ffn_post_2", 8),
                              ("b_gate", "b_gate_2", 16), ("mu", "rwkv_shift_mu_2", 14), ("w0", "rwkv_w0_2", 4),
                              ("a0", "rwkv_a0_2", 4), ("k_k", "rwkv_k_k_2", 4), ("k_a", "rwkv_k_a_2", 4),
                              ("r_k", "rwkv_r_k_2", 4), ("lnx_w", "rwkv_lnx_w_2", 4), ("lnx_b", "rwkv_lnx_b_2", 4),
                              ("a_re", "s5_a_re_2", 16), ("a_im", "s5_a_im_2", 16), ("s5_d", "s5_d_2", 4),
                              ("b_glu", "s5_b_glu_2", 4), ("conv_w", "ffn_conv_w_2", 3 * 2 * FT),
                              ("conv_b", "ffn_conv_b_2", 2 * FT)):
        add(name, array, 0, cols)
    for name, cols in (("log_step", 16), ("c_re", 32 * S5T), ("c_im", 32 * S5T)):
        at[name] = (n, cols)
        n += cols
    return at, src, n


def constant_plan():
    p = np.arange(P)
    row, col = p[:, None], p[None, :]
    same = row // CH == col // CH
    f = lambda a: a.astype(np.float32)
    t = dict(ident=f(row == col), ones=np.ones((P, P), np.float32), head_ones=f(same),
             ident2=f(row % CH == np.arange(CH)[None, :]),
             upto=f(same & (row <= col)), since=f(same & (row >= col)), before=f(same & (row < col)))
    for b in range(1, 7):
        t[f"level{b}"] = f((row < col) & (row >> b == col >> b) & (row >> (b - 1) != col >> (b - 1)))
    t["level1_turned"] = np.ascontiguousarray(t["level1"].T)
    half = ROPE // 2
    inv = np.float32(ROPE_BASE) ** (-np.arange(0, half, 2, dtype=np.float32) / np.float32(half))
    pos = np.arange(SEQ)
    ang_r, ang_c = f(pos // GRID_W)[:, None] * inv, f(pos % GRID_W)[:, None] * inv
    ang = np.concatenate([ang_r, ang_r, ang_c, ang_c], -1).astype(np.float32)
    sign = np.where(np.arange(ROPE) % half < half // 2, -1.0, 1.0).astype(np.float32)
    rope = np.zeros((P, TOK), np.float32)
    rope[NOPE:QK, :SEQ], rope[NOPE:QK, SEQ:] = np.cos(ang).T, 1.0
    rope[QK:, :SEQ] = (np.sin(ang) * sign).T
    t["rope"] = rope
    share = [1.0 / (np.clip(pos + w // 2, 0, SEQ) - np.clip(pos - w // 2, 0, SEQ)) for w in WINDOWS]
    edges = [np.concatenate([a[:PAD], a[-PAD:]]) for a in share]
    t["share"] = np.broadcast_to(f(np.concatenate(edges))[None], (P, 4 * 2 * PAD))
    t["carry"] = np.broadcast_to(f(np.arange(TOK) % CH != 0)[None], (P, TOK))
    t["step"] = np.broadcast_to(f(np.arange(SEQ))[None], (P, SEQ))
    return t


def build(nc, weights, vectors, constants, x_in, c_in, out):
    plan, order = stream_plan()
    vec_at, _, n_vec = vector_plan()
    const_at, n_const = {}, 0
    for name, a in constant_plan().items():
        const_at[name] = (n_const, a.shape[1])
        n_const += a.shape[1]
    n_panels = -(-len(order) // PANEL)
    WORK = 28400

    ctx = ExitStack()
    with ctx:
        def sb(name, cols):
            return ctx.enter_context(nc.sbuf_tensor(name, [P, cols], F32))

        def sem(name):
            return ctx.enter_context(nc.semaphore(name))

        panels = sb("panels", SLOTS * PANEL * P)
        vec_sb, const_sb = sb("vec_sb", n_vec), sb("const_sb", n_const)
        x_sb, h_sb, work = sb("x_sb", KD * TOK), sb("h_sb", KD * TOK), sb("work", WORK)
        small = sb("small", 1024)
        ps = ctx.enter_context(nc.psum_tensor("ps", [P, 8, 512], F32))

        panel_loaded = [sem(f"panel_loaded{i}") for i in range(SLOTS)]
        panel_used = sem("panel_used")
        inputs_loaded, x_loaded, stage_done, out_stored = sem("inputs_loaded"), sem("x_loaded"), sem("stage_done"), sem("out_stored")
        dve_step, act_step, pool_step = sem("dve_step"), sem("act_step"), sem("pool_step")

        shared_sems = {}

        def shared(kind, n):
            if kind not in shared_sems:
                shared_sems[kind] = [sem(kind), 0]
            shared_sems[kind][1] += n
            return shared_sems[kind][0], shared_sems[kind][1] - n

        def vec(name):
            return vec_sb[:, vec_at[name][0]:sum(vec_at[name])]

        def const(name):
            return const_sb[:, const_at[name][0]:sum(const_at[name])]

        def region(base, at, *dims):
            n = int(np.prod(dims))
            assert at + n <= base.shape[1], (at, n, base.shape)
            v = base[:, at:at + n]
            if len(dims) == 1:
                return v
            names = "abcd"[:len(dims)]
            return v.rearrange(f"p ({' '.join(names)}) -> p {' '.join(names)}",
                               **dict(zip(names[1:], dims[1:])))

        class Room:
            def __init__(self, base, at=0):
                self.base, self.at = base, at

            def __call__(self, *dims):
                self.at += int(np.prod(dims))
                return region(self.base, self.at - int(np.prod(dims)), *dims)

        def wide(a, n):
            k = len(a.shape)
            v = a.rearrange("p (a o) -> p a o", o=1) if k == 2 else a.rearrange("p a (b o) -> p a b o", o=1)
            return v.to_broadcast(list(a.shape) + [n])

        def each(a, n):
            return a.rearrange("p (o a) -> p o a", o=1).to_broadcast([a.shape[0], n, a.shape[1]])

        class Steps:
            def __init__(self, eng, stepped):
                self.eng, self.stepped, self.n = eng, stepped, 0

            def __call__(self, ins):
                self.n += 1
                ins.then_inc(self.stepped, 1)
                self.eng.wait_ge(self.stepped, self.n)

        steps = {}

        class Blocks:
            def __init__(self):
                self.panel, self.freed = -1, 0

            def lhs(self, pe, i, cols=(0, P), n=1):
                p = i // PANEL
                assert p >= self.panel
                while self.panel < p:
                    self.panel += 1
                    pe.wait_ge(panel_loaded[self.panel % SLOTS], 16 * (self.panel // SLOTS + 1))
                at = ((p % SLOTS) * PANEL + i % PANEL) * P
                return panels[:, at + cols[0]:at + (n - 1) * P + cols[1]]

            def product(self, pe, o, lhsT, rhs, start=True, stop=True, signal=None):
                mm = pe.matmul(o, lhsT, rhs, start=start, stop=stop)
                if signal is not None:
                    mm.then_inc(signal, 1)
                elif self.freed < self.panel:
                    self.freed += 1
                    mm.then_inc(panel_used, 1)

        blocks = Blocks()
        stages = []


        def projection(name, tiles, bank0=0, banks=8, gpsimd=None):
            n_act = np.cumsum([t.scalar is not None for t in tiles]).tolist()
            n_dve = np.cumsum([t.vector is not None for t in tiles]).tolist()
            filled, f0 = shared("tile_filled", len(tiles))
            by_act, a0 = shared("tile_act_took", n_act[-1])
            by_dve, d0 = shared("tile_dve_took", n_dve[-1])

            def tensor(pe):
                for i, t in enumerate(tiles):
                    if i >= banks:
                        if n_act[i - banks]:
                            pe.wait_ge(by_act, a0 + n_act[i - banks])
                        if n_dve[i - banks]:
                            pe.wait_ge(by_dve, d0 + n_dve[i - banks])
                    for j, (lhsT, rhs, rows, c0, n, start, stop) in enumerate(t.products):
                        w = blocks.lhs(pe, *lhsT) if isinstance(lhsT, tuple) else lhsT
                        if isinstance(rhs, tuple):
                            rhs = blocks.lhs(pe, *rhs)
                        blocks.product(pe, ps[0:rows, bank0 + i % banks, c0:c0 + n], w, rhs, start, stop,
                                       filled if j == len(t.products) - 1 else None)

            def scalar(act):
                for i, t in enumerate(tiles):
                    if t.scalar is not None:
                        act.wait_ge(filled, f0 + i + 1)
                        t.scalar(act, ps[:, bank0 + i % banks, :]).then_inc(by_act, 1)

            def vector(dve):
                for i, t in enumerate(tiles):
                    if t.vector is not None:
                        dve.wait_ge(filled, f0 + i + 1)
                        t.vector(dve, ps[:, bank0 + i % banks, :]).then_inc(by_dve, 1)

            stages.append(Stage(tensor, scalar, vector, gpsimd))

        def chain(block0, rhs, n, rows=P, cols=(0, P)):
            return [((block0 + k, cols), r, rows, 0, n, k == 0, k == len(rhs) - 1) for k, r in enumerate(rhs)]

        def copied(dst, n, func=ACT.Copy, rows=P, **kw):
            return lambda act, b: act.activation(dst, b[0:rows, 0:n], func, **kw)

        def copied_dve(dst, n):
            return lambda dve, b: dve.tensor_copy(dst, b[:, 0:n])

        def sums(groups, root, inverse, after=None):
            (summed, s0), (rooted, r0) = shared("squares_summed", 1), shared("rooted", 1)
            at = np.cumsum([0] + [n for _, n, _ in groups]).tolist()

            def tensor(pe):
                for i, (squares, n, _) in enumerate(groups):
                    for k, s in enumerate(squares):
                        last = i == len(groups) - 1 and k == len(squares) - 1
                        blocks.product(pe, ps[:, i, 0:n], const("ones"), s, k == 0, k == len(squares) - 1,
                                       summed if last else None)

            def scalar(act):
                act.wait_ge(summed, s0 + 1)
                for i, (_, n, width) in enumerate(groups):
                    ins = act.activation(root[:, at[i]:at[i + 1]], ps[:, i, 0:n], ACT.Sqrt, bias=eps_col[:, 0:1],
                                         scale=1.0 / width)
                ins.then_inc(rooted, 1)

            def vector(dve):
                dve.wait_ge(rooted, r0 + 1)
                steps["dve"](dve.reciprocal(inverse[:, 0:at[-1]], root[:, 0:at[-1]]))
                if after is not None:
                    after(dve)

            stages.append(Stage(tensor, scalar, vector))

        eps_col = region(small, 0, 4)

        c_sb = region(small, 4, KD, 2)
        silu_c = region(small, 20, KD, 2)
        mods = [region(small, 40 + 64 * l, 24, 2) for l in range(DEPTH)]
        gains = [region(small, 168 + 16 * l, KD, 2) for l in range(DEPTH)]
        posts = [region(small, 200 + 16 * l, KD, 2) for l in range(DEPTH)]
        alpha = region(small, 232, 2, NCH)
        alpha_arg = region(small, 250, 2, NCH)
        tail = region(small, 270, 2, NCH)

        def start_scalar(act):
            act.wait_ge(inputs_loaded, 48)
            act.activation(silu_c, c_sb, ACT.Silu)

        def start_vector(dve):
            dve.memset(eps_col[:, 0:1], EPS)
            dve.memset(eps_col[:, 1:2], LNX_EPS)
            dve.memset(eps_col[:, 2:3], 0.0)
            dve.wait_ge(inputs_loaded, 48)
            dve.wait_ge(x_loaded, 16)

        stages.append(Stage(None, start_scalar, start_vector, None))

        mod_filled, mod_row, mod_used, mod_turned = sem("mod_filled"), sem("mod_row"), sem("mod_used"), sem("mod_turned")
        row_sb = region(small, 512, 512)
        MOD_CHUNKS = 6

        def modulation(l, chunks):
            def tensor(pe):
                for n in chunks:
                    i = l * MOD_CHUNKS + n
                    if i:
                        pe.wait_ge(mod_row, i)
                    for k in range(KD):
                        w = blocks.lhs(pe, plan[f"mod{l}"] + (n * KD + k) * 4, (0, P), 4)
                        blocks.product(pe, ps[0:2, 6, :], silu_c[:, k, :], w, k == 0, k == KD - 1,
                                       mod_filled if k == KD - 1 else None)
                    pe.wait_ge(mod_row, i + 1)
                    if i:
                        pe.wait_ge(mod_used, i)
                    for q in range(4):
                        mm = pe.transpose(ps[:, 7, 2 * q:2 * q + 2], row_sb[0:2, q * P:(q + 1) * P], const("ident")[0:2, 0:2])
                    mm.then_inc(mod_turned, 1)

            def scalar(act):
                for n in chunks:
                    i = l * MOD_CHUNKS + n
                    act.wait_ge(mod_filled, i + 1)
                    if i:
                        act.wait_ge(mod_turned, i)
                    act.activation(row_sb[0:2, :], ps[0:2, 6, :], ACT.Copy).then_inc(mod_row, 1)

            def vector(dve):
                step = steps["dve"]
                for n in chunks:
                    i = l * MOD_CHUNKS + n
                    m = slice(4 * n, 4 * n + 4)
                    dve.wait_ge(mod_turned, i + 1)
                    ins = dve.tensor_tensor(mods[l][:, m, :], ps[:, 7, 0:8].rearrange("p (m c) -> p m c", c=2),
                                            wide(vec(f"mod_b{l}")[:, m], 2), ALU.add)
                    ins.then_inc(mod_used, 1)
                    dve.wait_ge(mod_used, i + 1)
                    m8 = slice(4 * n % 8, 4 * n % 8 + 4)
                    if n // 2 == 1:
                        step(dve.scalar_tensor_tensor(gains[l][:, m8, :], mods[l][:, m, :], 1.0,
                                                      wide(vec(f"pre{l}")[:, m8], 2), ALU.add, ALU.mult))
                    elif n // 2 == 2:
                        step(dve.tensor_tensor(posts[l][:, m8, :], mods[l][:, m, :], wide(vec(f"post{l}")[:, m8], 2), ALU.mult))
            return Stage(tensor, scalar, vector, None)

        def fuse(*others):
            parts = (stages.pop(),) + others

            def both(name):
                fs = [f for f in (p[name] for p in parts) if f is not None]
                return (lambda eng: [f(eng) for f in fs]) if fs else None
            stages.append(Stage(*(both(i) for i in range(4))))

        def squares_stage(dst, src):
            def scalar(act):
                act.activation(dst, src, ACT.Square)
            stages.append(Stage(None, scalar, None, None))

        def scaled_by(gain):
            def vector(dve, m, x, h, inverse):
                return dve.scalar_tensor_tensor(h[:, m, :], x[:, m, :], gain[:, m:m + 1], inverse, ALU.mult, ALU.mult)
            return vector, None

        def modulated_by(l, spans):
            def vector(dve, m, x, h, inverse):
                for t0, n, c in spans:
                    ins = dve.scalar_tensor_tensor(h[:, m, t0:t0 + n], x[:, m, t0:t0 + n], gains[l][:, m, c:c + 1],
                                                   inverse[:, t0:t0 + n], ALU.mult, ALU.mult)
                return ins

            def scalar(act, m, h):
                for t0, n, c in spans:
                    act.activation(h[:, m, t0:t0 + n], h[:, m, t0:t0 + n], ACT.Identity, bias=mods[l][:, m, c:c + 1])
            return vector, scalar

        def norm(T, x, h, scale, at, add=None, ready=None):
            sq, root, inverse = region(work, at, KD, T), region(work, at + KD * T, T), region(work, at + KD * T + T, T)
            order = [5, 6, 7, 0, 1, 2, 3, 4]
            added = add is not None
            (times, t0) = shared("o_times", KD * added)
            (by_pool, p0), (by_dve, d0) = shared("x_pool_added", 3 * added), shared("x_dve_added", 5 * added)
            (squared, q0), (summed, s0), (rooted, r0) = shared("x_squared", KD), shared("x_summed", 1), shared("x_rooted", 1)
            scaled, c0 = shared("x_scaled", KD)

            def tensor(pe):
                for i, m in enumerate(order):
                    pe.wait_ge(squared, q0 + i + 1)
                    blocks.product(pe, ps[:, 0, 0:T], const("ones"), sq[:, m, :], i == 0, i == KD - 1,
                                   summed if i == KD - 1 else None)

            def scalar(act):
                for i, m in enumerate(order):
                    if add is not None:
                        if i < 3:
                            act.wait_ge(by_pool, p0 + i + 1)
                        else:
                            act.wait_ge(by_dve, d0 + i - 2)
                    act.activation(sq[:, m, :], x[:, m, :], ACT.Square).then_inc(squared, 1)
                act.wait_ge(summed, s0 + 1)
                act.activation(root, ps[:, 0, 0:T], ACT.Sqrt, bias=eps_col[:, 0:1], scale=1.0 / D).then_inc(rooted, 1)
                if scale[1] is not None:
                    for m in range(KD):
                        act.wait_ge(scaled, c0 + m + 1)
                        scale[1](act, m, h)

            def vector(dve):
                step = steps["dve"]
                if add is not None:
                    o, inv = add
                    for i, m in enumerate(order):
                        dve.tensor_tensor(o[:, m, :], o[:, m, :], inv, ALU.mult).then_inc(times, 1)
                        if i >= 4:
                            j = order[i - 1]
                            dve.wait_ge(times, t0 + i)
                            dve.tensor_tensor(x[:, j, :], x[:, j, :], o[:, j, :], ALU.add).then_inc(by_dve, 1)
                    dve.wait_ge(times, t0 + KD)
                    dve.tensor_tensor(x[:, 4, :], x[:, 4, :], o[:, 4, :], ALU.add).then_inc(by_dve, 1)
                dve.wait_ge(rooted, r0 + 1)
                step(dve.reciprocal(inverse, root))
                if ready is not None:
                    ready(dve)
                for m in range(KD):
                    scale[0](dve, m, x, h, inverse).then_inc(scaled, 1)

            def gpsimd(pool):
                for i, m in enumerate(order[:3]):
                    pool.wait_ge(times, t0 + i + 1)
                    pool.tensor_tensor(x[:, m, :], x[:, m, :], add[0][:, m, :], ALU.add).then_inc(by_pool, 1)
                    pool.wait_ge(by_pool, p0 + i + 1)
            return Stage(tensor, scalar, vector, gpsimd if add is not None else None)

        def residual(name, block0, rhs, T, gain_cols, at, last_x=None):
            o, sq = region(work, at, KD, T), region(work, at + KD * T, KD, T)
            root, inverse = region(work, at + 2 * KD * T, T), region(work, at + 2 * KD * T + T, T)
            kt = len(rhs)

            def taken(m):
                def scalar(act, b):
                    act.activation(sq[:, m, :], b[:, 0:T], ACT.Square)
                    for t0, n, gain in gain_cols:
                        ins = act.activation(o[:, m, t0:t0 + n], b[:, t0:t0 + n], ACT.Copy, scale=gain(m))
                    return ins
                return scalar
            projection(name, [Tile(chain(block0 + m * kt, rhs, T), taken(m)) for m in range(KD)])

            def after(dve):
                for half in ((0, 4), (4, 8)):
                    m = slice(*half)
                    steps["dve"](dve.tensor_tensor(o[:, m, :], o[:, m, :], each(inverse, 4), ALU.mult))
                    dve.tensor_tensor(last_x[:, m, :], last_x[:, m, :], o[:, m, :], ALU.add)
            sums([([sq[:, k, :] for k in range(KD)], T, D)], root, inverse, after=None if last_x is None else after)
            return o, inverse

        def projection_serial(name, tiles, banks=8):
            filled, f0 = shared("serial_filled", len(tiles))
            by_act, a0 = shared("serial_act_took", len(tiles))
            by_dve, d0 = shared("serial_dve_took", len(tiles))

            def tensor(pe):
                for i, t in enumerate(tiles):
                    if i >= banks:
                        pe.wait_ge(by_dve, d0 + i - banks + 1)
                    for j, (lhsT, rhs, rows, c0, n, start, stop) in enumerate(t.products):
                        blocks.product(pe, ps[0:rows, i % banks, c0:c0 + n], blocks.lhs(pe, *lhsT), rhs, start, stop,
                                       filled if j == len(t.products) - 1 else None)

            def scalar(act):
                for i, t in enumerate(tiles):
                    act.wait_ge(filled, f0 + i + 1)
                    t.scalar(act, ps[:, i % banks, :]).then_inc(by_act, 1)

            def vector(dve):
                for i, t in enumerate(tiles):
                    dve.wait_ge(by_act, a0 + i + 1)
                    t.vector(dve, ps[:, i % banks, :]).then_inc(by_dve, 1)

            stages.append(Stage(tensor, scalar, vector, None))

        def level_update(name, tiles, per, gpsimd):
            filled, f0 = shared("level_filled", len(tiles))

            def tensor(pe):
                for i, t in enumerate(tiles):
                    for j, (lhsT, rhs, rows, c0, n, start, stop) in enumerate(t.products):
                        blocks.product(pe, ps[0:rows, i, c0:c0 + n], lhsT, rhs, start, stop,
                                       filled if j == len(t.products) - 1 else None)

            def vector(dve):
                for i, t in enumerate(tiles):
                    dve.wait_ge(filled, f0 + (i // per + 1) * per)
                    t.vector(dve, ps[:, i, :])

            stages.append(Stage(tensor, None, vector, gpsimd))

        def merge(name, block0, branches, h, merged, T, sig, tmp, bias=None):
            nb = len(branches)
            filled, f0 = shared("merge_filled", 2 * KD * nb)
            gated, g0 = shared("merge_gated", KD * nb)
            mixed, m0 = shared("merge_mixed", KD * nb)

            def tensor(pe):
                i, at = 0, block0
                for m in range(KD):
                    for b in range(nb):
                        if i >= 4:
                            pe.wait_ge(mixed, m0 + i - 3)
                        for k in range(KD):
                            blocks.product(pe, ps[:, 2 * (i % 4), 0:T], blocks.lhs(pe, at + k), h[:, k, 0:T], k == 0,
                                           k == KD - 1, filled if k == KD - 1 else None)
                        for k in range(4):
                            blocks.product(pe, ps[:, 2 * (i % 4) + 1, 0:T], blocks.lhs(pe, at + KD + k),
                                           branches[b][:, k, :], k == 0, k == 3, filled if k == 3 else None)
                        at += KD + 4
                        i += 1

            def scalar(act):
                for i in range(KD * nb):
                    act.wait_ge(filled, f0 + 2 * i + 1)
                    if i >= 4:
                        act.wait_ge(mixed, m0 + i - 3)
                    col = i // nb + (i % nb) * KD
                    kw = {} if bias is None else dict(bias=bias[:, col:col + 1])
                    act.activation(sig[:, i % 4, :], ps[:, 2 * (i % 4), 0:T], ACT.Sigmoid, **kw).then_inc(gated, 1)

            def vector(dve):
                step = steps["dve"]
                for i in range(KD * nb):
                    m, b = divmod(i, nb)
                    dve.wait_ge(filled, f0 + 2 * i + 2)
                    dve.wait_ge(gated, g0 + i + 1)
                    dst = merged[:, m, :] if b == 0 else tmp
                    dve.tensor_tensor(dst, ps[:, 2 * (i % 4) + 1, 0:T], sig[:, i % 4, :], ALU.mult).then_inc(mixed, 1)
                    if b:
                        dve.wait_ge(mixed, m0 + i + 1)
                        step(dve.tensor_tensor(merged[:, m, :], merged[:, m, :], tmp, ALU.add))

            stages.append(Stage(tensor, scalar, vector, None))

        xT = region(x_sb, 0, KD, TOK)
        hT = region(h_sb, 0, KD, TOK)

        spans = [(0, SEQ, 0), (SEQ, CTX, 1)]

        def trunk(l):
            TQ = TOK if l < DEPTH - 1 else SEQ
            h = [hT[:, k, :] for k in range(KD)]
            hq = [hT[:, k, 0:TQ] for k in range(KD)]

            if l == 0:
                stages.append(modulation(0, range(MOD_CHUNKS)))
                stages.append(norm(TOK, xT, hT, modulated_by(0, spans), 0))

            room = Room(work)
            y_mla = room(4, TQ)
            zq, zkv = room(2, TQ), room(1, TOK)
            k_rope, rope_tmp = room(TOK), room(2, TOK)
            q_h, k_h = room(HEADS, TQ), room(HEADS, TOK)
            v_t = room(4, 512)
            lat_sq, root, inverse = room(3 * TOK), room(2 * TOK), room(2 * TOK)
            b0 = plan[f"mla_in{l}"]
            rope = const("rope")

            def rotate(dst, T, tmp):
                def vector(dve, b):
                    dve.tensor_tensor(dst, b[NOPE:QK, 0:T], rope[NOPE:QK, 0:T], ALU.mult)
                    steps["dve"](dve.tensor_tensor(tmp[NOPE:QK, 0:T], b[QK:P, 0:T], rope[QK:P, 0:T], ALU.mult))
                    return dve.tensor_tensor(dst, dst, tmp[NOPE:QK, 0:T], ALU.add)
                return vector

            def latent(z, square, n):
                def scalar(act, b):
                    act.activation(z, b[:, 0:n], ACT.Copy)
                    return act.activation(square, b[:, 0:n], ACT.Square)
                return scalar
            tiles = [Tile(chain(b0 + 8 * m, hq, TQ), latent(zq[:, m, :], lat_sq[:, m * TQ:(m + 1) * TQ], TQ)) for m in range(2)]
            tiles += [Tile(chain(b0 + 16, h, TOK), latent(zkv[:, 0, :], lat_sq[:, 2 * TQ:2 * TQ + TOK], TOK)),
                      Tile(chain(b0 + 24, h, TOK), None, rotate(k_rope[NOPE:QK, :], TOK, rope_tmp[:, 0, :]))]
            tiles += [Tile(chain(b0 + 32 + 8 * m, hq, TQ), copied(y_mla[:, m, :], TQ, ACT.Silu)) for m in range(4)]
            projection(f"mla_in{l}", tiles)

            def latent_after(dve):
                for m in range(2):
                    dve.scalar_tensor_tensor(zq[:, m, :], zq[:, m, :], vec(f"q_norm{l}")[:, m:m + 1], inverse[:, 0:TQ],
                                             ALU.mult, ALU.mult)
                dve.scalar_tensor_tensor(zkv[:, 0, :], zkv[:, 0, :], vec(f"kv_norm{l}"), inverse[:, TQ:TQ + TOK],
                                         ALU.mult, ALU.mult)
            sums([([lat_sq[:, 0:TQ], lat_sq[:, TQ:2 * TQ]], TQ, 256), ([lat_sq[:, 2 * TQ:2 * TQ + TOK]], TOK, 128)],
                 root, inverse, after=latent_after)

            b0 = plan[f"mla_up{l}"]
            tiles = []
            for hd in range(HEADS):
                tiles.append(Tile(chain(b0 + 2 * hd, [zq[:, 0, :], zq[:, 1, :]], TQ),
                                  copied(q_h[0:NOPE, hd, :], TQ, rows=NOPE),
                                  rotate(q_h[NOPE:QK, hd, :], TQ, rope_tmp[:, hd % 2, :])))
            def key_head(hd):
                def scalar(act, b):
                    act.activation(k_h[NOPE:QK, hd, :], k_rope[NOPE:QK, :], ACT.Copy)
                    return act.activation(k_h[0:NOPE, hd, :], b[0:NOPE, 0:TOK], ACT.Copy)
                return scalar
            for hd in range(HEADS):
                c0 = NOPE * (hd % 2)
                tiles.append(Tile(chain(b0 + 16 + hd // 2, [zkv[:, 0, :]], TOK, NOPE, (c0, c0 + NOPE)),
                                  key_head(hd)))
            for tt in range(4):
                tiles.append(Tile([(zkv[:, 0, tt * P:(tt + 1) * P], (b0 + 20, (0, P), 4), P, 0, 512, True, True)],
                                  None, copied_dve(v_t[:, tt, :], 512)))
            projection(f"mla_up{l}", tiles)

            room.at -= 3 * TOK + 4 * TOK
            probs = [room(2, TOK) for _ in range(2)]
            probs_t = [room(4, 256) for _ in range(2)]
            top = region(small, 300, 2, 2)
            total = region(small, 304, 2, 2)
            share = region(small, 308, 2, 2)
            items = [(hd, q0, 0 if q0 == 0 else SEQ) for hd in range(HEADS) for q0 in range(0, TQ, SEQ)]
            n_items = len(items)
            scored, topped, expd = sem(f"scored{l}"), sem(f"topped{l}"), sem(f"expd{l}")
            normed, turned = sem(f"normed{l}"), sem(f"turned{l}")
            turned_act, turned_dve = sem(f"turned_act{l}"), sem(f"turned_dve{l}")
            valued, gated = sem(f"valued{l}"), sem(f"y_gated{l}")
            scale = float(QK) ** -0.5

            def attn_tensor(pe):
                for i in range(n_items + 2):
                    if i < n_items:
                        hd, q0, k0 = items[i]
                        nk = TOK - k0
                        if i >= 2:
                            pe.wait_ge(expd, i - 1)
                        for t in range(2):
                            blocks.product(pe, ps[:, 2 * (i % 2) + t, 0:nk], q_h[0:QK, hd, q0 + t * P:q0 + (t + 1) * P],
                                           k_h[0:QK, hd, k0:TOK], True, True, scored if t == 1 else None)
                    if 1 <= i <= n_items:
                        hd, q0, k0 = items[i - 1]
                        nkt = (TOK - k0) // P
                        pe.wait_ge(normed, i)
                        if i >= 2:
                            pe.wait_ge(turned_act, i - 1)
                            pe.wait_ge(turned_dve, i - 1)
                        for kt in range(nkt):
                            for t in range(2):
                                mm = pe.transpose(ps[:, 4 + kt // (nkt // 2), (kt % (nkt // 2)) * 256 + t * P:
                                                     (kt % (nkt // 2)) * 256 + (t + 1) * P],
                                                  probs[(i - 1) % 2][:, t, kt * P:(kt + 1) * P], const("ident"))
                        mm.then_inc(turned, 1)
                    if i >= 2:
                        j = i - 2
                        hd, q0, k0 = items[j]
                        nkt, r0 = (TOK - k0) // P, VDIM * (hd % 2)
                        pe.wait_ge(turned_act, j + 1)
                        pe.wait_ge(turned_dve, j + 1)
                        if j >= 2:
                            pe.wait_ge(gated, j - 1)
                        for kt in range(nkt):
                            blocks.product(pe, ps[r0:r0 + VDIM, 6 + j % 2, 0:256],
                                           v_t[:, k0 // P + kt, hd * VDIM:(hd + 1) * VDIM], probs_t[j % 2][:, kt, :],
                                           kt == 0, kt == nkt - 1, valued if kt == nkt - 1 else None)

            def attn_scalar(act):
                for i in range(n_items + 1):
                    if i < n_items:
                        nk = TOK - items[i][2]
                        act.wait_ge(topped, i + 1)
                        if i >= 2:
                            act.wait_ge(turned, i - 1)
                        for t in range(2):
                            ins = act.activation(probs[i % 2][:, t, 0:nk], ps[:, 2 * (i % 2) + t, 0:nk], ACT.Exp,
                                                 bias=top[:, i % 2, t:t + 1], scale=scale,
                                                 accum_out=total[:, i % 2, t:t + 1])
                        ins.then_inc(expd, 1)
                    if i >= 1:
                        half = (TOK - items[i - 1][2]) // P // 2
                        act.wait_ge(turned, i)
                        if i >= 3:
                            act.wait_ge(valued, i - 2)
                        act.activation(probs_t[(i - 1) % 2][:, 0:half, :],
                                       ps[:, 4, 0:half * 256].rearrange("p (k q) -> p k q", q=256),
                                       ACT.Copy).then_inc(turned_act, 1)

            def attn_vector(dve):
                step = steps["dve"]
                for i in range(n_items + 2):
                    if i < n_items:
                        nk = TOK - items[i][2]
                        dve.wait_ge(scored, i + 1)
                        step(dve.tensor_reduce(share[:, i % 2, :], ps[:, 2 * (i % 2):2 * (i % 2) + 2, 0:nk], AX.X, ALU.max))
                        dve.tensor_scalar(top[:, i % 2, :], share[:, i % 2, :], -scale, None, ALU.mult).then_inc(topped, 1)
                        dve.wait_ge(expd, i + 1)
                        step(dve.reciprocal(share[:, i % 2, :], total[:, i % 2, :]))
                        for t in range(2):
                            p = probs[i % 2][:, t, 0:nk]
                            ins = dve.tensor_scalar(p, p, share[:, i % 2, t:t + 1], None, ALU.mult)
                        ins.then_inc(normed, 1)
                    if 1 <= i <= n_items:
                        half = (TOK - items[i - 1][2]) // P // 2
                        dve.wait_ge(turned, i)
                        if i >= 3:
                            dve.wait_ge(valued, i - 2)
                        dve.tensor_copy(probs_t[(i - 1) % 2][:, half:2 * half, :],
                                        ps[:, 5, 0:half * 256].rearrange("p (k q) -> p k q", q=256)).then_inc(turned_dve, 1)
                    if i >= 2:
                        hd, q0, _ = items[i - 2]
                        r0 = VDIM * (hd % 2)
                        y = y_mla[r0:r0 + VDIM, hd // 2, q0:q0 + 256]
                        dve.wait_ge(valued, i - 1)
                        dve.tensor_tensor(y, ps[r0:r0 + VDIM, 6 + i % 2, 0:256], y, ALU.mult).then_inc(gated, 1)

            stages.append(Stage(attn_tensor, attn_scalar, attn_vector, None))

            room = Room(work, 4 * TQ)
            ns = TQ // SEQ
            y_pool = room(4, TQ)
            W = SEQ + 2 * PAD
            y_gla = room(4, TQ)
            merge_at = room.at
            gq, gk, gv = room(2, TQ), room(2, TOK), room(4, 512)
            free_at = room.at
            ga, padded = room(TOK), room(4, ns, W)
            sum_a, sum_b, pooled = room(ns, W), room(ns, W), room(4, ns, SEQ)

            soft, log_a, summed = room(4, TOK), room(4, TOK), room(4, TOK)

            def clear_pads(pool):
                pool.memset(padded, 0.0)
            stages.append(Stage(None, None, None, clear_pads))

            b0 = plan[f"pool_in{l}"]
            tiles = [Tile(chain(b0 + 8 * g, hq, TQ), None,
                          lambda dve, b, g=g: dve.tensor_copy(padded[:, g, :, PAD:PAD + SEQ],
                                                              b[:, 0:TQ].rearrange("p (s t) -> p s t", s=ns)))
                     for g in range(4)]
            tiles += [Tile(chain(b0 + 32 + 8 * m, hq, TQ), copied(y_pool[:, m, :], TQ, ACT.Silu)) for m in range(4)]
            projection(f"pool_in{l}", tiles)

            def windows(pool):
                step = steps["pool"]
                for g, w in enumerate(WINDOWS):
                    src, size, lo = padded[:, g, :, :], 1, 0
                    first = True
                    for n in range(g + 1):
                        dst = (sum_a, sum_b)[n % 2]
                        back, ahead = (1, 0) if first else (size // 2, size // 2)
                        lo, hi = lo + back, W - (lo + back)
                        step(pool.tensor_tensor(dst[:, :, lo:hi], src[:, :, lo - back:hi - back],
                                                src[:, :, lo + ahead:hi + ahead], ALU.add))
                        src, size, first = dst, size * 2, False
                    step(pool.tensor_scalar(pooled[:, g, :, PAD:SEQ - PAD], src[:, :, 2 * PAD:SEQ], 1.0 / w, 0.0,
                                            ALU.mult, ALU.add))
                    for t0, e in ((0, 0), (SEQ - PAD, PAD)):
                        share = const("share")[:, 2 * g * PAD + e:2 * g * PAD + e + PAD]
                        step(pool.tensor_tensor(pooled[:, g, :, t0:t0 + PAD], src[:, :, PAD + t0:2 * PAD + t0],
                                                each(share, ns), ALU.mult))
                    step(pool.tensor_tensor(pooled[:, g, :, :], pooled[:, g, :, :], padded[:, g, :, PAD:PAD + SEQ],
                                            ALU.subtract))

            b0 = plan[f"gla_in{l}"]
            tiles = []
            for m in range(2):
                tiles.append(Tile(chain(b0 + 8 * m, hq, TQ), None,
                                  lambda dve, b, m=m: dve.tensor_scalar(gq[:, m, :], b[:, 0:TQ], 64.0 ** -0.5, None, ALU.mult)))
            for m in range(2):
                tiles.append(Tile(chain(b0 + 16 + 8 * m, h, TOK), None, copied_dve(gk[:, m, :], TOK)))
            tiles.append(Tile(chain(b0 + 32, h, TOK), None, copied_dve(ga, TOK)))
            for m in range(4):
                tiles.append(Tile(chain(b0 + 40 + 8 * m, hq, TQ), copied(y_gla[:, m, :], TQ, ACT.Silu)))
            projection(f"gla_in{l}", tiles, gpsimd=windows)

            v_filled = sem(f"gla_v_filled{l}")

            def v_tensor(pe):
                b0 = plan[f"gla_v{l}"]
                for k in range(KD):
                    for tt in range(4):
                        w = blocks.lhs(pe, b0 + 4 * k, (0, P), 4)
                        blocks.product(pe, ps[:, tt, :], hT[:, k, tt * P:(tt + 1) * P], w, k == 0, k == KD - 1,
                                       v_filled if k == KD - 1 else None)

            def v_vector(dve):
                for tt in range(0, 4, 2):
                    dve.wait_ge(v_filled, tt + 1)
                    dve.tensor_copy(gv[:, tt, :], ps[:, tt, :])

            def v_scalar(act):
                for tt in range(1, 4, 2):
                    act.wait_ge(v_filled, tt + 1)
                    act.activation(gv[:, tt, :], ps[:, tt, :], ACT.Copy)
            stages.append(Stage(v_tensor, v_scalar, v_vector, None))

            tiles = []
            for g in range(4):
                tiles.append(Tile(chain(plan[f"pool_w{l}"] + g, [pooled[:, g, :, :].rearrange("p s t -> p (s t)")], TQ), None,
                                  lambda dve, b, g=g: dve.scalar_tensor_tensor(
                                      y_pool[:, g, :], b[:, 0:TQ], vec(f"pool_scale{l}")[:, g:g + 1], y_pool[:, g, :],
                                      ALU.mult, ALU.mult)))
            projection(f"pool_w{l}", tiles)

            tiles = []
            for i in range(4):
                bias = vec(("af_b", "ab_b")[i // 2] + str(l))[:, i % 2:i % 2 + 1]
                tiles.append(Tile(chain(plan[f"gla_w{l}"] + i, [ga], TOK),
                                  lambda act, b, i=i, bias=bias: act.activation(soft[:, i, :], b[:, 0:TOK], ACT.Abs, bias=bias),
                                  lambda dve, b, i=i, bias=bias: dve.tensor_scalar(log_a[:, i, :], b[:, 0:TOK], bias, 0.0,
                                                                                   ALU.add, ALU.min)))
            projection_serial(f"gla_w{l}", tiles)

            soft_done = sem(f"soft_done{l}")

            def decay_scalar(act):
                steps["act"](act.activation(soft, soft, ACT.Exp, scale=-1.0))
                act.activation(soft, soft, ACT.Ln, bias=1.0).then_inc(soft_done, 1)

            def decay_vector(dve):
                dve.wait_ge(soft_done, 1)
                steps["dve"](dve.tensor_tensor(log_a, log_a, soft, ALU.subtract))
                for i in range(4):
                    dve.tensor_tensor_scan(summed[:, i, :], const("carry"), log_a[:, i, :], 0.0, ALU.mult, ALU.add)
            stages.append(Stage(None, decay_scalar, decay_vector, None))
            fill(l, 0, 1)

            low = Room(work, free_at)
            e_pos, e_neg = low(2, TOK), low(2, TOK)
            k_dec, k_tok = low(2, TOK), low(4, 256)
            q_pad, state = low(2, 2, TQ), low(2, 2, P)
            attn, states, o_sum = room(4, TQ // P, P), room(2, NCH, P), room(4, TQ)
            assert low.at <= room.at - 3 * 4 * TOK, "the direction's buffers reach into the decays"

            for d in range(2):
                gla_direction(l, f"{l}{d}", d, TQ, gq, gk, gv, log_a, summed, e_pos, e_neg, q_pad, k_dec, k_tok, attn,
                              state, states, o_sum)

            sq = region(work, free_at, 4, TQ)
            squares_stage(sq, o_sum)

            def gla_after(dve):
                step = steps["dve"]
                flat = lambda a: a.rearrange("p h t -> p (h t)")
                step(dve.scalar_tensor_tensor(flat(o_sum), flat(o_sum), vec(f"gla_norm{l}"), ginv, ALU.mult, ALU.mult))
                dve.tensor_tensor(y_gla, y_gla, o_sum, ALU.mult)
            groot, ginv = region(work, free_at + 4 * TQ, 4 * TQ), region(work, free_at + 8 * TQ, 4 * TQ)
            sums([([sq[:, hd, :]], TQ, P) for hd in range(4)], groot, ginv, after=gla_after)
            fill(l, 3, 6)

            room = Room(work, merge_at)
            merged, sig, tmp = room(KD, TQ), room(4, TQ), room(TQ)
            merge(f"merge{l}", plan[f"merge{l}"], [y_mla, y_pool, y_gla], hT, merged, TQ, sig, tmp)
            at = room.at if l == 0 else 18000
            o, inverse_o = residual(f"out{l}", plan[f"out{l}"], [merged[:, k, :] for k in range(KD)], TQ,
                                    [(t0, n, lambda m, c=c: posts[l][:, m, c:c + 1]) for t0, n, c in spans if t0 < TQ], at)
            last = l == DEPTH - 1
            stages.append(norm(TQ, xT[:, :, 0:TQ], region(h_sb, 0, KD, TQ),
                               scaled_by(vec("mix_pre")) if last else modulated_by(l + 1, spans),
                               at + 2 * KD * TQ + 2 * TQ if last else 0, add=(o, inverse_o)))

        def gla_direction(l, tag, d, TQ, gq, gk, gv, log_a, summed, e_pos, e_neg, q_pad, k_dec, k_tok, attn, state,
                          states, o_sum):
            visits = [4, 5, 6, 7, 0, 1, 2, 3] if d == 0 else list(range(NCH - 1, -1, -1))
            by_chunk = summed[:, 2 * d:2 * d + 2, :].rearrange("p a (c t) -> p (a c) t", t=CH)
            two = lambda a: a.rearrange("p (a c) o -> p a (c o)", a=2)
            mid, end = by_chunk[:, :, CH // 2 - 1:CH // 2], by_chunk[:, :, CH - 1:CH]
            mid2, end2 = two(mid), two(end)
            e = e_pos.rearrange("p a (c t) -> p (a c) t", t=CH)
            la = log_a[:, 2 * d:2 * d + 2, :]
            lim = GLA_LIMIT * GLA_TAU
            e_ready, e_done = sem(f"gla_e_ready{tag}"), sem(f"gla_e_done{tag}")

            def exp_vector(dve):
                step = steps["dve"]
                if d == 0:
                    step(dve.tensor_tensor(e, by_chunk, mid.to_broadcast([P, 2 * NCH, CH]), ALU.subtract))
                else:
                    step(dve.tensor_tensor(e, mid.to_broadcast([P, 2 * NCH, CH]), by_chunk, ALU.subtract))
                    step(dve.tensor_tensor(e_pos, e_pos, la, ALU.add))
                step(dve.tensor_scalar(e_pos, e_pos, -lim, lim, ALU.max, ALU.min))
                dve.memset(alpha_arg, 0.0)
                step(dve.tensor_tensor(tail, end2, mid2, ALU.subtract))
                if d == 0:
                    dve.tensor_tensor(alpha_arg[:, :, 4:7], tail[:, :, 4:7], mid2[:, :, 5:8], ALU.add)
                    dve.tensor_tensor(alpha_arg[:, :, 7:8], tail[:, :, 7:8], mid2[:, :, 0:1], ALU.add)
                    ins = dve.tensor_tensor(alpha_arg[:, :, 0:3], tail[:, :, 0:3], mid2[:, :, 1:4], ALU.add)
                else:
                    ins = dve.tensor_tensor(alpha_arg[:, :, 1:8], mid2[:, :, 1:8], tail[:, :, 0:7], ALU.add)
                ins.then_inc(e_ready, 1)
                dve.wait_ge(e_done, 1)
                for j in range(2):
                    r = slice(64 * j, 64 * j + 64)
                    dve.tensor_tensor(q_pad[r, :, j, :], gq[r, :, :], e_neg[r, :, 0:TQ], ALU.mult)
                dve.tensor_tensor(k_dec, gk, e_pos, ALU.mult)

            def exp_scalar(act):
                act.wait_ge(e_ready, 1)
                act.activation(alpha, alpha_arg, ACT.Exp, scale=1.0 / GLA_TAU)
                steps["act"](act.activation(e_neg, e_pos, ACT.Exp, scale=1.0 / GLA_TAU))
                act.activation(e_pos, e_pos, ACT.Exp, scale=-1.0 / GLA_TAU).then_inc(e_done, 1)

            def exp_gpsimd(pool):
                if d:
                    pool.memset(attn, 0.0)
                else:
                    steps["pool"](pool.memset(attn, 0.0))
                    steps["pool"](pool.memset(q_pad[0:64, :, 1, :], 0.0))
                    pool.memset(q_pad[64:P, :, 0, :], 0.0)
            stages.append(Stage(None, exp_scalar, exp_vector, exp_gpsimd))
            fill(l, 1 + d, 2 + d)

            nt = TQ // P
            k_turned, s_filled = sem(f"gla_k_turned{tag}"), sem(f"gla_s_filled{tag}")

            def intra_tensor(pe):
                for tt in range(4):
                    for pair in range(2):
                        c0 = (tt % 2) * 256 + pair * P
                        mm = pe.transpose(ps[:, tt // 2, c0:c0 + P], k_dec[:, pair, tt * P:(tt + 1) * P], const("ident"))
                    if tt % 2:
                        mm.then_inc(k_turned, 1)
                for hd in range(4):
                    for tt in range(nt):
                        t = slice(tt * P, (tt + 1) * P)
                        blocks.product(pe, ps[:, 2 + hd, t], k_dec[:, hd // 2, t], q_pad[:, hd // 2, hd % 2, t],
                                       True, True, s_filled if tt == nt - 1 else None)

            def intra_scalar(act):
                for b in range(2):
                    act.wait_ge(k_turned, b + 1)
                    act.activation(k_tok[:, 2 * b:2 * b + 2, :], ps[:, b, :].rearrange("p (t n) -> p t n", n=256), ACT.Copy)

            def intra_vector(dve):
                mask = each(const("upto" if d == 0 else "since").bitcast(U32), nt)
                for hd in range(4):
                    dve.wait_ge(s_filled, hd + 1)
                    dve.copy_predicated(attn[:, hd, :, :], mask, ps[:, 2 + hd, 0:TQ].rearrange("p (t n) -> p t n", n=P))
            stages.append(Stage(intra_tensor, intra_scalar, intra_vector, None))

            kv_filled, kv_taken = sem(f"gla_kv_filled{tag}"), sem(f"gla_kv_taken{tag}")
            carried = sem(f"gla_carried{tag}")

            def state_tensor(pe):
                n = 0
                for c in visits[:-1]:
                    r, tt = slice(CH * (c % 2), CH * (c % 2) + CH), c // 2
                    for pair in range(2):
                        if n >= 8:
                            pe.wait_ge(kv_taken, n - 7)
                        blocks.product(pe, ps[:, n % 8, 0:256], k_tok[r, tt, pair * P:(pair + 1) * P],
                                       gv[r, tt, pair * 256:(pair + 1) * 256], True, True, kv_filled)
                        n += 1

            def state_vector(dve):
                n = 0
                for i, c in enumerate(visits[:-1]):
                    for pair in range(2):
                        dve.wait_ge(kv_filled, n + 1)
                        if n >= 4:
                            dve.wait_ge(carried, n - 3)
                        if n >= 2:
                            dve.wait_ge(kv_taken, n - 1)
                        for j in range(2):
                            r = slice(64 * j, 64 * j + 64)
                            kv = ps[r, n % 8, j * P:(j + 1) * P]
                            if i == 0:
                                ins = dve.tensor_copy(state[r, 0, pair, :], kv)
                            else:
                                a = alpha[r, pair, visits[i - 1]:visits[i - 1] + 1]
                                ins = dve.scalar_tensor_tensor(state[r, i % 2, pair, :], state[r, 1 - i % 2, pair, :], a, kv,
                                                               ALU.mult, ALU.add)
                        ins.then_inc(kv_taken, 1)
                        n += 1

            def state_scalar(act):
                n = 0
                for i, c in enumerate(visits[:-1]):
                    for pair in range(2):
                        act.wait_ge(kv_taken, n + 1)
                        act.activation(states[:, pair, visits[i + 1], :], state[:, i % 2, pair, :], ACT.Copy,
                                       scale=alpha[:, pair, c:c + 1]).then_inc(carried, 1)
                        n += 1
            stages.append(Stage(state_tensor, state_scalar, state_vector, None))

            tiles = []
            for hd in range(4):
                products = []
                for tt in range(nt):
                    products.append((gv[:, tt, hd * P:(hd + 1) * P], attn[:, hd, tt, :], P, tt * P, P, True, False))
                    for c in (2 * tt, 2 * tt + 1):
                        if c != visits[0]:
                            products.append((states[:, hd // 2, c, :], q_pad[:, hd // 2, hd % 2, c * CH:(c + 1) * CH], P,
                                             c * CH, CH, False, False))
                    products[-1] = products[-1][:-1] + (True,)
                if d == 0:
                    tiles.append(Tile(products, copied(o_sum[:, hd, :], TQ)))
                else:
                    tiles.append(Tile(products, None, lambda dve, b, hd=hd: dve.tensor_tensor(
                        o_sum[:, hd, :], o_sum[:, hd, :], b[:, 0:TQ], ALU.add)))
            projection(f"gla_o{tag}", tiles)

        def fill(l, n0, n1):
            if l + 1 < DEPTH:
                fuse(modulation(l + 1, range(n0, n1)))

        for l in range(DEPTH):
            trunk(l)

        T = SEQ
        NC = T // CH
        PC = 4 * NC
        xS = xT[:, :, 0:T]
        h2 = region(h_sb, 0, KD, T)
        hk = [h2[:, k, :] for k in range(KD)]
        spare = Room(h_sb, KD * T)

        room = Room(work)
        mixed_p = room(14, T)
        r_t, k_t, v_t = mixed_p[:, 0:4, :], mixed_p[:, 4:8, :], mixed_p[:, 8:12, :]
        g_t, bonus, y_rw = room(4, T), room(4, T), room(4, T)
        r_pad, a_pad, k_pad, b_pad = [room(PC, 2, CH) for _ in range(4)]
        temp_at = room.at
        raw = region(work, temp_at, 14, T + 1)
        flat = lambda a: a.rearrange("p a t -> p (a t)")

        def pads_gpsimd(pool):
            step = steps["pool"]
            step(pool.memset(raw[:, :, 0:1], 0.0))
            for a in (r_pad, a_pad, k_pad, b_pad):
                step(pool.memset(a[0:64, :, 1, :], 0.0))
                step(pool.memset(a[64:P, :, 0, :], 0.0))
        tiles = []
        for m in range(14):
            dst = raw[:, m, 1:T + 1]
            fn = copied(dst, T) if m % 2 else None
            tiles.append(Tile(chain(plan["rw_in"] + KD * m, hk, T), fn, None if m % 2 else copied_dve(dst, T)))
        projection("rw_in", tiles, gpsimd=pads_gpsimd)

        shifted = sem("shifted")
        ranks = spare(T)

        def shift_vector(dve):
            step = steps["dve"]
            step(dve.tensor_tensor(mixed_p, raw[:, :, 0:T], raw[:, :, 1:T + 1], ALU.subtract))
            for m in range(13, -1, -1):
                ins = dve.scalar_tensor_tensor(mixed_p[:, m, :], mixed_p[:, m, :], vec("mu")[:, m:m + 1], raw[:, m, 1:T + 1],
                                               ALU.mult, ALU.add)
                if m == 12:
                    ins.then_inc(shifted, 1)

        def shift_scalar(act):
            act.wait_ge(shifted, 1)
            act.activation(ranks[0:64, :], mixed_p[0:64, 12, :], ACT.Tanh)
            act.activation(ranks[64:P, :], mixed_p[64:P, 12, :], ACT.Copy)
            act.activation(mixed_p[:, 13, :], mixed_p[:, 13, :], ACT.Sigmoid)
        stages.append(Stage(None, shift_scalar, shift_vector, None))

        room = Room(work, temp_at)
        lw, a_t, kk, k2, b_t, e_t, ex_t, tmp, root, inv = [room(4, T) for _ in range(10)]
        e1, e2, e3 = [room(4, T) for _ in range(3)]
        tiles = []
        for m in range(4):
            tiles.append(Tile(chain(plan["rw_w"] + m, [ranks], T), copied(lw[:, m, :], T, ACT.Sigmoid, bias=vec("w0")[:, m:m + 1])))
        for m in range(4):
            tiles.append(Tile(chain(plan["rw_w"] + 4 + m, [ranks], T), copied(a_t[:, m, :], T, ACT.Sigmoid, bias=vec("a0")[:, m:m + 1])))
        for m in range(4):
            tiles.append(Tile(chain(plan["rw_w"] + 8 + m, [mixed_p[:, 13, :]], T), None, copied_dve(g_t[:, m, :], T)))
        projection("rw_w", tiles)

        def keys_vector(dve):
            step = steps["dve"]
            step(dve.tensor_scalar(lw, lw, -float(np.exp(-0.5)), None, ALU.mult))
            step(dve.tensor_tensor(kk, k_t, wide(vec("k_k"), T), ALU.mult))
            dve.tensor_tensor(tmp, kk, kk, ALU.mult)
            for m in range(4):
                dve.tensor_tensor_scan(e_t[:, m, :], const("carry")[:, 0:T], lw[:, m, :], 0.0, ALU.mult, ALU.add)
        stages.append(Stage(None, None, keys_vector, None))

        kk_sum, kk_root = sem("kk_sum"), sem("kk_root")

        def kk_tensor(pe):
            for m in range(4):
                blocks.product(pe, ps[:, m // 2, (m % 2) * T:(m % 2 + 1) * T], const("head_ones"), tmp[:, m, :], True, True,
                               kk_sum if m == 3 else None)

        def kk_scalar(act):
            act.wait_ge(kk_sum, 1)
            act.activation(flat(root), ps[:, 0:2, :].rearrange("p a t -> p (a t)"), ACT.Sqrt).then_inc(kk_root, 1)

        def kk_vector(dve):
            step = steps["dve"]
            step(dve.scalar_tensor_tensor(k2, a_t, -1.0, wide(vec("k_a"), T), ALU.add, ALU.mult))
            step(dve.scalar_tensor_tensor(k2, k2, 1.0, k_t, ALU.add, ALU.mult))
            dve.wait_ge(kk_root, 1)
            step(dve.tensor_scalar(root, root, 1e-12, None, ALU.max))
            step(dve.reciprocal(flat(inv), flat(root)))
            step(dve.tensor_tensor(kk, kk, inv, ALU.mult))
            dve.tensor_tensor(b_t, kk, a_t, ALU.mult)
            step(dve.tensor_tensor(bonus, r_t, k2, ALU.mult))
            dve.tensor_tensor(bonus, bonus, wide(vec("r_k"), T), ALU.mult)
        stages.append(Stage(kk_tensor, kk_scalar, kk_vector, None))

        by_chunk = lambda a: a.rearrange("p a (c t) -> p (a c) t", t=CH)
        carry = region(small, 320, 4, NC)
        carry_arg = region(small, 340, 4, NC)
        ends = region(small, 360, 4, NC)
        rel_ready, rel_done = sem("rel_ready"), sem("rel_done")
        bonus_summed = sem("bonus_summed")

        def rel_tensor(pe):
            for m in range(4):
                blocks.product(pe, ps[:, 2 + m // 2, (m % 2) * T:(m % 2 + 1) * T], const("head_ones"), bonus[:, m, :], True,
                               True, bonus_summed if m == 3 else None)

        def rel_vector(dve):
            step = steps["dve"]
            c = by_chunk(e_t)
            mid, end = c[:, :, CH // 2 - 1:CH // 2], c[:, :, CH - 1:CH]
            four = lambda a: a.rearrange("p (a c) o -> p a (c o)", a=4)
            dve.memset(carry_arg, 0.0)
            step(dve.tensor_tensor(ends, four(end), four(mid), ALU.subtract))
            step(dve.tensor_tensor(carry_arg[:, :, 0:NC - 1], ends[:, :, 0:NC - 1], four(mid)[:, :, 1:NC], ALU.add))
            step(dve.tensor_tensor(by_chunk(tmp), c, mid.to_broadcast([P, PC, CH]), ALU.subtract))
            dve.tensor_tensor(ex_t, tmp, lw, ALU.subtract).then_inc(rel_ready, 1)
            dve.wait_ge(bonus_summed, 1)
            dve.tensor_tensor(flat(bonus), ps[:, 2:4, :].rearrange("p a t -> p (a t)"), flat(v_t), ALU.mult)
            dve.wait_ge(rel_done, 1)
            for j in range(2):
                r = slice(64 * j, 64 * j + 64)
                dve.tensor_tensor(r_pad[r, :, j, :], by_chunk(r_t)[r], by_chunk(e1)[r], ALU.mult)
                dve.scalar_tensor_tensor(a_pad[r, :, j, :], by_chunk(kk)[r], -1.0, by_chunk(e2)[r], ALU.mult, ALU.mult)
                dve.tensor_tensor(k_pad[r, :, j, :], by_chunk(k2)[r], by_chunk(e3)[r], ALU.mult)
                dve.tensor_tensor(b_pad[r, :, j, :], by_chunk(b_t)[r], by_chunk(e3)[r], ALU.mult)

        def rel_scalar(act):
            act.wait_ge(rel_ready, 1)
            act.activation(carry, carry_arg, ACT.Exp)
            act.activation(e1, tmp, ACT.Exp)
            act.activation(e2, ex_t, ACT.Exp)
            act.activation(e3, tmp, ACT.Exp, scale=-1.0).then_inc(rel_done, 1)
        stages.append(Stage(rel_tensor, rel_scalar, rel_vector, None))

        room = Room(work, temp_at)
        ab, inv_m, inv_t, mid_m, level, ak = [room(PC, P) for _ in range(6)]
        rb = region(work, 0, PC, P)
        rk = region(h_sb, KD * T, PC, P)
        pads = lambda a, i: a[:, i, :, :].rearrange("p h t -> p (h t)")

        def block_tiles(lhs, rhs, vector=None, scalar=None):
            tiles = []
            for g in range(PC // 4):
                products = [(lhs(4 * g + i), rhs(4 * g + i), P, i * P, P, True, True) for i in range(4)]
                tiles.append(Tile(products, None if scalar is None else scalar(slice(4 * g, 4 * g + 4)),
                                  None if vector is None else vector(slice(4 * g, 4 * g + 4))))
            return tiles

        bank4 = lambda b: b.rearrange("p (i t) -> p i t", t=P)

        def masked(dst, mask):
            return lambda g: lambda dve, b: dve.tensor_tensor(dst[:, g, :], bank4(b), each(const(mask), 4), ALU.mult)

        def to(dst):
            return lambda g: lambda act, b: act.activation(dst[:, g, :], bank4(b), ACT.Copy)

        def added(dst):
            return lambda g: lambda dve, b: dve.tensor_tensor(dst[:, g, :], dst[:, g, :], bank4(b), ALU.add)

        tiles = block_tiles(lambda i: pads(b_pad, i), lambda i: pads(a_pad, i), masked(ab, "before"))
        tiles += block_tiles(lambda i: pads(a_pad, i), lambda i: pads(b_pad, i), masked(inv_m, "level1_turned"))
        tiles += block_tiles(lambda i: pads(k_pad, i), lambda i: pads(a_pad, i), masked(ak, "before"))
        tiles += block_tiles(lambda i: pads(b_pad, i), lambda i: pads(r_pad, i), masked(rb, "upto"))
        tiles += block_tiles(lambda i: pads(k_pad, i), lambda i: pads(r_pad, i), masked(rk, "upto"))
        projection("rw_chunks", tiles)

        def unit_vector(dve):
            step = steps["dve"]
            step(dve.tensor_tensor(inv_t, ab, each(const("level1"), PC), ALU.mult))
            dve.tensor_tensor(inv_t, inv_t, each(const("ident"), PC), ALU.add)

        def level_scalar(b):
            def gpsimd(pool):
                pool.tensor_tensor(level, ab, each(const(f"level{b}"), PC), ALU.mult)
            return gpsimd

        def unit_pool(pool):
            steps["pool"](pool.tensor_tensor(inv_m, inv_m, each(const("ident"), PC), ALU.add))
            level_scalar(2)(pool)
        stages.append(Stage(None, None, unit_vector, unit_pool))
        for b in range(2, 7):
            projection(f"rw_join{b}", block_tiles(lambda i: level[:, i, :], lambda i: inv_m[:, i, :], scalar=to(mid_m)))
            t_tiles = block_tiles(lambda i: mid_m[:, i, :], lambda i: inv_t[:, i, :], added(inv_t))
            m_tiles = block_tiles(lambda i: inv_t[:, i, :], lambda i: mid_m[:, i, :], added(inv_m))
            tiles = []
            for g in range(PC // 4):
                tiles += [m_tiles[g], t_tiles[g]] if b < 6 else [t_tiles[g]]
            level_update(f"rw_inv{b}", tiles, 2 if b < 6 else 1, level_scalar(b + 1) if b < 6 else None)

        room = Room(work, temp_at)
        ab_, k_tok, inv_t_, b_tok, v_low, ak_ = [room(PC, P) for _ in range(6)]
        v_pad = ab
        v_tok = region(work, temp_at + 4 * PC * P, PC, CH)
        scratch = Room(work, temp_at + 4 * PC * P + PC * CH)
        w_s, u_s, g_s, h_s = scratch(4, CH), scratch(2, 4, CH), scratch(4, CH), scratch(4, CH)
        y_s = region(work, temp_at + 6 * PC * P, PC, CH)

        def v_pad_gpsimd(pool):
            steps["pool"](pool.memset(v_pad[0:64, :, 64:P], 0.0))
            pool.memset(v_pad[64:P, :, 0:64], 0.0)

        def v_pad_vector(dve):
            for j in range(2):
                r = slice(64 * j, 64 * j + 64)
                dve.tensor_copy(v_pad[r, :, 64 * j:64 * j + 64], by_chunk(v_t)[r])
        k_turned = sem("k_turned")
        k_took = [sem("k_act_took"), sem("k_dve_took")]

        def turn_tensor(pe):
            for n in range(8):
                src = (k_pad, b_pad)[n // 4]
                for i in range(4):
                    mm = pe.transpose(ps[:, n, i * P:(i + 1) * P], pads(src, 4 * (n % 4) + i), const("ident"))
                mm.then_inc(k_turned, 1)

        def turn_scalar(act):
            for n in range(4):
                act.wait_ge(k_turned, n + 1)
                act.activation(k_tok[:, 4 * n:4 * n + 4, :], bank4(ps[:, n, :]), ACT.Copy)

        def turn_vector(dve):
            v_pad_vector(dve)
            for n in range(4):
                dve.wait_ge(k_turned, n + 5)
                dve.tensor_copy(b_tok[:, 4 * n:4 * n + 4, :], bank4(ps[:, 4 + n, :]))
        stages.append(Stage(turn_tensor, turn_scalar, turn_vector, v_pad_gpsimd))

        tiles = []
        for g in range(2):
            tiles.append(Tile([(v_pad[:, 8 * g + i, :], const("ident2"), P, i * CH, CH, True, True) for i in range(8)], None,
                              lambda dve, b, g=g: dve.tensor_copy(v_tok[:, 8 * g:8 * g + 8, :],
                                                                  b.rearrange("p (i t) -> p i t", t=CH))))
        projection("rw_values", tiles)

        at_chunk = lambda a, c: a.rearrange("p (a c) t -> p a c t", c=NC)[:, :, c, :]
        bank_of = lambda n: ps[:, n, 0:4 * CH].rearrange("p (a t) -> p a t", t=CH)
        w_filled, w_taken, u_filled, u_taken = sem("w_filled"), sem("w_taken"), sem("u_filled"), sem("u_taken")
        h_filled, g_ready, y_filled, y_taken = sem("h_filled"), sem("g_ready"), sem("y_filled"), sem("y_taken")

        def seq_tensor(pe):
            for c in range(NC):
                o = lambda n, a: ps[:, n, a * CH:(a + 1) * CH]
                if c:
                    pe.wait_ge(w_taken, c)
                    pe.wait_ge(g_ready, c)
                for a in range(4):
                    i = a * NC + c
                    blocks.product(pe, o(0, a), ak[:, i, :], v_tok[:, i, :], True, c == 0,
                                   w_filled if c == 0 and a == 3 else None)
                    if c:
                        blocks.product(pe, o(0, a), pads(a_pad, i), g_s[:, a, :], False, True, w_filled if a == 3 else None)
                pe.wait_ge(w_taken, c + 1)
                if c:
                    pe.wait_ge(u_taken, c)
                for a in range(4):
                    blocks.product(pe, o(1, a), inv_t[:, a * NC + c, :], w_s[:, a, :], True, True, u_filled if a == 3 else None)
                pe.wait_ge(u_taken, c + 1)
                if c < NC - 1:
                    for a in range(4):
                        i = a * NC + c
                        blocks.product(pe, o(2, a), k_tok[:, i, :], v_tok[:, i, :], True, False)
                        blocks.product(pe, o(2, a), b_tok[:, i, :], u_s[:, c % 2, a, :], False, True, h_filled if a == 3 else None)
                if c >= 2:
                    pe.wait_ge(y_taken, c - 1)
                for a in range(4):
                    i = a * NC + c
                    blocks.product(pe, o(3 + c % 2, a), rk[:, i, :], v_tok[:, i, :], True, False)
                    if c:
                        blocks.product(pe, o(3 + c % 2, a), pads(r_pad, i), g_s[:, a, :], False, False)
                    blocks.product(pe, o(3 + c % 2, a), rb[:, i, :], u_s[:, c % 2, a, :], False, True, y_filled if a == 3 else None)

        def seq_vector(dve):
            step = steps["dve"]
            for c in range(NC):
                dve.wait_ge(w_filled, c + 1)
                dve.tensor_copy(w_s, bank_of(0)).then_inc(w_taken, 1)
                if c < NC - 1:
                    dve.wait_ge(h_filled, c + 1)
                    if c == 0:
                        src = bank_of(2)
                    else:
                        step(dve.tensor_tensor(h_s, bank_of(2), g_s, ALU.add))
                        src = h_s
                        dve.wait_ge(y_filled, c + 1)
                    dve.tensor_tensor(g_s, src, wide(carry[:, :, c], CH), ALU.mult).then_inc(g_ready, 1)

        def seq_scalar(act):
            for c in range(NC):
                act.wait_ge(u_filled, c + 1)
                if c >= 2:
                    act.wait_ge(y_filled, c - 1)
                act.activation(u_s[:, c % 2, :, :], bank_of(1), ACT.Copy).then_inc(u_taken, 1)
                act.wait_ge(y_filled, c + 1)
                act.activation(at_chunk(y_s, c), bank_of(3 + c % 2), ACT.Copy).then_inc(y_taken, 1)
        stages.append(Stage(seq_tensor, seq_scalar, seq_vector, None))

        y_bd, y_sq = k_pad.rearrange("p i h t -> p i (h t)"), region(work, temp_at, PC, CH)
        mean, var = region(small, 380, PC), region(small, 400, PC)
        var_ready, var_rooted = sem("var_ready"), sem("var_rooted")

        def norm_gpsimd(pool):
            pool.memset(y_bd, 0.0).then_inc(var_ready, 1)

        def norm_vector(dve):
            step = steps["dve"]
            step(dve.tensor_reduce(mean, y_s, AX.X, ALU.add))
            step(dve.tensor_scalar(mean, mean, 1.0 / CH, None, ALU.mult))
            step(dve.tensor_tensor(y_s, y_s, wide(mean, CH), ALU.subtract))
            step(dve.tensor_tensor(y_sq, y_s, y_s, ALU.mult))
            dve.tensor_reduce(var, y_sq, AX.X, ALU.add).then_inc(var_ready, 1)
            dve.wait_ge(var_rooted, 1)
            step(dve.reciprocal(mean, var))
            for j in range(2):
                r = slice(64 * j, 64 * j + 64)
                dve.tensor_tensor(y_bd[r, :, 64 * j:64 * j + 64], y_s[r], wide(mean[r], CH), ALU.mult)

        def norm_scalar(act):
            act.wait_ge(var_ready, 2)
            act.activation(var, var, ACT.Sqrt, bias=eps_col[:, 1:2], scale=1.0 / CH).then_inc(var_rooted, 1)
        stages.append(Stage(None, norm_scalar, norm_vector, norm_gpsimd))

        def y_out(g):
            def vector(dve, b):
                step = steps["dve"]
                for m in (2 * g, 2 * g + 1):
                    src = b[:, (m % 2) * T:(m % 2 + 1) * T]
                    step(dve.tensor_scalar(y_rw[:, m, :], src, vec("lnx_w")[:, m:m + 1], vec("lnx_b")[:, m:m + 1],
                                           ALU.mult, ALU.add))
                two = slice(2 * g, 2 * g + 2)
                step(dve.tensor_tensor(y_rw[:, two, :], y_rw[:, two, :], bonus[:, two, :], ALU.add))
                return dve.tensor_tensor(y_rw[:, two, :], y_rw[:, two, :], g_t[:, two, :], ALU.mult)
            return vector
        tiles = [Tile([(y_bd[:, 8 * g + i, :], const("ident2"), P, i * CH, CH, True, True) for i in range(8)], None, y_out(g))
                 for g in range(2)]
        projection("rw_y", tiles)

        low, high = Room(work), Room(work, 14 * T + 3 * 4 * T)
        x4, u_t = low(S5T, T), low(4, T)
        cos_t, sin_t, x1, x2, x3 = [high(S5T, T) for _ in range(5)]
        one = Room(small, 420)
        dt, mag, th, turn, f_hi, f_lo, c_re, c_im, s_r, c_r = [one(S5T) for _ in range(10)]
        two_pi = 2.0 * float(np.pi)
        pi_a = 6.28125
        pi_b = float(np.float32(round((two_pi - pi_a) * 2 ** 20) / 2 ** 20))
        pi_c = float(np.float32(two_pi - pi_a - pi_b))
        whole = 1.5 * 2 ** 23
        half_pi = 3.1415925 / 2
        full = 6.283185

        dt_done, arg_ready, arg_done = sem("dt_done"), sem("arg_ready"), sem("arg_done")
        half_col = region(small, 4, 1)

        def par_scalar(act):
            act.activation(dt, vec("log_step"), ACT.Exp).then_inc(dt_done, 1)
            act.wait_ge(arg_ready, 1)
            act.activation(mag, mag, ACT.Exp)
            act.activation(s_r, th, ACT.Sin)
            steps["act"](act.activation(c_r, th, ACT.Abs))
            act.activation(c_r, c_r, ACT.Sin, bias=half_col, scale=-1.0).then_inc(arg_done, 1)

        def par_vector(dve):
            step = steps["dve"]
            dve.memset(half_col, half_pi)
            dve.wait_ge(dt_done, 1)
            step(dve.tensor_tensor(mag, vec("a_re"), dt, ALU.mult))
            step(dve.tensor_tensor(th, vec("a_im"), dt, ALU.mult))
            step(dve.tensor_scalar(turn, th, 1.0 / two_pi, None, ALU.mult))
            step(dve.tensor_scalar(turn, turn, whole, None, ALU.add))
            step(dve.tensor_scalar(turn, turn, -whole, None, ALU.add))
            for c in (pi_a, pi_b, pi_c):
                step(dve.scalar_tensor_tensor(th, turn, -c, th, ALU.mult, ALU.add))
            step(dve.tensor_scalar(th, th, -3.1415925, 3.1415925, ALU.max, ALU.min))
            step(dve.tensor_scalar(turn, th, 1.0 / two_pi, None, ALU.mult))
            step(dve.tensor_scalar(f_hi, turn, 1.5 * 2 ** 11, None, ALU.add))
            step(dve.tensor_scalar(f_hi, f_hi, -1.5 * 2 ** 11, None, ALU.add))
            dve.tensor_tensor(f_lo, turn, f_hi, ALU.subtract).then_inc(arg_ready, 1)
            dve.wait_ge(arg_done, 1)
            re, im, den = dt, th, turn
            step(dve.tensor_tensor(s_r, s_r, mag, ALU.mult))
            step(dve.tensor_tensor(c_r, c_r, mag, ALU.mult))
            step(dve.tensor_scalar(c_r, c_r, -1.0, None, ALU.add))
            step(dve.tensor_tensor(den, vec("a_re"), vec("a_re"), ALU.mult))
            step(dve.tensor_tensor(re, vec("a_im"), vec("a_im"), ALU.mult))
            step(dve.tensor_tensor(den, den, re, ALU.add))
            step(dve.reciprocal(den, den))
            step(dve.tensor_tensor(re, c_r, vec("a_re"), ALU.mult))
            step(dve.tensor_tensor(im, s_r, vec("a_im"), ALU.mult))
            step(dve.tensor_tensor(re, re, im, ALU.add))
            step(dve.tensor_tensor(c_re, re, den, ALU.mult))
            step(dve.tensor_tensor(re, s_r, vec("a_re"), ALU.mult))
            step(dve.tensor_tensor(im, c_r, vec("a_im"), ALU.mult))
            step(dve.tensor_tensor(re, re, im, ALU.subtract))
            step(dve.tensor_tensor(c_im, re, den, ALU.mult))
        stages.append(Stage(None, par_scalar, par_vector, None))

        u_filled5, g_turns, g_abs = sem("s5_u_filled"), sem("g_turns"), sem("g_abs")

        def table_tensor(pe):
            for m in range(4):
                for k in range(KD):
                    blocks.product(pe, ps[:, m, 0:T], blocks.lhs(pe, plan["s5_in"] + KD * m + k), hk[k], k == 0, k == KD - 1,
                                   u_filled5 if k == KD - 1 else None)

        def table_vector(dve):
            step = steps["dve"]
            t = each(const("step"), S5T)
            step(dve.tensor_tensor(x1, wide(f_hi, T), t, ALU.mult))
            step(dve.tensor_scalar(x2, x1, whole, None, ALU.add))
            step(dve.tensor_scalar(x2, x2, -whole, None, ALU.add))
            step(dve.tensor_tensor(x1, x1, x2, ALU.subtract))
            step(dve.tensor_tensor(x2, wide(f_lo, T), t, ALU.mult))
            step(dve.tensor_tensor(x1, x1, x2, ALU.add))
            step(dve.tensor_scalar(x2, x1, whole, None, ALU.add))
            step(dve.tensor_scalar(x2, x2, -whole, None, ALU.add))
            dve.tensor_tensor(x1, x1, x2, ALU.subtract).then_inc(g_turns, 1)

        def table_scalar(act):
            for m in range(4):
                act.wait_ge(u_filled5, m + 1)
                act.activation(u_t[:, m, :], ps[:, m, 0:T], ACT.Copy)
            act.wait_ge(g_turns, 1)
            act.activation(x3, x1, ACT.Abs).then_inc(g_abs, 1)
            act.activation(sin_t, x1, ACT.Sin, scale=full)
            act.wait_ge(g_abs, 1)
            act.activation(cos_t, x3, ACT.Sin, bias=half_col, scale=-full)
        stages.append(Stage(table_tensor, table_scalar, table_vector, None))

        tiles = []
        for name, dst in (("s5_b_re_2", x1), ("s5_b_im_2", x2)):
            for n in range(S5T // 2):
                products = [((plan[name] + i,), u_t[:, i // 4, :], P, (i % 2) * T, T, True, True) for i in (2 * n, 2 * n + 1)]
                d2 = dst[:, 2 * n:2 * n + 2, :].rearrange("p a t -> p (a t)")
                tiles.append(Tile(products, copied(d2, 2 * T)) if n % 2 else Tile(products, None, copied_dve(d2, 2 * T)))
        projection("s5_bu", tiles)

        SPLIT = 11
        own = {"dve": slice(0, SPLIT), "pool": slice(SPLIT, S5T)}
        framed = sem("framed")
        cc = Room(h_sb, KD * T)
        cc_re, cc_im, cc_tmp = cc(S5T, 32), cc(S5T, 32), cc(S5T, 32)

        def into_frame(eng, who):
            step, i = steps[who], own[who]
            tt = lambda o, a, b, op: eng.tensor_tensor(o[:, i, :], a[:, i, :], b[:, i, :], op)
            step(tt(x3, cos_t, x1, ALU.mult))
            step(tt(x4, sin_t, x2, ALU.mult))
            step(tt(x3, x3, x4, ALU.add))
            step(tt(x4, cos_t, x2, ALU.mult))
            step(tt(x1, sin_t, x1, ALU.mult))
            return tt(x4, x4, x1, ALU.subtract)

        def out_of_frame(eng, who):
            step, i = steps[who], own[who]
            tt = lambda o, a, b, op: eng.tensor_tensor(o[:, i, :], a[:, i, :], b[:, i, :], op)
            step(tt(x3, cos_t, x1, ALU.mult))
            step(tt(x4, sin_t, x2, ALU.mult))
            step(tt(x3, x3, x4, ALU.subtract))
            step(tt(x4, sin_t, x1, ALU.mult))
            step(tt(x2, cos_t, x2, ALU.mult))
            tt(x4, x4, x2, ALU.add)

        def frame_vector(dve):
            step = steps["dve"]
            step(into_frame(dve, "dve"))
            for i in range(S5T):
                if i == SPLIT:
                    dve.wait_ge(framed, 1)
                for dst, src in ((x1, x3), (x2, x4)):
                    dve.tensor_tensor_scan(dst[:, i, :], mag[:, i:i + 1].to_broadcast([P, T]), src[:, i, :], 0.0,
                                           ALU.mult, ALU.add)
            w = lambda v: wide(v, 32)
            cv = lambda n: vec(n).rearrange("p (i c) -> p i c", c=32)
            dve.tensor_tensor(cc_re, cv("c_re"), w(c_re), ALU.mult)
            step(dve.tensor_tensor(cc_tmp, cv("c_im"), w(c_im), ALU.mult))
            step(dve.tensor_tensor(cc_re, cc_re, cc_tmp, ALU.subtract))
            dve.tensor_tensor(cc_im, cv("c_re"), w(c_im), ALU.mult)
            step(dve.tensor_tensor(cc_tmp, cv("c_im"), w(c_re), ALU.mult))
            step(dve.scalar_tensor_tensor(cc_im, cc_im, -1.0, cc_tmp, ALU.mult, ALU.subtract))

        def frame_gpsimd(pool):
            into_frame(pool, "pool").then_inc(framed, 1)
        stages.append(Stage(None, None, frame_vector, frame_gpsimd))

        stages.append(Stage(None, None, lambda dve: out_of_frame(dve, "dve"), lambda pool: out_of_frame(pool, "pool")))

        wide_re, wide_im = region(work, high.at - 3 * S5T * T, S5T, P), region(work, high.at - 3 * S5T * T + S5T * P, S5T, P)
        cleared = sem("c_cleared")

        def c_gpsimd(pool):
            steps["pool"](pool.memset(wide_re, 0.0))
            pool.memset(wide_im, 0.0).then_inc(cleared, 1)

        def c_vector(dve):
            dve.wait_ge(cleared, 1)
            quads = lambda a: a.rearrange("p (q i) c -> p q i c", i=4)
            for i in range(4):
                for dst, src in ((wide_re, cc_re), (wide_im, cc_im)):
                    dve.tensor_copy(quads(dst)[:, :, i, 32 * i:32 * i + 32], quads(src)[:, :, i, :])
        stages.append(Stage(None, None, c_vector, c_gpsimd))

        yroom = Room(work, high.at - 2 * S5T * T)
        y_pre, y_sig, y_s5 = yroom(4, T), yroom(4, T), yroom(4, T)
        tiles = []
        for q in range(4):
            products = []
            for i in range(4 * q, 4 * q + 4):
                products.append((wide_re[:, i, :], x3[:, i, :], P, 0, T, i == 4 * q, False))
                products.append((wide_im[:, i, :], x4[:, i, :], P, 0, T, False, i == 4 * q + 3))
            tiles.append(Tile(products, None, lambda dve, b, q=q: dve.scalar_tensor_tensor(
                y_pre[:, q, :], u_t[:, q, :], vec("s5_d")[:, q:q + 1], b[:, 0:T], ALU.mult, ALU.add)))
        projection("s5_y", tiles)
        stages.append(Stage(None, lambda act: act.activation(y_s5, y_pre, ACT.Gelu_apprx_tanh), None, None))
        projection("s5_glu", [Tile(chain(plan["s5_glu"] + 4 * m, [y_s5[:, k, :] for k in range(4)], T),
                                   copied(y_sig[:, m, :], T, ACT.Sigmoid, bias=vec("b_glu")[:, m:m + 1])) for m in range(4)])
        stages.append(Stage(None, None, lambda dve: dve.tensor_tensor(y_s5, y_s5, y_sig, ALU.mult), None))

        room = Room(work)
        merged, sig, tmp2 = room(KD, T), room(4, T), room(T)
        merge("merge2", plan["merge2"], [y_rw, y_s5], h2, merged, T, sig, tmp2, bias=vec("b_gate"))
        o2, inverse2 = residual("out2", plan["out2"], [merged[:, k, :] for k in range(KD)], T,
                                [(0, T, lambda m: vec("mix_post")[:, m:m + 1])], 14 * T + 12 * T)

        stages.append(norm(T, xS, h2, scaled_by(vec("ffn_pre")), 0, add=(o2, inverse2)))
        room = Room(work, 8192)
        hidden = room(FT, T)
        conv = room(2, 2, T)
        gelu = room(2, T)
        up_filled, affine, convolved = sem("up_filled"), sem("affine"), sem("convolved")
        gelud, hidden_done = sem("gelud"), sem("hidden_done")
        tap = lambda j, m: vec("conv_w")[:, j * 2 * FT + m:j * 2 * FT + m + 1]

        def up_tensor(pe):
            for i in range(2 * FT):
                if i >= 8:
                    pe.wait_ge(convolved, i - 7)
                for k in range(KD):
                    blocks.product(pe, ps[:, i % 8, 0:T], blocks.lhs(pe, plan["ff_up"] + KD * i + k), hk[k], k == 0, k == KD - 1,
                                   up_filled if k == KD - 1 else None)

        def up_scalar(act):
            for j in range(FT):
                for v in range(2):
                    i, m = 2 * j + v, j + v * FT
                    act.wait_ge(up_filled, i + 1)
                    if j >= 2:
                        act.wait_ge(hidden_done, j - 1)
                    act.activation(conv[:, j % 2, v, :], ps[:, i % 8, 0:T], ACT.Identity, bias=vec("conv_b")[:, m:m + 1],
                                   scale=tap(2, m)).then_inc(affine, 1)
                act.wait_ge(convolved, 2 * j + 1)
                act.activation(gelu[:, j % 2, :], conv[:, j % 2, 0, :], ACT.Gelu_apprx_tanh).then_inc(gelud, 1)

        def up_vector(dve):
            step = steps["dve"]
            for j in range(FT):
                for v in range(2):
                    i, m = 2 * j + v, j + v * FT
                    dve.wait_ge(affine, i + 1)
                    z = conv[:, j % 2, v, :]
                    step(dve.scalar_tensor_tensor(z[:, 1:T], ps[:, i % 8, 0:T - 1], tap(1, m), z[:, 1:T], ALU.mult, ALU.add))
                    dve.scalar_tensor_tensor(z[:, 2:T], ps[:, i % 8, 0:T - 2], tap(0, m), z[:, 2:T], ALU.mult,
                                             ALU.add).then_inc(convolved, 1)
                dve.wait_ge(gelud, j + 1)
                dve.wait_ge(convolved, 2 * j + 2)
                dve.tensor_tensor(hidden[:, j, :], gelu[:, j % 2, :], conv[:, j % 2, 1, :], ALU.mult).then_inc(hidden_done, 1)
        stages.append(Stage(up_tensor, up_scalar, up_vector, None))
        residual("ff_down", plan["ff_down"], [hidden[:, j, :] for j in range(FT)], T,
                 [(0, T, lambda m: vec("ffn_post")[:, m:m + 1])], 16384, last_x=xS)

        def rejoin(eng, n):
            eng.drain().then_inc(stage_done, 1)
            eng.wait_ge(stage_done, 4 * n)

        block = ctx.enter_context(nc.Block())

        @block.sync
        def _(sp):
            sp.dma_start(c_sb, c_in.rearrange("p (k c) -> p k c", c=2)).then_inc(inputs_loaded, 16)
            sp.dma_start(vec_sb[:, :], vectors).then_inc(inputs_loaded, 16)
            sp.dma_start(const_sb[:, :], constants).then_inc(inputs_loaded, 16)
            for i in range(n_panels):
                if i >= SLOTS:
                    sp.wait_ge(panel_used, i - SLOTS + 1)
                n = PANEL * P
                s = i % SLOTS
                sp.dma_start(panels[:, s * n:(s + 1) * n], weights[i]).then_inc(panel_loaded[s], 16)
                if i == SLOTS - 1:
                    sp.dma_start(x_sb[:, :], x_in).then_inc(x_loaded, 16)
            sp.wait_ge(stage_done, 4 * len(stages))
            sp.dma_start(out, xS).then_inc(out_stored, 16)
            sp.wait_ge(out_stored, 16)

        @block.tensor
        def _(pe):
            for n, stage in enumerate(stages, 1):
                if stage.tensor is not None:
                    stage.tensor(pe)
                rejoin(pe, n)

        @block.scalar
        def _(act):
            steps["act"] = Steps(act, act_step)
            for n, stage in enumerate(stages, 1):
                if stage.scalar is not None:
                    stage.scalar(act)
                rejoin(act, n)

        @block.vector
        def _(dve):
            steps["dve"] = Steps(dve, dve_step)
            for n, stage in enumerate(stages, 1):
                if stage.vector is not None:
                    stage.vector(dve)
                rejoin(dve, n)

        @block.gpsimd
        def _(pool):
            steps["pool"] = Steps(pool, pool_step)
            for n, stage in enumerate(stages, 1):
                if stage.gpsimd is not None:
                    stage.gpsimd(pool)
                rejoin(pool, n)


def by_partition(a, cols):
    return np.asarray(a).reshape(cols, P).T


def lay_out(inputs):
    _, order = stream_plan()
    w = np.zeros((-(-len(order) // PANEL) * PANEL, P, P), np.float32)
    for n, pieces in enumerate(order):
        for piece in pieces:
            a = inputs[piece.array][piece.index]
            a = a.T if piece.turned else a
            w[n, piece.row:piece.row + a.shape[0], piece.col:piece.col + a.shape[1]] = a
    w = np.ascontiguousarray(w.reshape(-1, PANEL, P, P).transpose(0, 2, 1, 3)).reshape(-1, P, PANEL * P)
    vec_at, sources, n_vec = vector_plan()
    v = np.zeros((P, n_vec), np.float32)
    for at, cols, array, l in sources:
        v[:, at:at + cols] = by_partition(inputs[array][l], cols)
    at, cols = vec_at["log_step"]
    v[:, at:at + cols] = by_partition(np.repeat(inputs["s5_log_step_2"][0], 64), cols)
    for name, array in (("c_re", "s5_c_re_2"), ("c_im", "s5_c_im_2")):
        at, cols = vec_at[name]
        c = np.zeros((P, S5T, 32), np.float32)
        pairs = inputs[array][0].reshape(S5T, 2, 16, 64)
        for j in range(2):
            c[64 * j:64 * j + 64, :, 16 * j:16 * j + 16] = pairs[:, j].transpose(2, 0, 1)
        v[:, at:at + cols] = c.reshape(P, cols)
    tokens = np.concatenate([inputs["x"][0], inputs["ctx"][0]], 0)
    x = np.ascontiguousarray(tokens.T.reshape(KD, P, TOK).transpose(1, 0, 2)).reshape(P, KD * TOK)
    conds = np.stack([inputs["c"][0], inputs["c_ctx"]], -1)
    c = np.ascontiguousarray(conds.reshape(KD, P, 2).transpose(1, 0, 2)).reshape(P, KD * 2)
    constants = np.ascontiguousarray(np.concatenate(list(constant_plan().values()), 1)).astype(np.float32)
    return dict(weights=w, vectors=v, constants=constants, x_in=x, c_in=c)


def kernel(**inputs):
    import concourse.bacc as bacc
    from concourse.bass_utils import run_bass_kernel_spmd

    arrays = lay_out({k: np.asarray(v) for k, v in inputs.items()})
    nc = bacc.Bacc("TRN2", target_bir_lowering=False, num_devices=1)
    args = {k: nc.dram_tensor(k, a.shape, F32, kind="ExternalInput").ap() for k, a in arrays.items()}
    out = nc.dram_tensor("out", (P, KD, SEQ), F32, kind="ExternalOutput").ap()
    build(nc, out=out, **args)
    r = run_bass_kernel_spmd(nc, [arrays], core_ids=[0])
    y = np.asarray(r.results[0]["out"])
    return np.ascontiguousarray(y.transpose(1, 0, 2).reshape(D, SEQ).T)[None]
```

```python
from collections import namedtuple
from contextlib import ExitStack

import numpy as np

import concourse.bass as bass
from concourse import mybir

P = 128
D = 1024
KD = D // P
SEQ = 256
CTX = 256
TOK = SEQ + CTX
DEPTH = 2
HEADS, NOPE, ROPE, VDIM = 8, 64, 32, 64
QK = NOPE + ROPE
GRID_W = 64
ROPE_BASE = 10000.0
WINDOWS = (2, 4, 8, 16)
PAD = max(WINDOWS) // 2
CH = 64
NCH = TOK // CH
GLA_TAU = 16.0
GLA_LIMIT = 80.0
EPS = 1e-6
LNX_EPS = 64e-5
S5T = 16
FF = 2816
FT = FF // P
IN_SIZES = dict(mla_q=256, mla_kv=128, mla_kr=32, mla_gate=512, pool_x=512, pool_gate=512, gla_q=256,
                gla_k=256, gla_v=512, gla_af=16, gla_ab=16, gla_gate=512, merge=3 * D)
IN_AT = dict(zip(IN_SIZES, np.cumsum([0] + list(IN_SIZES.values()))[:-1].tolist()))
RW = 512
S5_AT = 3 * RW + 64 + 64 + 128
G2_AT = S5_AT + 512

PANEL = 8
SLOTS = 6
HI_SLOTS = 4

F32 = mybir.dt.float32
F32R = mybir.dt.float32r
U32 = mybir.dt.uint32
ALU = mybir.AluOpType
ACT = mybir.ActivationFunctionType
AX = mybir.AxisListType

Piece = namedtuple("Piece", "array index turned row col")
Stage = namedtuple("Stage", "tensor scalar vector gpsimd", defaults=(None, None, None, None))
Tile = namedtuple("Tile", "products scalar vector", defaults=(None, None))


class Pair:
    def __init__(self, hi, lo):
        self.hi, self.lo = hi, lo

    def __getitem__(self, at):
        return Pair(self.hi[at], self.lo[at])



def part(array, l, r0, nr, c0, nc, row=0, col=0):
    return Piece(array, (l, slice(r0, r0 + nr), slice(c0, c0 + nc)), False, row, col)


def tiles_of(array, l, rows, c0, cols):
    return [[part(array, l, k * P, P, c0 + m * P, P)] for m in range(cols // P) for k in range(rows // P)]


def rotated(array, l, r0, c0, col):
    h, q = ROPE // 2, ROPE // 4
    return [part(array, l, r0, P, c0 + a * h + (1 - b) * q, q, 0, col + a * h + b * q) for a in range(2) for b in range(2)]


def stream_plan():
    plan, order, split_panels = {}, [], []

    def add(name, blocks, split=False):
        if len(order) % PANEL and split != split_panels[-1]:
            order.extend([[]] * (-len(order) % PANEL))
        plan[name] = len(order)
        order.extend(blocks)
        split_panels.extend([split] * (-(-len(order) // PANEL) - len(split_panels)))

    def mod(l):
        add(f"mod{l}", [[part("mod_w", l, k * P, P, n * 512 + q * P, P)] for n in range(6) for k in range(KD) for q in range(4)])

    mod(0)
    for l in range(DEPTH):
        z = lambda name: tiles_of("w_in", l, D, IN_AT[name], IN_SIZES[name])
        kr = [[part("w_in", l, k * P, P, IN_AT["mla_kr"], ROPE, 0, NOPE)]
              + rotated("w_in", l, k * P, IN_AT["mla_kr"], QK) for k in range(KD)]
        add(f"mla_in{l}", z("mla_q") + z("mla_kv") + kr + z("mla_gate"), split=True)
        q = [[part("mla_w_uq", l, k * P, P, h * QK, QK)] + rotated("mla_w_uq", l, k * P, h * QK + NOPE, QK)
             for h in range(HEADS) for k in range(2)]
        k = [[part("mla_w_ukv", l, 0, P, (h + j) * 128, NOPE, 0, j * NOPE) for j in range(2)] for h in range(0, HEADS, 2)]
        v = [[part("mla_w_ukv", l, 0, P, (h + j) * 128 + NOPE, VDIM, 0, j * VDIM) for j in range(2)]
             for h in range(0, HEADS, 2)]
        add(f"mla_up{l}", q + k + v)
        add(f"pool_in{l}", z("pool_x") + z("pool_gate"), split=True)
        a = [[part("w_in", l, k * P, P, IN_AT["gla_af"], 32)] for k in range(KD)]
        add(f"gla_in{l}", z("gla_q") + z("gla_k") + a + z("gla_gate"), split=True)
        add(f"gla_v{l}", [[part("w_in", l, k * P, P, IN_AT["gla_v"] + n * P, P)] for k in range(KD) for n in range(4)],
            split=True)
        add(f"pool_w{l}", [[Piece("pool_w", (l, g), False, 0, 0)] for g in range(len(WINDOWS))])
        add(f"gla_w{l}", [[part("gla_af_w2", l, 0, 16, m * P, P)] for m in range(2)]
            + [[part("gla_ab_w2", l, 0, 16, m * P, P, 16)] for m in range(2)])
        if l + 1 < DEPTH:
            mod(l + 1)
        merge = []
        for m in range(KD):
            for b, name in enumerate(("w_branch_mla", "w_branch_pool", "w_branch_gla")):
                merge += tiles_of("w_in", l, D, IN_AT["merge"] + b * D + m * P, P) + tiles_of(name, l, 512, m * P, P)
        add(f"merge{l}", merge, split=True)
        add(f"out{l}", tiles_of("w_out", l, D, 0, D), split=True)
    add("s5_in", tiles_of("w_in_2", 0, D, S5_AT, 512), split=True)
    for name in ("s5_b_re_2", "s5_b_im_2"):
        add(name, [[Piece(name, (0, 2 * i + j), True, 32 * (i % 4) + 16 * j, 64 * j) for j in range(2)] for i in range(S5T)])
    add("rw_in", tiles_of("w_in_2", 0, D, 0, S5_AT), split=True)
    add("s5_glu", tiles_of("s5_w_glu_2", 0, 512, 0, 512))
    add("rw_w", [[part("rwkv_w2_2", 0, 0, 64, m * P, P)] for m in range(4)]
        + [[part("rwkv_a2_2", 0, 0, 64, m * P, P, 64)] for m in range(4)] + tiles_of("rwkv_g2_2", 0, P, 0, RW))
    merge = []
    for m in range(KD):
        for b, name in enumerate(("w_branch_rwkv_2", "w_branch_s5_2")):
            merge += tiles_of("w_in_2", 0, D, G2_AT + b * D + m * P, P) + tiles_of(name, 0, 512, m * P, P)
    add("merge2", merge, split=True)
    add("out2", tiles_of("w_out_2", 0, D, 0, D), split=True)
    up = []
    for j in range(FT):
        up += tiles_of("ffn_w_up_2", 0, D, j * P, P) + tiles_of("ffn_w_up_2", 0, D, FF + j * P, P)
    add("ff_up", up, split=True)
    add("ff_down", tiles_of("ffn_w_down_2", 0, FF, 0, D), split=True)
    return plan, order, split_panels


def vector_plan():
    at, src, n = {}, [], 0

    def add(name, array, l, cols):
        nonlocal n
        at[name] = (n, cols)
        src.append((n, cols, array, l))
        n += cols

    for l in range(DEPTH):
        for name, array, cols in (("pre", "pre_norm", 8), ("post", "post_norm", 8), ("mod_b", "mod_b", 24),
                                  ("q_norm", "mla_q_norm", 2), ("kv_norm", "mla_kv_norm", 1),
                                  ("pool_scale", "pool_scale", 4), ("af_b", "gla_af_b", 2), ("ab_b", "gla_ab_b", 2),
                                  ("gla_norm", "gla_norm", 1)):
            add(f"{name}{l}", array, l, cols)
    for name, array, cols in (("mix_pre", "norm_mix_pre_2", 8), ("mix_post", "norm_mix_post_2", 8),
                              ("ffn_pre", "norm_ffn_pre_2", 8), ("ffn_post", "norm_ffn_post_2", 8),
                              ("b_gate", "b_gate_2", 16), ("mu", "rwkv_shift_mu_2", 14), ("w0", "rwkv_w0_2", 4),
                              ("a0", "rwkv_a0_2", 4), ("k_k", "rwkv_k_k_2", 4), ("k_a", "rwkv_k_a_2", 4),
                              ("r_k", "rwkv_r_k_2", 4), ("lnx_w", "rwkv_lnx_w_2", 4), ("lnx_b", "rwkv_lnx_b_2", 4),
                              ("a_re", "s5_a_re_2", 16), ("a_im", "s5_a_im_2", 16), ("s5_d", "s5_d_2", 4),
                              ("b_glu", "s5_b_glu_2", 4), ("conv_w", "ffn_conv_w_2", 3 * 2 * FT),
                              ("conv_b", "ffn_conv_b_2", 2 * FT)):
        add(name, array, 0, cols)
    for name, cols in (("log_step", 16), ("c_re", 32 * S5T), ("c_im", 32 * S5T)):
        at[name] = (n, cols)
        n += cols
    return at, src, n


def constant_plan():
    p = np.arange(P)
    row, col = p[:, None], p[None, :]
    same = row // CH == col // CH
    f = lambda a: a.astype(np.float32)
    t = dict(ident=f(row == col), ones=np.ones((P, P), np.float32), head_ones=f(same),
             ident2=f(row % CH == np.arange(CH)[None, :]),
             upto=f(same & (row <= col)), since=f(same & (row >= col)), before=f(same & (row < col)))
    for b in range(1, 7):
        t[f"level{b}"] = f((row < col) & (row >> b == col >> b) & (row >> (b - 1) != col >> (b - 1)))
    t["level1_turned"] = np.ascontiguousarray(t["level1"].T)
    half = ROPE // 2
    inv = np.float32(ROPE_BASE) ** (-np.arange(0, half, 2, dtype=np.float32) / np.float32(half))
    pos = np.arange(SEQ)
    ang_r, ang_c = f(pos // GRID_W)[:, None] * inv, f(pos % GRID_W)[:, None] * inv
    ang = np.concatenate([ang_r, ang_r, ang_c, ang_c], -1).astype(np.float32)
    sign = np.where(np.arange(ROPE) % half < half // 2, -1.0, 1.0).astype(np.float32)
    rope = np.zeros((P, TOK), np.float32)
    rope[NOPE:QK, :SEQ], rope[NOPE:QK, SEQ:] = np.cos(ang).T, 1.0
    rope[QK:, :SEQ] = (np.sin(ang) * sign).T
    t["rope"] = rope
    share = [1.0 / (np.clip(pos + w // 2, 0, SEQ) - np.clip(pos - w // 2, 0, SEQ)) for w in WINDOWS]
    edges = [np.concatenate([a[:PAD], a[-PAD:]]) for a in share]
    t["share"] = np.broadcast_to(f(np.concatenate(edges))[None], (P, 4 * 2 * PAD))
    t["carry"] = np.broadcast_to(f(np.arange(TOK) % CH != 0)[None], (P, TOK))
    t["step"] = np.broadcast_to(f(np.arange(SEQ))[None], (P, SEQ))
    return t


def build(nc, weights, vectors, constants, x_in, c_in, out):
    plan, order, split_panels = stream_plan()
    to_split = [p for p, split in enumerate(split_panels) if split]
    vec_at, _, n_vec = vector_plan()
    const_at, n_const = {}, 0
    for name, a in constant_plan().items():
        const_at[name] = (n_const, a.shape[1])
        n_const += a.shape[1]
    n_panels = -(-len(order) // PANEL)
    WORK = 25128

    ctx = ExitStack()
    with ctx:
        def sb(name, cols, dtype=F32, scope=ctx):
            return scope.enter_context(nc.sbuf_tensor(name, [P, cols], dtype))

        def sem(name):
            return ctx.enter_context(nc.semaphore(name))

        vec_sb, const_sb = sb("vec_sb", n_vec), sb("const_sb", n_const)
        x_sb, small = sb("x_sb", KD * TOK), sb("small", 1024)
        panels_hi = sb("panels_hi", HI_SLOTS * PANEL * P, F32R)
        shared_memory = dict(panels=SLOTS * PANEL * P, h_sb=KD * TOK, hi_sb=KD * TOK, work=WORK)
        with ExitStack() as in_float32:
            panels, h_sb, hi_sb, work = [sb(name, cols, F32, in_float32) for name, cols in shared_memory.items()]
        panels_r, h_sb_r, hi_sb_r, work_r = [sb(name + "_r", cols, F32R) for name, cols in shared_memory.items()]
        ps = ctx.enter_context(nc.psum_tensor("ps", [P, 8, 512], F32))

        panel_loaded = [sem(f"panel_loaded{i}") for i in range(SLOTS)]
        panel_used, panel_rounded, panel_split = sem("panel_used"), sem("panel_rounded"), sem("panel_split")
        pool_done = sem("pool_done")
        c_loaded, vectors_loaded, constants_loaded = sem("c_loaded"), sem("vectors_loaded"), sem("constants_loaded")
        x_loaded, stage_done, out_stored = sem("x_loaded"), sem("stage_done"), sem("out_stored")
        dve_step, act_step, pool_step = sem("dve_step"), sem("act_step"), sem("pool_step")

        shared_sems = {}

        def shared(kind, n):
            if kind not in shared_sems:
                shared_sems[kind] = [sem(kind), 0]
            shared_sems[kind][1] += n
            return shared_sems[kind][0], shared_sems[kind][1] - n

        def vec(name):
            return vec_sb[:, vec_at[name][0]:sum(vec_at[name])]

        def const(name):
            return const_sb[:, const_at[name][0]:sum(const_at[name])]

        def region(base, at, *dims):
            n = int(np.prod(dims))
            assert at + n <= base.shape[1], (at, n, base.shape)
            v = base[:, at:at + n]
            if len(dims) == 1:
                return v
            names = "abcd"[:len(dims)]
            return v.rearrange(f"p ({' '.join(names)}) -> p {' '.join(names)}",
                               **dict(zip(names[1:], dims[1:])))

        class Room:
            def __init__(self, base, at=0):
                self.base, self.at = base, at

            def __call__(self, *dims):
                self.at += int(np.prod(dims))
                return region(self.base, self.at - int(np.prod(dims)), *dims)

        def wide(a, n):
            k = len(a.shape)
            v = a.rearrange("p (a o) -> p a o", o=1) if k == 2 else a.rearrange("p a (b o) -> p a b o", o=1)
            return v.to_broadcast(list(a.shape) + [n])

        def each(a, n):
            return a.rearrange("p (o a) -> p o a", o=1).to_broadcast([a.shape[0], n, a.shape[1]])

        class Steps:
            def __init__(self, eng, stepped):
                self.eng, self.stepped, self.n = eng, stepped, 0

            def __call__(self, ins):
                self.n += 1
                ins.then_inc(self.stepped, 1)
                self.eng.wait_ge(self.stepped, self.n)

        steps = {}

        def panel_at(p):
            return (p % SLOTS) * PANEL * P

        def hi_at(n):
            return (n % HI_SLOTS) * PANEL * P

        class Blocks:
            def __init__(self):
                self.panel, self.freed, self.n_split = -1, 0, 0
                self.reached = {}

            def lhs(self, pe, i, cols=(0, P), n=1):
                p = i // PANEL
                assert p >= self.panel
                while self.panel < p:
                    self.panel += 1
                    if split_panels[self.panel]:
                        self.n_split += 1
                        pe.wait_ge(panel_split, self.n_split)
                    else:
                        pe.wait_ge(panel_loaded[self.panel % SLOTS], 16 * (self.panel // SLOTS + 1))
                part = lambda base, at: base[:, at + i % PANEL * P + cols[0]:at + (i % PANEL + n - 1) * P + cols[1]]
                if split_panels[p]:
                    return Pair(part(panels_hi, hi_at(self.n_split - 1)), part(panels_r, panel_at(p)))
                return part(panels, panel_at(p))

            def product(self, pe, o, lhsT, rhs, start=True, stop=True, signal=None):
                if isinstance(lhsT, Pair):
                    pe.matmul(o, lhsT.hi, rhs.hi, start=start, stop=False)
                    pe.matmul(o, lhsT.hi, rhs.lo, start=False, stop=False)
                    mm = pe.matmul(o, lhsT.lo, rhs.hi, start=False, stop=stop)
                else:
                    mm = pe.matmul(o, lhsT, rhs, start=start, stop=stop)
                if signal is not None:
                    mm.then_inc(signal, 1)
                elif self.freed < self.panel:
                    self.freed += 1
                    mm.then_inc(panel_used, 1)

            def mark(self, *point):
                self.reached[point] = self.freed, self.panel

        class Rounding:
            def __init__(self):
                self.n, self.freed = 0, 0
                self.after_stage = [0]

            def before(self, act, *point):
                freed, panel = blocks.reached[point]
                self.freed = max(self.freed, freed)
                while self.n < len(to_split):
                    p, old = to_split[self.n], to_split[self.n - HI_SLOTS] if self.n >= HI_SLOTS else -1
                    if p > panel and (old >= self.freed or p - SLOTS >= self.freed):
                        break
                    act.wait_ge(panel_loaded[p % SLOTS], 16 * (p // SLOTS + 1))
                    if old >= 0:
                        act.wait_ge(panel_used, old + 1)
                    n, m = panel_at(p), hi_at(self.n)
                    act.activation(panels_hi[:, m:m + PANEL * P], panels[:, n:n + PANEL * P], ACT.Copy).then_inc(panel_rounded, 1)
                    self.n += 1

        rounding = Rounding()

        def take_rest(pool, n):
            at, m = panel_at(to_split[n]), hi_at(n)
            pool.wait_ge(panel_rounded, n + 1)
            pool.tensor_tensor(panels_r[:, at:at + PANEL * P], panels[:, at:at + PANEL * P], panels_hi[:, m:m + PANEL * P],
                               ALU.subtract).then_inc(panel_split, 1)

        blocks = Blocks()
        stages = []


        def projection(name, tiles, bank0=0, banks=8, first=None, then=None):
            n_act = np.cumsum([t.scalar is not None for t in tiles]).tolist()
            n_dve = np.cumsum([t.vector is not None for t in tiles]).tolist()
            filled, f0 = shared("tile_filled", len(tiles))
            by_act, a0 = shared("tile_act_took", n_act[-1])
            by_dve, d0 = shared("tile_dve_took", n_dve[-1])

            def tensor(pe):
                for i, t in enumerate(tiles):
                    if i >= banks:
                        if n_act[i - banks]:
                            pe.wait_ge(by_act, a0 + n_act[i - banks])
                        if n_dve[i - banks]:
                            pe.wait_ge(by_dve, d0 + n_dve[i - banks])
                    for j, (lhsT, rhs, rows, c0, n, start, stop) in enumerate(t.products):
                        w = blocks.lhs(pe, *lhsT) if isinstance(lhsT, tuple) else lhsT
                        if isinstance(rhs, tuple):
                            rhs = blocks.lhs(pe, *rhs)
                        blocks.product(pe, ps[0:rows, bank0 + i % banks, c0:c0 + n], w, rhs, start, stop,
                                       filled if j == len(t.products) - 1 else None)
                    blocks.mark("tile", f0 + i)

            def scalar(act):
                for i, t in enumerate(tiles):
                    if t.scalar is not None:
                        rounding.before(act, "tile", f0 + i)
                        act.wait_ge(filled, f0 + i + 1)
                        t.scalar(act, ps[:, bank0 + i % banks, :]).then_inc(by_act, 1)

            def vector(dve):
                if first is not None:
                    first(dve)
                for i, t in enumerate(tiles):
                    if t.vector is not None:
                        dve.wait_ge(filled, f0 + i + 1)
                        t.vector(dve, ps[:, bank0 + i % banks, :]).then_inc(by_dve, 1)
                if then is not None:
                    then(dve)

            stages.append(Stage(tensor, scalar, vector, None))

        def chain(block0, rhs, n, rows=P, cols=(0, P)):
            return [((block0 + k, cols), r, rows, 0, n, k == 0, k == len(rhs) - 1) for k, r in enumerate(rhs)]

        def copied(dst, n, func=ACT.Copy, rows=P, **kw):
            return lambda act, b: act.activation(dst, b[0:rows, 0:n], func, **kw)

        def copied_dve(dst, n):
            return lambda dve, b: dve.tensor_copy(dst, b[:, 0:n])

        def sums(groups, root, inverse, after=None):
            (summed, s0), (rooted, r0) = shared("squares_summed", 1), shared("rooted", 1)
            at = np.cumsum([0] + [n for _, n, _ in groups]).tolist()

            def tensor(pe):
                for i, (squares, n, _) in enumerate(groups):
                    for k, s in enumerate(squares):
                        last = i == len(groups) - 1 and k == len(squares) - 1
                        blocks.product(pe, ps[:, i, 0:n], const("ones"), s, k == 0, k == len(squares) - 1,
                                       summed if last else None)

            def scalar(act):
                act.wait_ge(summed, s0 + 1)
                for i, (_, n, width) in enumerate(groups):
                    ins = act.activation(root[:, at[i]:at[i + 1]], ps[:, i, 0:n], ACT.Sqrt, bias=eps_col[:, 0:1],
                                         scale=1.0 / width)
                ins.then_inc(rooted, 1)

            def vector(dve):
                dve.wait_ge(rooted, r0 + 1)
                steps["dve"](dve.reciprocal(inverse[:, 0:at[-1]], root[:, 0:at[-1]]))
                if after is not None:
                    after(dve)

            stages.append(Stage(tensor, scalar, vector))

        eps_col = region(small, 0, 4)

        c_sb = region(small, 4, KD, 2)
        silu_c = region(small, 20, KD, 2)
        mods = [region(small, 40 + 64 * l, 24, 2) for l in range(DEPTH)]
        gains = [region(small, 168 + 16 * l, KD, 2) for l in range(DEPTH)]
        posts = [region(small, 200 + 16 * l, KD, 2) for l in range(DEPTH)]
        alpha = region(small, 232, 2, NCH)
        alpha_arg = region(small, 250, 2, NCH)
        tail = region(small, 270, 2, NCH)

        def start_scalar(act):
            act.wait_ge(c_loaded, 16)
            act.activation(silu_c, c_sb, ACT.Silu)

        def start_vector(dve):
            dve.memset(eps_col[:, 0:1], EPS)
            dve.memset(eps_col[:, 1:2], LNX_EPS)
            dve.memset(eps_col[:, 2:3], 0.0)

        stages.append(Stage(None, start_scalar, start_vector, None))

        mod_filled, mod_row, mod_used, mod_turned = sem("mod_filled"), sem("mod_row"), sem("mod_used"), sem("mod_turned")
        row_sb = region(small, 512, 512)
        MOD_CHUNKS = 6

        def modulation(l, chunks):
            def tensor(pe):
                for n in chunks:
                    i = l * MOD_CHUNKS + n
                    if i:
                        pe.wait_ge(mod_row, i)
                    for k in range(KD):
                        w = blocks.lhs(pe, plan[f"mod{l}"] + (n * KD + k) * 4, (0, P), 4)
                        blocks.product(pe, ps[0:2, 6, :], silu_c[:, k, :], w, k == 0, k == KD - 1,
                                       mod_filled if k == KD - 1 else None)
                    pe.wait_ge(mod_row, i + 1)
                    if i == 0:
                        pe.wait_ge(constants_loaded, 16)
                    if i:
                        pe.wait_ge(mod_used, i)
                    for q in range(4):
                        mm = pe.transpose(ps[:, 7, 2 * q:2 * q + 2], row_sb[0:2, q * P:(q + 1) * P], const("ident")[0:2, 0:2])
                    mm.then_inc(mod_turned, 1)

            def scalar(act):
                for n in chunks:
                    i = l * MOD_CHUNKS + n
                    act.wait_ge(mod_filled, i + 1)
                    if i:
                        act.wait_ge(mod_turned, i)
                    act.activation(row_sb[0:2, :], ps[0:2, 6, :], ACT.Copy).then_inc(mod_row, 1)

            def vector(dve):
                step = steps["dve"]
                for n in chunks:
                    i = l * MOD_CHUNKS + n
                    m = slice(4 * n, 4 * n + 4)
                    if i == 0:
                        dve.wait_ge(vectors_loaded, 16)
                    dve.wait_ge(mod_turned, i + 1)
                    ins = dve.tensor_tensor(mods[l][:, m, :], ps[:, 7, 0:8].rearrange("p (m c) -> p m c", c=2),
                                            wide(vec(f"mod_b{l}")[:, m], 2), ALU.add)
                    ins.then_inc(mod_used, 1)
                    dve.wait_ge(mod_used, i + 1)
                    m8 = slice(4 * n % 8, 4 * n % 8 + 4)
                    if n // 2 == 1:
                        step(dve.scalar_tensor_tensor(gains[l][:, m8, :], mods[l][:, m, :], 1.0,
                                                      wide(vec(f"pre{l}")[:, m8], 2), ALU.add, ALU.mult))
                    elif n // 2 == 2:
                        step(dve.tensor_tensor(posts[l][:, m8, :], mods[l][:, m, :], wide(vec(f"post{l}")[:, m8], 2), ALU.mult))
            return Stage(tensor, scalar, vector, None)

        def fuse(*others):
            parts = (stages.pop(),) + others

            def both(name):
                fs = [f for f in (p[name] for p in parts) if f is not None]
                return (lambda eng: [f(eng) for f in fs]) if fs else None
            stages.append(Stage(*(both(i) for i in range(4))))

        def squares_stage(dst, src, then=None):
            def scalar(act):
                act.activation(dst, src, ACT.Square)
                if then is not None:
                    then(act)
            stages.append(Stage(None, scalar, None, None))

        def load_x(eng):
            eng.dma_start(x_sb[:, :], x_in).then_inc(x_loaded, 16)

        def scaled_by(gain):
            def vector(dve, m, x, h, inverse):
                return dve.scalar_tensor_tensor(h[:, m, :], x[:, m, :], gain[:, m:m + 1], inverse, ALU.mult, ALU.mult)

            def scalar(act, m, h, hi):
                return act.activation(hi[:, m, :], h[:, m, :], ACT.Copy)

            def rest(dve, m, h, hi, lo):
                dve.tensor_tensor(lo[:, m, :], h[:, m, :], hi[:, m, :], ALU.subtract)
            return vector, scalar, rest

        def modulated_by(l, spans):
            def vector(dve, m, x, h, inverse):
                for t0, n, c in spans:
                    ins = dve.scalar_tensor_tensor(h[:, m, t0:t0 + n], x[:, m, t0:t0 + n], gains[l][:, m, c:c + 1],
                                                   inverse[:, t0:t0 + n], ALU.mult, ALU.mult)
                return ins

            def scalar(act, m, h, hi):
                for t0, n, c in spans:
                    ins = act.activation(hi[:, m, t0:t0 + n], h[:, m, t0:t0 + n], ACT.Identity, bias=mods[l][:, m, c:c + 1])
                return ins

            def rest(dve, m, h, hi, lo):
                for t0, n, c in spans:
                    t = slice(t0, t0 + n)
                    dve.scalar_tensor_tensor(lo[:, m, t], h[:, m, t], mods[l][:, m, c:c + 1], hi[:, m, t], ALU.add, ALU.subtract)
            return vector, scalar, rest

        def norm(T, x, h, split, scale, at, add=None):
            sq, root, inverse = region(work, at, KD, T), region(work, at + KD * T, T), region(work, at + KD * T + T, T)
            order = [5, 6, 7, 0, 1, 2, 3, 4]
            added = add is not None
            (times, t0) = shared("o_times", KD * added)
            (by_pool, p0), (by_dve, d0) = shared("x_pool_added", 3 * added), shared("x_dve_added", 5 * added)
            (squared, q0), (summed, s0), (rooted, r0) = shared("x_squared", KD), shared("x_summed", 1), shared("x_rooted", 1)
            (scaled, c0), (rounded, h0) = shared("x_scaled", KD), shared("h_rounded", KD)

            def tensor(pe):
                for i, m in enumerate(order):
                    pe.wait_ge(squared, q0 + i + 1)
                    blocks.product(pe, ps[:, 0, 0:T], const("ones"), sq[:, m, :], i == 0, i == KD - 1,
                                   summed if i == KD - 1 else None)

            def scalar(act):
                if add is None:
                    act.wait_ge(x_loaded, 16)
                for i, m in enumerate(order):
                    if add is not None:
                        if i < 3:
                            act.wait_ge(by_pool, p0 + i + 1)
                        else:
                            act.wait_ge(by_dve, d0 + i - 2)
                    act.activation(sq[:, m, :], x[:, m, :], ACT.Square).then_inc(squared, 1)
                act.wait_ge(summed, s0 + 1)
                act.activation(root, ps[:, 0, 0:T], ACT.Sqrt, bias=eps_col[:, 0:1], scale=1.0 / D).then_inc(rooted, 1)
                for m in range(KD):
                    act.wait_ge(scaled, c0 + m + 1)
                    scale[1](act, m, h, split.hi).then_inc(rounded, 1)

            def vector(dve):
                step = steps["dve"]
                if add is not None:
                    o, inv = add
                    for i, m in enumerate(order):
                        dve.tensor_tensor(o[:, m, :], o[:, m, :], inv, ALU.mult).then_inc(times, 1)
                        if i >= 4:
                            j = order[i - 1]
                            dve.wait_ge(times, t0 + i)
                            dve.tensor_tensor(x[:, j, :], x[:, j, :], o[:, j, :], ALU.add).then_inc(by_dve, 1)
                    dve.wait_ge(times, t0 + KD)
                    dve.tensor_tensor(x[:, 4, :], x[:, 4, :], o[:, 4, :], ALU.add).then_inc(by_dve, 1)
                dve.wait_ge(rooted, r0 + 1)
                step(dve.reciprocal(inverse, root))
                for m in range(KD + 1):
                    if m < KD:
                        scale[0](dve, m, x, h, inverse).then_inc(scaled, 1)
                    if m:
                        dve.wait_ge(rounded, h0 + m)
                        scale[2](dve, m - 1, h, split.hi, split.lo)

            def gpsimd(pool):
                for i, m in enumerate(order[:3]):
                    pool.wait_ge(times, t0 + i + 1)
                    pool.tensor_tensor(x[:, m, :], x[:, m, :], add[0][:, m, :], ALU.add).then_inc(by_pool, 1)
                    pool.wait_ge(by_pool, p0 + i + 1)
            return Stage(tensor, scalar, vector, gpsimd if add is not None else None)

        def residual(name, block0, rhs, T, gain_cols, at, last_x=None):
            o, sq = region(work, at, KD, T), region(work, at + KD * T, KD, T)
            root, inverse = region(work, at + 2 * KD * T, T), region(work, at + 2 * KD * T + T, T)
            kt = len(rhs)

            def taken(m):
                def scalar(act, b):
                    act.activation(sq[:, m, :], b[:, 0:T], ACT.Square)
                    for t0, n, gain in gain_cols:
                        ins = act.activation(o[:, m, t0:t0 + n], b[:, t0:t0 + n], ACT.Copy, scale=gain(m))
                    return ins
                return scalar
            projection(name, [Tile(chain(block0 + m * kt, rhs, T), taken(m)) for m in range(KD)])

            def after(dve):
                for half in ((0, 4), (4, 8)):
                    m = slice(*half)
                    steps["dve"](dve.tensor_tensor(o[:, m, :], o[:, m, :], each(inverse, 4), ALU.mult))
                    dve.tensor_tensor(last_x[:, m, :], last_x[:, m, :], o[:, m, :], ALU.add)
            sums([([sq[:, k, :] for k in range(KD)], T, D)], root, inverse, after=None if last_x is None else after)
            return o, inverse

        def projection_serial(name, tiles, banks=8):
            filled, f0 = shared("serial_filled", len(tiles))
            by_act, a0 = shared("serial_act_took", len(tiles))
            by_dve, d0 = shared("serial_dve_took", len(tiles))

            def tensor(pe):
                for i, t in enumerate(tiles):
                    if i >= banks:
                        pe.wait_ge(by_dve, d0 + i - banks + 1)
                    for j, (lhsT, rhs, rows, c0, n, start, stop) in enumerate(t.products):
                        blocks.product(pe, ps[0:rows, i % banks, c0:c0 + n], blocks.lhs(pe, *lhsT), rhs, start, stop,
                                       filled if j == len(t.products) - 1 else None)

            def scalar(act):
                for i, t in enumerate(tiles):
                    act.wait_ge(filled, f0 + i + 1)
                    t.scalar(act, ps[:, i % banks, :]).then_inc(by_act, 1)

            def vector(dve):
                for i, t in enumerate(tiles):
                    dve.wait_ge(by_act, a0 + i + 1)
                    t.vector(dve, ps[:, i % banks, :]).then_inc(by_dve, 1)

            stages.append(Stage(tensor, scalar, vector, None))

        def level_update(name, tiles, per, gpsimd):
            filled, f0 = shared("level_filled", len(tiles))

            def tensor(pe):
                for i, t in enumerate(tiles):
                    for j, (lhsT, rhs, rows, c0, n, start, stop) in enumerate(t.products):
                        blocks.product(pe, ps[0:rows, i, c0:c0 + n], lhsT, rhs, start, stop,
                                       filled if j == len(t.products) - 1 else None)

            def vector(dve):
                for i, t in enumerate(tiles):
                    dve.wait_ge(filled, f0 + (i // per + 1) * per)
                    t.vector(dve, ps[:, i, :])

            stages.append(Stage(tensor, None, vector, gpsimd))

        def merge(name, block0, branches, h, merged, merged_split, T, sig, tmp, bias=None, loaded=None, aside=({}, {})):
            nb = len(branches)
            (y_rounded, r0), (y_split, s0) = shared("y_rounded", nb), shared("y_split", nb)
            filled, f0 = shared("merge_filled", 2 * KD * nb)
            gated, g0 = shared("merge_gated", KD * nb)
            mixed, m0 = shared("merge_mixed", KD * nb)

            def tensor(pe):
                i, at = 0, block0
                for m in range(KD):
                    for b in range(nb):
                        if i >= 4:
                            pe.wait_ge(mixed, m0 + i - 3)
                        for k in range(KD):
                            blocks.product(pe, ps[:, 2 * (i % 4), 0:T], blocks.lhs(pe, at + k), h[:, k, 0:T], k == 0,
                                           k == KD - 1, filled if k == KD - 1 else None)
                        blocks.mark("gate", f0 + 2 * i)
                        if m == 0:
                            pe.wait_ge(y_split, s0 + b + 1)
                        for k in range(4):
                            blocks.product(pe, ps[:, 2 * (i % 4) + 1, 0:T], blocks.lhs(pe, at + KD + k),
                                           branches[b][1][:, k, :], k == 0, k == 3, filled if k == 3 else None)
                        at += KD + 4
                        i += 1

            def scalar(act):
                for y, parts in branches:
                    act.activation(parts.hi, y, ACT.Copy).then_inc(y_rounded, 1)
                for i in range(KD * nb):
                    rounding.before(act, "gate", f0 + 2 * i)
                    act.wait_ge(filled, f0 + 2 * i + 1)
                    if i >= 4:
                        act.wait_ge(mixed, m0 + i - 3)
                    col = i // nb + (i % nb) * KD
                    kw = {} if bias is None else dict(bias=bias[:, col:col + 1])
                    act.activation(sig[:, i % 4, :], ps[:, 2 * (i % 4), 0:T], ACT.Sigmoid, **kw).then_inc(gated, 1)
                    if i in aside[0]:
                        aside[0][i](act)

            def vector(dve):
                step = steps["dve"]
                if loaded is not None:
                    dve.wait_ge(x_loaded, loaded)
                for b, (y, parts) in enumerate(branches):
                    dve.wait_ge(y_rounded, r0 + b + 1)
                    dve.tensor_tensor(parts.lo, y, parts.hi, ALU.subtract).then_inc(y_split, 1)
                for i in range(KD * nb):
                    m, b = divmod(i, nb)
                    dve.wait_ge(filled, f0 + 2 * i + 2)
                    dve.wait_ge(gated, g0 + i + 1)
                    dst = merged[:, m, :] if b == 0 else tmp
                    dve.tensor_tensor(dst, ps[:, 2 * (i % 4) + 1, 0:T], sig[:, i % 4, :], ALU.mult).then_inc(mixed, 1)
                    if b:
                        dve.wait_ge(mixed, m0 + i + 1)
                        step(dve.tensor_tensor(merged[:, m, :], merged[:, m, :], tmp, ALU.add))
                    if b == nb - 1:
                        step(dve.tensor_copy(merged_split.hi[:, m, :], merged[:, m, :]))
                        dve.tensor_tensor(merged_split.lo[:, m, :], merged[:, m, :], merged_split.hi[:, m, :], ALU.subtract)
                    if i in aside[1]:
                        aside[1][i](dve)

            stages.append(Stage(tensor, scalar, vector, None))

        xT = region(x_sb, 0, KD, TOK)
        hT, h_split = region(h_sb, 0, KD, TOK), Pair(region(hi_sb_r, 0, KD, TOK), region(h_sb_r, 0, KD, TOK))

        spans = [(0, SEQ, 0), (SEQ, CTX, 1)]

        def trunk(l):
            TQ = TOK if l < DEPTH - 1 else SEQ
            h = [h_split[:, k, :] for k in range(KD)]
            hq = [h_split[:, k, 0:TQ] for k in range(KD)]

            if l == 0:
                stages.append(modulation(0, range(MOD_CHUNKS)))
                stages.append(norm(TOK, xT, hT, h_split, modulated_by(0, spans), 0))

            room = Room(work)
            y_mla = room(4, TQ)
            zq, zkv = room(2, TQ), room(1, TOK)
            k_rope, rope_tmp = room(TOK), room(2, TOK)
            q_h, k_h = room(HEADS, TQ), room(HEADS, TOK)
            v_t = room(4, 512)
            lat_sq, root, inverse = room(3 * TOK), room(2 * TOK), room(2 * TOK)
            b0 = plan[f"mla_in{l}"]
            rope = const("rope")

            def rotate(dst, T, tmp):
                def vector(dve, b):
                    dve.tensor_tensor(dst, b[NOPE:QK, 0:T], rope[NOPE:QK, 0:T], ALU.mult)
                    steps["dve"](dve.tensor_tensor(tmp[NOPE:QK, 0:T], b[QK:P, 0:T], rope[QK:P, 0:T], ALU.mult))
                    return dve.tensor_tensor(dst, dst, tmp[NOPE:QK, 0:T], ALU.add)
                return vector

            def latent(z, square, n):
                def scalar(act, b):
                    act.activation(z, b[:, 0:n], ACT.Copy)
                    return act.activation(square, b[:, 0:n], ACT.Square)
                return scalar
            tiles = [Tile(chain(b0 + 8 * m, hq, TQ), latent(zq[:, m, :], lat_sq[:, m * TQ:(m + 1) * TQ], TQ)) for m in range(2)]
            tiles += [Tile(chain(b0 + 16, h, TOK), latent(zkv[:, 0, :], lat_sq[:, 2 * TQ:2 * TQ + TOK], TOK)),
                      Tile(chain(b0 + 24, h, TOK), None, rotate(k_rope[NOPE:QK, :], TOK, rope_tmp[:, 0, :]))]
            tiles += [Tile(chain(b0 + 32 + 8 * m, hq, TQ), copied(y_mla[:, m, :], TQ, ACT.Silu)) for m in range(4)]
            projection(f"mla_in{l}", tiles)

            def latent_after(dve):
                for m in range(2):
                    dve.scalar_tensor_tensor(zq[:, m, :], zq[:, m, :], vec(f"q_norm{l}")[:, m:m + 1], inverse[:, 0:TQ],
                                             ALU.mult, ALU.mult)
                dve.scalar_tensor_tensor(zkv[:, 0, :], zkv[:, 0, :], vec(f"kv_norm{l}"), inverse[:, TQ:TQ + TOK],
                                         ALU.mult, ALU.mult)
            sums([([lat_sq[:, 0:TQ], lat_sq[:, TQ:2 * TQ]], TQ, 256), ([lat_sq[:, 2 * TQ:2 * TQ + TOK]], TOK, 128)],
                 root, inverse, after=latent_after)

            b0 = plan[f"mla_up{l}"]
            tiles = []
            for hd in range(HEADS):
                tiles.append(Tile(chain(b0 + 2 * hd, [zq[:, 0, :], zq[:, 1, :]], TQ),
                                  copied(q_h[0:NOPE, hd, :], TQ, rows=NOPE),
                                  rotate(q_h[NOPE:QK, hd, :], TQ, rope_tmp[:, hd % 2, :])))
            def key_head(hd):
                def scalar(act, b):
                    act.activation(k_h[NOPE:QK, hd, :], k_rope[NOPE:QK, :], ACT.Copy)
                    return act.activation(k_h[0:NOPE, hd, :], b[0:NOPE, 0:TOK], ACT.Copy)
                return scalar
            for hd in range(HEADS):
                c0 = NOPE * (hd % 2)
                tiles.append(Tile(chain(b0 + 16 + hd // 2, [zkv[:, 0, :]], TOK, NOPE, (c0, c0 + NOPE)),
                                  key_head(hd)))
            for tt in range(4):
                tiles.append(Tile([(zkv[:, 0, tt * P:(tt + 1) * P], (b0 + 20, (0, P), 4), P, 0, 512, True, True)],
                                  None, copied_dve(v_t[:, tt, :], 512)))
            projection(f"mla_up{l}", tiles)

            room.at -= 3 * TOK + 4 * TOK
            probs = [room(2, TOK) for _ in range(3)]
            probs_t = [room(4, 256) for _ in range(2)]
            top, total, share = [region(small, 300 + 6 * i, 3, 2) for i in range(3)]
            items = [(hd, q0, 0 if q0 == 0 else SEQ) for hd in range(HEADS) for q0 in range(0, TQ, SEQ)]
            n_items = len(items)
            scored, topped, expd = sem(f"scored{l}"), sem(f"topped{l}"), sem(f"expd{l}")
            normed, turned = sem(f"normed{l}"), sem(f"turned{l}")
            turned_act, turned_dve = sem(f"turned_act{l}"), sem(f"turned_dve{l}")
            valued, gated = sem(f"valued{l}"), sem(f"y_gated{l}")
            scale = float(QK) ** -0.5

            def attn_tensor(pe):
                for i in range(n_items + 3):
                    if i < n_items:
                        hd, q0, k0 = items[i]
                        nk = TOK - k0
                        if i >= 2:
                            pe.wait_ge(expd, i - 1)
                        for t in range(2):
                            blocks.product(pe, ps[:, 2 * (i % 2) + t, 0:nk], q_h[0:QK, hd, q0 + t * P:q0 + (t + 1) * P],
                                           k_h[0:QK, hd, k0:TOK], True, True, scored if t == 1 else None)
                    if 2 <= i < n_items + 2:
                        j = i - 2
                        nkt = (TOK - items[j][2]) // P
                        pe.wait_ge(normed, j + 1)
                        if j >= 1:
                            pe.wait_ge(turned_act, j)
                            pe.wait_ge(turned_dve, j)
                        for kt in range(nkt):
                            for t in range(2):
                                mm = pe.transpose(ps[:, 4 + kt // (nkt // 2), (kt % (nkt // 2)) * 256 + t * P:
                                                     (kt % (nkt // 2)) * 256 + (t + 1) * P],
                                                  probs[j % 3][:, t, kt * P:(kt + 1) * P], const("ident"))
                        mm.then_inc(turned, 1)
                    if i >= 3:
                        j = i - 3
                        hd, q0, k0 = items[j]
                        nkt, r0 = (TOK - k0) // P, VDIM * (hd % 2)
                        pe.wait_ge(turned_act, j + 1)
                        pe.wait_ge(turned_dve, j + 1)
                        if j >= 2:
                            pe.wait_ge(gated, j - 1)
                        for kt in range(nkt):
                            blocks.product(pe, ps[r0:r0 + VDIM, 6 + j % 2, 0:256],
                                           v_t[:, k0 // P + kt, hd * VDIM:(hd + 1) * VDIM], probs_t[j % 2][:, kt, :],
                                           kt == 0, kt == nkt - 1, valued if kt == nkt - 1 else None)

            def attn_scalar(act):
                for i in range(n_items + 2):
                    if i < n_items:
                        nk = TOK - items[i][2]
                        act.wait_ge(topped, i + 1)
                        if i >= 3:
                            act.wait_ge(turned, i - 2)
                        for t in range(2):
                            ins = act.activation(probs[i % 3][:, t, 0:nk], ps[:, 2 * (i % 2) + t, 0:nk], ACT.Exp,
                                                 bias=top[:, i % 3, t:t + 1], scale=scale,
                                                 accum_out=total[:, i % 3, t:t + 1])
                        ins.then_inc(expd, 1)
                    if i >= 2:
                        j = i - 2
                        half = (TOK - items[j][2]) // P // 2
                        act.wait_ge(turned, j + 1)
                        if j >= 2:
                            act.wait_ge(valued, j - 1)
                        act.activation(probs_t[j % 2][:, 0:half, :],
                                       ps[:, 4, 0:half * 256].rearrange("p (k q) -> p k q", q=256),
                                       ACT.Copy).then_inc(turned_act, 1)

            def attn_vector(dve):
                step = steps["dve"]
                for i in range(n_items + 3):
                    if i < n_items:
                        nk = TOK - items[i][2]
                        dve.wait_ge(scored, i + 1)
                        step(dve.tensor_reduce(share[:, i % 3, :], ps[:, 2 * (i % 2):2 * (i % 2) + 2, 0:nk], AX.X, ALU.max))
                        dve.tensor_scalar(top[:, i % 3, :], share[:, i % 3, :], -scale, None, ALU.mult).then_inc(topped, 1)
                        dve.wait_ge(topped, i + 1)
                    if 1 <= i <= n_items:
                        j = i - 1
                        nk = TOK - items[j][2]
                        dve.wait_ge(expd, j + 1)
                        step(dve.reciprocal(share[:, j % 3, :], total[:, j % 3, :]))
                        for t in range(2):
                            p = probs[j % 3][:, t, 0:nk]
                            ins = dve.tensor_scalar(p, p, share[:, j % 3, t:t + 1], None, ALU.mult)
                        ins.then_inc(normed, 1)
                    if 2 <= i < n_items + 2:
                        j = i - 2
                        half = (TOK - items[j][2]) // P // 2
                        dve.wait_ge(turned, j + 1)
                        if j >= 2:
                            dve.wait_ge(valued, j - 1)
                        dve.tensor_copy(probs_t[j % 2][:, half:2 * half, :],
                                        ps[:, 5, 0:half * 256].rearrange("p (k q) -> p k q", q=256)).then_inc(turned_dve, 1)
                    if i >= 3:
                        j = i - 3
                        hd, q0, _ = items[j]
                        r0 = VDIM * (hd % 2)
                        y = y_mla[r0:r0 + VDIM, hd // 2, q0:q0 + 256]
                        dve.wait_ge(valued, j + 1)
                        dve.tensor_tensor(y, ps[r0:r0 + VDIM, 6 + j % 2, 0:256], y, ALU.mult).then_inc(gated, 1)

            stages.append(Stage(attn_tensor, attn_scalar, attn_vector, None))

            room = Room(work, 4 * TQ)
            ns = TQ // SEQ
            y_pool = room(4, TQ)
            W = SEQ + 2 * PAD
            y_gla = room(4, TQ)
            merge_at = room.at
            gq, gk, gv = room(2, TQ), room(2, TOK), room(4, 512)
            free_at = room.at
            ga, padded = room(TOK), room(4, ns, W)
            sum_a, sum_b, pooled = room(ns, W), room(ns, W), room(4, ns, SEQ)

            soft = room(4, TOK)
            decays_at = room.at = max(room.at, free_at + 3 * 2 * TOK + 4 * 256 + 4 * TQ + 4 * P)
            log_a, summed = room(4, TOK), room(4, TOK)

            def clear_pads(dve):
                steps["dve"](dve.memset(padded, 0.0))

            b0 = plan[f"pool_in{l}"]
            tiles = [Tile(chain(b0 + 8 * g, hq, TQ), None,
                          lambda dve, b, g=g: dve.tensor_copy(padded[:, g, :, PAD:PAD + SEQ],
                                                              b[:, 0:TQ].rearrange("p (s t) -> p s t", s=ns)))
                     for g in range(4)]
            tiles += [Tile(chain(b0 + 32 + 8 * m, hq, TQ), copied(y_pool[:, m, :], TQ, ACT.Silu)) for m in range(4)]
            projection(f"pool_in{l}", tiles, first=clear_pads)

            def windows(dve):
                step = steps["dve"]
                for g, w in enumerate(WINDOWS):
                    src, size, lo = padded[:, g, :, :], 1, 0
                    first = True
                    for n in range(g + 1):
                        dst = (sum_a, sum_b)[n % 2]
                        back, ahead = (1, 0) if first else (size // 2, size // 2)
                        lo, hi = lo + back, W - (lo + back)
                        step(dve.tensor_tensor(dst[:, :, lo:hi], src[:, :, lo - back:hi - back],
                                                src[:, :, lo + ahead:hi + ahead], ALU.add))
                        src, size, first = dst, size * 2, False
                    step(dve.tensor_scalar(pooled[:, g, :, PAD:SEQ - PAD], src[:, :, 2 * PAD:SEQ], 1.0 / w, 0.0,
                                            ALU.mult, ALU.add))
                    for t0, e in ((0, 0), (SEQ - PAD, PAD)):
                        share = const("share")[:, 2 * g * PAD + e:2 * g * PAD + e + PAD]
                        step(dve.tensor_tensor(pooled[:, g, :, t0:t0 + PAD], src[:, :, PAD + t0:2 * PAD + t0],
                                                each(share, ns), ALU.mult))
                    step(dve.tensor_tensor(pooled[:, g, :, :], pooled[:, g, :, :], padded[:, g, :, PAD:PAD + SEQ],
                                            ALU.subtract))

            b0 = plan[f"gla_in{l}"]
            tiles = []
            for m in range(2):
                tiles.append(Tile(chain(b0 + 8 * m, hq, TQ), None,
                                  lambda dve, b, m=m: dve.tensor_scalar(gq[:, m, :], b[:, 0:TQ], 64.0 ** -0.5, None, ALU.mult)))
            for m in range(2):
                tiles.append(Tile(chain(b0 + 16 + 8 * m, h, TOK), None, copied_dve(gk[:, m, :], TOK)))
            tiles.append(Tile(chain(b0 + 32, h, TOK), None, copied_dve(ga, TOK)))
            for m in range(4):
                tiles.append(Tile(chain(b0 + 40 + 8 * m, hq, TQ), copied(y_gla[:, m, :], TQ, ACT.Silu)))
            projection(f"gla_in{l}", tiles, then=windows)

            v_filled = sem(f"gla_v_filled{l}")

            def v_tensor(pe):
                b0 = plan[f"gla_v{l}"]
                for k in range(KD):
                    for tt in range(4):
                        w = blocks.lhs(pe, b0 + 4 * k, (0, P), 4)
                        blocks.product(pe, ps[:, tt, :], h_split[:, k, tt * P:(tt + 1) * P], w, k == 0, k == KD - 1,
                                       v_filled if k == KD - 1 else None)
                blocks.mark("gla_v", l)

            def v_vector(dve):
                for tt in range(0, 4, 2):
                    dve.wait_ge(v_filled, tt + 1)
                    dve.tensor_copy(gv[:, tt, :], ps[:, tt, :])

            def v_scalar(act):
                rounding.before(act, "gla_v", l)
                for tt in range(1, 4, 2):
                    act.wait_ge(v_filled, tt + 1)
                    act.activation(gv[:, tt, :], ps[:, tt, :], ACT.Copy)
            stages.append(Stage(v_tensor, v_scalar, v_vector, None))

            tiles = []
            for g in range(4):
                tiles.append(Tile(chain(plan[f"pool_w{l}"] + g, [pooled[:, g, :, :].rearrange("p s t -> p (s t)")], TQ), None,
                                  lambda dve, b, g=g: dve.scalar_tensor_tensor(
                                      y_pool[:, g, :], b[:, 0:TQ], vec(f"pool_scale{l}")[:, g:g + 1], y_pool[:, g, :],
                                      ALU.mult, ALU.mult)))
            projection(f"pool_w{l}", tiles)

            tiles = []
            for i in range(4):
                bias = vec(("af_b", "ab_b")[i // 2] + str(l))[:, i % 2:i % 2 + 1]
                tiles.append(Tile(chain(plan[f"gla_w{l}"] + i, [ga], TOK),
                                  lambda act, b, i=i, bias=bias: act.activation(soft[:, i, :], b[:, 0:TOK], ACT.Abs, bias=bias),
                                  lambda dve, b, i=i, bias=bias: dve.tensor_scalar(log_a[:, i, :], b[:, 0:TOK], bias, 0.0,
                                                                                   ALU.add, ALU.min)))
            projection_serial(f"gla_w{l}", tiles)

            soft_done = sem(f"soft_done{l}")

            def decay_scalar(act):
                steps["act"](act.activation(soft, soft, ACT.Exp, scale=-1.0))
                act.activation(soft, soft, ACT.Ln, bias=1.0).then_inc(soft_done, 1)

            def decay_vector(dve):
                dve.wait_ge(soft_done, 1)
                steps["dve"](dve.tensor_tensor(log_a, log_a, soft, ALU.subtract))
                for i in range(4):
                    dve.tensor_tensor_scan(summed[:, i, :], const("carry"), log_a[:, i, :], 0.0, ALU.mult, ALU.add)
            stages.append(Stage(None, decay_scalar, decay_vector, None))
            fill(l, 0, 1)

            low = Room(work, free_at)
            e_pos, e_neg = low(2, TOK), low(2, TOK)
            k_dec, k_tok = low(2, TOK), low(4, 256)
            q_pad, state = low(2, 2, TQ), low(2, 2, P)
            if l == 0:
                lent = Room(x_sb)
                attn, states, o_sum = lent(4, TQ // P, P), lent(2, NCH, P), room(4, TQ)
            else:
                attn, states, o_sum = room(4, TQ // P, P), room(2, NCH, P), room(4, TQ)
            assert low.at <= decays_at, "the direction's buffers reach into the decays"

            for d in range(2):
                gla_direction(l, f"{l}{d}", d, TQ, gq, gk, gv, log_a, summed, e_pos, e_neg, q_pad, k_dec, k_tok, attn,
                              state, states, o_sum)

            sq = region(work, free_at, 4, TQ)
            squares_stage(sq, o_sum, then=load_x if l == 0 else None)

            def gla_after(dve):
                step = steps["dve"]
                flat = lambda a: a.rearrange("p h t -> p (h t)")
                step(dve.scalar_tensor_tensor(flat(o_sum), flat(o_sum), vec(f"gla_norm{l}"), ginv, ALU.mult, ALU.mult))
                dve.tensor_tensor(y_gla, y_gla, o_sum, ALU.mult)
            groot, ginv = region(work, free_at + 4 * TQ, 4 * TQ), region(work, free_at + 8 * TQ, 4 * TQ)
            sums([([sq[:, hd, :]], TQ, P) for hd in range(4)], groot, ginv, after=gla_after)
            fill(l, 3, 6)

            room = Room(work)
            ys_at = room.at
            room(3, 4, TQ)
            hi_at0 = room.at
            room(3, 4, TQ)
            parts = [Pair(region(work_r, hi_at0 + b * 4 * TQ, 4, TQ), region(work_r, ys_at + b * 4 * TQ, 4, TQ)) for b in range(3)]
            merged_at = room.at
            merged, merged_hi_at = room(KD, TQ), room.at
            room(KD, TQ)
            sig, tmp = room(4, TQ), room(TQ)
            merged_split = Pair(region(work_r, merged_hi_at, KD, TQ), region(work_r, merged_at, KD, TQ))
            merge(f"merge{l}", plan[f"merge{l}"], list(zip([y_mla, y_pool, y_gla], parts)), h_split, merged, merged_split, TQ,
                  sig, tmp, loaded=32 if l == 0 else None, aside=s5_tables() if l == DEPTH - 1 else ({}, {}))
            last = l == DEPTH - 1
            at = 0 if l == 0 else room.at
            o, inverse_o = residual(f"out{l}", plan[f"out{l}"], [merged_split[:, k, :] for k in range(KD)], TQ,
                                    [(t0, n, lambda m, c=c: posts[l][:, m, c:c + 1]) for t0, n, c in spans if t0 < TQ], at)
            stages.append(norm(TQ, xT[:, :, 0:TQ], h2 if last else hT, h2_split if last else h_split,
                               scaled_by(vec("mix_pre")) if last else modulated_by(l + 1, spans),
                               0 if last else at + 2 * KD * TQ + 2 * TQ, add=(o, inverse_o)))

        def gla_direction(l, tag, d, TQ, gq, gk, gv, log_a, summed, e_pos, e_neg, q_pad, k_dec, k_tok, attn, state,
                          states, o_sum):
            visits = [4, 5, 6, 7, 0, 1, 2, 3] if d == 0 else list(range(NCH - 1, -1, -1))
            by_chunk = summed[:, 2 * d:2 * d + 2, :].rearrange("p a (c t) -> p (a c) t", t=CH)
            two = lambda a: a.rearrange("p (a c) o -> p a (c o)", a=2)
            mid, end = by_chunk[:, :, CH // 2 - 1:CH // 2], by_chunk[:, :, CH - 1:CH]
            mid2, end2 = two(mid), two(end)
            e = e_pos.rearrange("p a (c t) -> p (a c) t", t=CH)
            la = log_a[:, 2 * d:2 * d + 2, :]
            lim = GLA_LIMIT * GLA_TAU
            e_ready, e_done = sem(f"gla_e_ready{tag}"), sem(f"gla_e_done{tag}")

            def exp_vector(dve):
                step = steps["dve"]
                if d == 0:
                    step(dve.tensor_tensor(e, by_chunk, mid.to_broadcast([P, 2 * NCH, CH]), ALU.subtract))
                else:
                    step(dve.tensor_tensor(e, mid.to_broadcast([P, 2 * NCH, CH]), by_chunk, ALU.subtract))
                    step(dve.tensor_tensor(e_pos, e_pos, la, ALU.add))
                step(dve.tensor_scalar(e_pos, e_pos, -lim, lim, ALU.max, ALU.min))
                dve.memset(alpha_arg, 0.0)
                step(dve.tensor_tensor(tail, end2, mid2, ALU.subtract))
                if d == 0:
                    dve.tensor_tensor(alpha_arg[:, :, 4:7], tail[:, :, 4:7], mid2[:, :, 5:8], ALU.add)
                    dve.tensor_tensor(alpha_arg[:, :, 7:8], tail[:, :, 7:8], mid2[:, :, 0:1], ALU.add)
                    ins = dve.tensor_tensor(alpha_arg[:, :, 0:3], tail[:, :, 0:3], mid2[:, :, 1:4], ALU.add)
                else:
                    ins = dve.tensor_tensor(alpha_arg[:, :, 1:8], mid2[:, :, 1:8], tail[:, :, 0:7], ALU.add)
                ins.then_inc(e_ready, 1)
                dve.wait_ge(e_done, 1)
                for j in range(2):
                    r = slice(64 * j, 64 * j + 64)
                    dve.tensor_tensor(q_pad[r, :, j, :], gq[r, :, :], e_neg[r, :, 0:TQ], ALU.mult)
                dve.tensor_tensor(k_dec, gk, e_pos, ALU.mult)

            def exp_scalar(act):
                act.wait_ge(e_ready, 1)
                act.activation(alpha, alpha_arg, ACT.Exp, scale=1.0 / GLA_TAU)
                steps["act"](act.activation(e_neg, e_pos, ACT.Exp, scale=1.0 / GLA_TAU))
                act.activation(e_pos, e_pos, ACT.Exp, scale=-1.0 / GLA_TAU).then_inc(e_done, 1)

            def exp_gpsimd(pool):
                if d:
                    pool.memset(attn, 0.0)
                else:
                    steps["pool"](pool.memset(attn, 0.0))
                    steps["pool"](pool.memset(q_pad[0:64, :, 1, :], 0.0))
                    pool.memset(q_pad[64:P, :, 0, :], 0.0)
            stages.append(Stage(None, exp_scalar, exp_vector, exp_gpsimd))
            fill(l, 1 + d, 2 + d)

            nt = TQ // P
            k_turned, s_filled = sem(f"gla_k_turned{tag}"), sem(f"gla_s_filled{tag}")

            def intra_tensor(pe):
                for tt in range(4):
                    for pair in range(2):
                        c0 = (tt % 2) * 256 + pair * P
                        mm = pe.transpose(ps[:, tt // 2, c0:c0 + P], k_dec[:, pair, tt * P:(tt + 1) * P], const("ident"))
                    if tt % 2:
                        mm.then_inc(k_turned, 1)
                for hd in range(4):
                    for tt in range(nt):
                        t = slice(tt * P, (tt + 1) * P)
                        blocks.product(pe, ps[:, 2 + hd, t], k_dec[:, hd // 2, t], q_pad[:, hd // 2, hd % 2, t],
                                       True, True, s_filled if tt == nt - 1 else None)

            def intra_scalar(act):
                for b in range(2):
                    act.wait_ge(k_turned, b + 1)
                    act.activation(k_tok[:, 2 * b:2 * b + 2, :], ps[:, b, :].rearrange("p (t n) -> p t n", n=256), ACT.Copy)

            def intra_vector(dve):
                mask = each(const("upto" if d == 0 else "since").bitcast(U32), nt)
                for hd in range(4):
                    dve.wait_ge(s_filled, hd + 1)
                    dve.copy_predicated(attn[:, hd, :, :], mask, ps[:, 2 + hd, 0:TQ].rearrange("p (t n) -> p t n", n=P))
            stages.append(Stage(intra_tensor, intra_scalar, intra_vector, None))

            kv_filled, kv_taken = sem(f"gla_kv_filled{tag}"), sem(f"gla_kv_taken{tag}")
            carried = sem(f"gla_carried{tag}")

            def state_tensor(pe):
                n = 0
                for c in visits[:-1]:
                    r, tt = slice(CH * (c % 2), CH * (c % 2) + CH), c // 2
                    for pair in range(2):
                        if n >= 8:
                            pe.wait_ge(kv_taken, n - 7)
                        blocks.product(pe, ps[:, n % 8, 0:256], k_tok[r, tt, pair * P:(pair + 1) * P],
                                       gv[r, tt, pair * 256:(pair + 1) * 256], True, True, kv_filled)
                        n += 1

            def state_vector(dve):
                n = 0
                for i, c in enumerate(visits[:-1]):
                    for pair in range(2):
                        dve.wait_ge(kv_filled, n + 1)
                        if n >= 4:
                            dve.wait_ge(carried, n - 3)
                        if n >= 2:
                            dve.wait_ge(kv_taken, n - 1)
                        for j in range(2):
                            r = slice(64 * j, 64 * j + 64)
                            kv = ps[r, n % 8, j * P:(j + 1) * P]
                            if i == 0:
                                ins = dve.tensor_copy(state[r, 0, pair, :], kv)
                            else:
                                a = alpha[r, pair, visits[i - 1]:visits[i - 1] + 1]
                                ins = dve.scalar_tensor_tensor(state[r, i % 2, pair, :], state[r, 1 - i % 2, pair, :], a, kv,
                                                               ALU.mult, ALU.add)
                        ins.then_inc(kv_taken, 1)
                        n += 1

            def state_scalar(act):
                n = 0
                for i, c in enumerate(visits[:-1]):
                    for pair in range(2):
                        act.wait_ge(kv_taken, n + 1)
                        act.activation(states[:, pair, visits[i + 1], :], state[:, i % 2, pair, :], ACT.Copy,
                                       scale=alpha[:, pair, c:c + 1]).then_inc(carried, 1)
                        n += 1
            stages.append(Stage(state_tensor, state_scalar, state_vector, None))

            tiles = []
            for hd in range(4):
                products = []
                for tt in range(nt):
                    products.append((gv[:, tt, hd * P:(hd + 1) * P], attn[:, hd, tt, :], P, tt * P, P, True, False))
                    for c in (2 * tt, 2 * tt + 1):
                        if c != visits[0]:
                            products.append((states[:, hd // 2, c, :], q_pad[:, hd // 2, hd % 2, c * CH:(c + 1) * CH], P,
                                             c * CH, CH, False, False))
                    products[-1] = products[-1][:-1] + (True,)
                if d == 0:
                    tiles.append(Tile(products, copied(o_sum[:, hd, :], TQ)))
                else:
                    tiles.append(Tile(products, None, lambda dve, b, hd=hd: dve.tensor_tensor(
                        o_sum[:, hd, :], o_sum[:, hd, :], b[:, 0:TQ], ALU.add)))
            projection(f"gla_o{tag}", tiles)

        def fill(l, n0, n1):
            if l + 1 < DEPTH:
                fuse(modulation(l + 1, range(n0, n1)))

        h2 = region(h_sb, 0, KD, SEQ)
        h2_split = Pair(region(h_sb_r, KD * SEQ, KD, SEQ), region(h_sb_r, 0, KD, SEQ))

        T = SEQ
        x_1 = region(work, 0, S5T, T)
        raw_at = S5T * T
        s5_room = Room(work, raw_at + 14 * (T + 1))
        x_2, x_3, cc_re, cc_im = s5_room(S5T, T), s5_room(S5T, T), s5_room(S5T, 32), s5_room(S5T, 32)
        s5_room.at = WORK - 2 * S5T * T
        sin_t, cos_t = s5_room(S5T, T), s5_room(S5T, T)
        x_4 = region(hi_sb, 0, S5T, T)
        of_context = x_sb[:, :].rearrange("p (k s t) -> p k s t", s=2, t=T)[:, :, 1, :]
        one = Room(small, 420)
        dt, mag, th, turn, f_hi, f_lo, c_re, c_im, s_r, c_r = [one(S5T) for _ in range(10)]
        two_pi = 2.0 * float(np.pi)
        pi_a = 6.28125
        pi_b = float(np.float32(round((two_pi - pi_a) * 2 ** 20) / 2 ** 20))
        pi_c = float(np.float32(two_pi - pi_a - pi_b))
        whole = 1.5 * 2 ** 23
        half_pi = 3.1415925 / 2
        full = 6.283185

        dt_done, arg_ready, arg_done = sem("dt_done"), sem("arg_ready"), sem("arg_done")
        half_col = region(small, 4, 1)

        g_turns = sem("g_turns")

        def s5_tables():
            def step_size(act):
                act.activation(dt, vec("log_step"), ACT.Exp).then_inc(dt_done, 1)

            def angles(dve):
                step = steps["dve"]
                dve.memset(half_col, half_pi)
                dve.wait_ge(dt_done, 1)
                step(dve.tensor_tensor(mag, vec("a_re"), dt, ALU.mult))
                step(dve.tensor_tensor(th, vec("a_im"), dt, ALU.mult))
                step(dve.tensor_scalar(turn, th, 1.0 / two_pi, None, ALU.mult))
                step(dve.tensor_scalar(turn, turn, whole, None, ALU.add))
                step(dve.tensor_scalar(turn, turn, -whole, None, ALU.add))
                for c in (pi_a, pi_b, pi_c):
                    step(dve.scalar_tensor_tensor(th, turn, -c, th, ALU.mult, ALU.add))
                step(dve.tensor_scalar(th, th, -3.1415925, 3.1415925, ALU.max, ALU.min))
                step(dve.tensor_scalar(turn, th, 1.0 / two_pi, None, ALU.mult))
                step(dve.tensor_scalar(f_hi, turn, 1.5 * 2 ** 11, None, ALU.add))
                step(dve.tensor_scalar(f_hi, f_hi, -1.5 * 2 ** 11, None, ALU.add))
                dve.tensor_tensor(f_lo, turn, f_hi, ALU.subtract).then_inc(arg_ready, 1)

            def polar(act):
                act.wait_ge(arg_ready, 1)
                act.activation(mag, mag, ACT.Exp)
                act.activation(s_r, th, ACT.Sin)
                steps["act"](act.activation(c_r, th, ACT.Abs))
                act.activation(c_r, c_r, ACT.Sin, bias=half_col, scale=-1.0).then_inc(arg_done, 1)

            def factors(dve):
                step = steps["dve"]
                dve.wait_ge(arg_done, 1)
                re, im, den = dt, th, turn
                step(dve.tensor_tensor(s_r, s_r, mag, ALU.mult))
                step(dve.tensor_tensor(c_r, c_r, mag, ALU.mult))
                step(dve.tensor_scalar(c_r, c_r, -1.0, None, ALU.add))
                step(dve.tensor_tensor(den, vec("a_re"), vec("a_re"), ALU.mult))
                step(dve.tensor_tensor(re, vec("a_im"), vec("a_im"), ALU.mult))
                step(dve.tensor_tensor(den, den, re, ALU.add))
                step(dve.reciprocal(den, den))
                step(dve.tensor_tensor(re, c_r, vec("a_re"), ALU.mult))
                step(dve.tensor_tensor(im, s_r, vec("a_im"), ALU.mult))
                step(dve.tensor_tensor(re, re, im, ALU.add))
                step(dve.tensor_tensor(c_re, re, den, ALU.mult))
                step(dve.tensor_tensor(re, s_r, vec("a_re"), ALU.mult))
                step(dve.tensor_tensor(im, c_r, vec("a_im"), ALU.mult))
                step(dve.tensor_tensor(re, re, im, ALU.subtract))
                step(dve.tensor_tensor(c_im, re, den, ALU.mult))

            t, turns, tmp = each(const("step"), S5T), sin_t, cos_t
            table_steps = [
                lambda dve: dve.tensor_tensor(turns, wide(f_hi, T), t, ALU.mult),
                lambda dve: dve.tensor_scalar(tmp, turns, whole, None, ALU.add),
                lambda dve: dve.tensor_scalar(tmp, tmp, -whole, None, ALU.add),
                lambda dve: dve.tensor_tensor(turns, turns, tmp, ALU.subtract),
                lambda dve: dve.tensor_tensor(tmp, wide(f_lo, T), t, ALU.mult),
                lambda dve: dve.tensor_tensor(turns, turns, tmp, ALU.add),
                lambda dve: dve.tensor_scalar(tmp, turns, whole, None, ALU.add),
                lambda dve: dve.tensor_scalar(tmp, tmp, -whole, None, ALU.add)]

            def last_turns(dve):
                dve.tensor_tensor(turns, turns, tmp, ALU.subtract).then_inc(g_turns, 1)

            def magnitudes(act):
                act.wait_ge(g_turns, 1)
                steps["act"](act.activation(cos_t, turns, ACT.Abs))

            def sines(act):
                act.activation(sin_t, turns, ACT.Sin, scale=full)

            def cosines(act):
                act.activation(cos_t, cos_t, ACT.Sin, bias=half_col, scale=-full)
            on_vector = {1: angles, 6: factors, 7 + len(table_steps): last_turns}
            for n, f in enumerate(table_steps):
                on_vector[7 + n] = lambda dve, f=f: steps["dve"](f(dve))
            return {0: step_size, 4: polar, 17: magnitudes, 19: sines, 21: cosines}, on_vector

        for l in range(DEPTH):
            trunk(l)

        NC = T // CH
        PC = 4 * NC
        xS = xT[:, :, 0:T]
        hk = [h2_split[:, k, :] for k in range(KD)]
        spare = Room(hi_sb)

        mixed_p = region(work, 0, 14, T)

        u_t = of_context[:, 0:4, :]
        projection("s5_in", [Tile(chain(plan["s5_in"] + KD * m, hk, T), copied(u_t[:, m, :], T)) for m in range(4)])

        tiles = []
        for name, dst in (("s5_b_re_2", x_1), ("s5_b_im_2", x_2)):
            for n in range(S5T // 2):
                products = [((plan[name] + i,), u_t[:, i // 4, :], P, (i % 2) * T, T, True, True) for i in (2 * n, 2 * n + 1)]
                d2 = dst[:, 2 * n:2 * n + 2, :].rearrange("p a t -> p (a t)")
                tiles.append(Tile(products, copied(d2, 2 * T)) if n % 2 else Tile(products, None, copied_dve(d2, 2 * T)))
        def c_factors(dve):
            step = steps["dve"]
            w = lambda v: wide(v, 32)
            cv = lambda n: vec(n).rearrange("p (i c) -> p i c", c=32)
            cc_tmp = region(work, raw_at + 14 * (T + 1) + S5T * T, S5T, 32)
            dve.tensor_tensor(cc_re, cv("c_re"), w(c_re), ALU.mult)
            step(dve.tensor_tensor(cc_tmp, cv("c_im"), w(c_im), ALU.mult))
            step(dve.tensor_tensor(cc_re, cc_re, cc_tmp, ALU.subtract))
            dve.tensor_tensor(cc_im, cv("c_re"), w(c_im), ALU.mult)
            step(dve.tensor_tensor(cc_tmp, cv("c_im"), w(c_re), ALU.mult))
            step(dve.scalar_tensor_tensor(cc_im, cc_im, -1.0, cc_tmp, ALU.mult, ALU.subtract))
        projection("s5_bu", tiles, first=c_factors)

        SPLIT = 11
        own = {"dve": slice(0, SPLIT), "pool": slice(SPLIT, S5T), "all": slice(0, S5T)}

        def into_frame(eng):
            step, i = steps["dve"], own["all"]
            tt = lambda o, a, b, op: eng.tensor_tensor(o[:, i, :], a[:, i, :], b[:, i, :], op)
            step(tt(x_3, cos_t, x_1, ALU.mult))
            step(tt(x_4, sin_t, x_2, ALU.mult))
            step(tt(x_3, x_3, x_4, ALU.add))
            step(tt(x_4, cos_t, x_2, ALU.mult))
            step(tt(x_1, sin_t, x_1, ALU.mult))
            return tt(x_4, x_4, x_1, ALU.subtract)

        def out_of_frame(eng, who):
            step, i = steps[who], own[who]
            tt = lambda o, a, b, op: eng.tensor_tensor(o[:, i, :], a[:, i, :], b[:, i, :], op)
            step(tt(x_3, cos_t, x_1, ALU.mult))
            step(tt(x_4, sin_t, x_2, ALU.mult))
            step(tt(x_3, x_3, x_4, ALU.subtract))
            step(tt(x_4, sin_t, x_1, ALU.mult))
            step(tt(x_2, cos_t, x_2, ALU.mult))
            tt(x_4, x_4, x_2, ALU.add)

        def frame_vector(dve):
            steps["dve"](into_frame(dve))
            for i in range(S5T):
                for dst, src in ((x_1, x_3), (x_2, x_4)):
                    dve.tensor_tensor_scan(dst[:, i, :], mag[:, i:i + 1].to_broadcast([P, T]), src[:, i, :], 0.0,
                                           ALU.mult, ALU.add)

        raw = region(work, raw_at, 14, T + 1)
        tiles = [Tile(chain(plan["rw_in"] + KD * m, hk, T), copied(raw[:, m, 1:T + 1], T)) for m in range(14)]
        projection("rw_in", tiles, first=lambda dve: dve.memset(raw[:, :, 0:1], 0.0), then=frame_vector)

        stages.append(Stage(None, None, lambda dve: out_of_frame(dve, "dve"), lambda pool: out_of_frame(pool, "pool")))

        wide_at = raw_at + 14 * (T + 1)
        wide_re, wide_im = region(work, wide_at, S5T, P), region(work, wide_at + S5T * P, S5T, P)
        cleared = sem("c_cleared")

        def c_gpsimd(pool):
            steps["pool"](pool.memset(wide_re, 0.0))
            pool.memset(wide_im, 0.0).then_inc(cleared, 1)

        def c_vector(dve):
            dve.wait_ge(cleared, 1)
            quads = lambda a: a.rearrange("p (q i) c -> p q i c", i=4)
            for i in range(4):
                for dst, src in ((wide_re, cc_re), (wide_im, cc_im)):
                    dve.tensor_copy(quads(dst)[:, :, i, 32 * i:32 * i + 32], quads(src)[:, :, i, :])
        stages.append(Stage(None, None, c_vector, c_gpsimd))

        yroom = Room(work, WORK - 2 * S5T * T)
        y_pre, y_sig, y_gelu = yroom(4, T), yroom(4, T), yroom(4, T)
        y_s5 = region(vec_sb, vec_at["c_re"][0], 4, T)
        tiles = []
        for q in range(4):
            products = []
            for i in range(4 * q, 4 * q + 4):
                products.append((wide_re[:, i, :], x_3[:, i, :], P, 0, T, i == 4 * q, False))
                products.append((wide_im[:, i, :], x_4[:, i, :], P, 0, T, False, i == 4 * q + 3))
            tiles.append(Tile(products, None, lambda dve, b, q=q: dve.scalar_tensor_tensor(
                y_pre[:, q, :], u_t[:, q, :], vec("s5_d")[:, q:q + 1], b[:, 0:T], ALU.mult, ALU.add)))
        projection("s5_y", tiles)
        s5_y = stages.pop()

        shifted = sem("shifted")
        ranks = of_context[:, 4, :]

        def shift_vector(dve):
            step = steps["dve"]
            step(dve.tensor_tensor(mixed_p, raw[:, :, 0:T], raw[:, :, 1:T + 1], ALU.subtract))
            for m in range(13, -1, -1):
                ins = dve.scalar_tensor_tensor(mixed_p[:, m, :], mixed_p[:, m, :], vec("mu")[:, m:m + 1], raw[:, m, 1:T + 1],
                                               ALU.mult, ALU.add)
                if m == 12:
                    ins.then_inc(shifted, 1)

        def shift_scalar(act):
            act.wait_ge(shifted, 1)
            act.activation(ranks[0:64, :], mixed_p[0:64, 12, :], ACT.Tanh)
            act.activation(ranks[64:P, :], mixed_p[64:P, 12, :], ACT.Copy)
            act.activation(mixed_p[:, 13, :], mixed_p[:, 13, :], ACT.Sigmoid)
        stages.append(Stage(None, shift_scalar, shift_vector, None))
        fuse(s5_y)
        stages.append(Stage(None, lambda act: act.activation(y_gelu, y_pre, ACT.Gelu_apprx_tanh), None, None))
        projection("s5_glu", [Tile(chain(plan["s5_glu"] + 4 * m, [y_gelu[:, k, :] for k in range(4)], T),
                                   copied(y_sig[:, m, :], T, ACT.Sigmoid, bias=vec("b_glu")[:, m:m + 1])) for m in range(4)])
        stages.append(Stage(None, None, lambda dve: dve.tensor_tensor(y_s5, y_gelu, y_sig, ALU.mult), None))


        room = Room(work)
        room(14, T)
        r_t, k_t, v_t = mixed_p[:, 0:4, :], mixed_p[:, 4:8, :], mixed_p[:, 8:12, :]
        g_t, bonus, y_rw = room(4, T), room(4, T), room(4, T)
        r_pad, a_pad, k_pad, b_pad = [room(PC, 2, CH) for _ in range(4)]
        temp_at = room.at
        flat = lambda a: a.rearrange("p a t -> p (a t)")

        def clear_operands(pool):
            step = steps["pool"]
            for a in (r_pad, a_pad, k_pad, b_pad):
                step(pool.memset(a[0:64, :, 1, :], 0.0))
                step(pool.memset(a[64:P, :, 0, :], 0.0))


        room = Room(work, temp_at)
        lw, a_t, kk, k2, b_t, e_t, ex_t, tmp, root, inv = [room(4, T) for _ in range(10)]
        e1, e2, e3 = [spare(4, T) for _ in range(3)]
        tiles = []
        for m in range(4):
            tiles.append(Tile(chain(plan["rw_w"] + m, [ranks], T), copied(lw[:, m, :], T, ACT.Sigmoid, bias=vec("w0")[:, m:m + 1])))
        for m in range(4):
            tiles.append(Tile(chain(plan["rw_w"] + 4 + m, [ranks], T), copied(a_t[:, m, :], T, ACT.Sigmoid, bias=vec("a0")[:, m:m + 1])))
        for m in range(4):
            tiles.append(Tile(chain(plan["rw_w"] + 8 + m, [mixed_p[:, 13, :]], T), None, copied_dve(g_t[:, m, :], T)))
        projection("rw_w", tiles)
        fuse(Stage(None, None, None, clear_operands))

        def keys_vector(dve):
            step = steps["dve"]
            step(dve.tensor_scalar(lw, lw, -float(np.exp(-0.5)), None, ALU.mult))
            step(dve.tensor_tensor(kk, k_t, wide(vec("k_k"), T), ALU.mult))
            dve.tensor_tensor(tmp, kk, kk, ALU.mult)
            for m in range(4):
                dve.tensor_tensor_scan(e_t[:, m, :], const("carry")[:, 0:T], lw[:, m, :], 0.0, ALU.mult, ALU.add)
        stages.append(Stage(None, None, keys_vector, None))

        kk_sum, kk_root = sem("kk_sum"), sem("kk_root")

        def kk_tensor(pe):
            for m in range(4):
                blocks.product(pe, ps[:, m // 2, (m % 2) * T:(m % 2 + 1) * T], const("head_ones"), tmp[:, m, :], True, True,
                               kk_sum if m == 3 else None)

        def kk_scalar(act):
            act.wait_ge(kk_sum, 1)
            act.activation(flat(root), ps[:, 0:2, :].rearrange("p a t -> p (a t)"), ACT.Sqrt).then_inc(kk_root, 1)

        def kk_vector(dve):
            step = steps["dve"]
            step(dve.scalar_tensor_tensor(k2, a_t, -1.0, wide(vec("k_a"), T), ALU.add, ALU.mult))
            step(dve.scalar_tensor_tensor(k2, k2, 1.0, k_t, ALU.add, ALU.mult))
            dve.wait_ge(kk_root, 1)
            step(dve.tensor_scalar(root, root, 1e-12, None, ALU.max))
            step(dve.reciprocal(flat(inv), flat(root)))
            step(dve.tensor_tensor(kk, kk, inv, ALU.mult))
            dve.tensor_tensor(b_t, kk, a_t, ALU.mult)
            step(dve.tensor_tensor(bonus, r_t, k2, ALU.mult))
            dve.tensor_tensor(bonus, bonus, wide(vec("r_k"), T), ALU.mult)
        stages.append(Stage(kk_tensor, kk_scalar, kk_vector, None))

        by_chunk = lambda a: a.rearrange("p a (c t) -> p (a c) t", t=CH)
        carry = region(small, 320, 4, NC)
        carry_arg = region(small, 340, 4, NC)
        ends = region(small, 360, 4, NC)
        rel_ready, rel_done = sem("rel_ready"), sem("rel_done")
        bonus_summed = sem("bonus_summed")

        def rel_tensor(pe):
            for m in range(4):
                blocks.product(pe, ps[:, 2 + m // 2, (m % 2) * T:(m % 2 + 1) * T], const("head_ones"), bonus[:, m, :], True,
                               True, bonus_summed if m == 3 else None)

        def rel_vector(dve):
            step = steps["dve"]
            c = by_chunk(e_t)
            mid, end = c[:, :, CH // 2 - 1:CH // 2], c[:, :, CH - 1:CH]
            four = lambda a: a.rearrange("p (a c) o -> p a (c o)", a=4)
            dve.memset(carry_arg, 0.0)
            step(dve.tensor_tensor(ends, four(end), four(mid), ALU.subtract))
            step(dve.tensor_tensor(carry_arg[:, :, 0:NC - 1], ends[:, :, 0:NC - 1], four(mid)[:, :, 1:NC], ALU.add))
            step(dve.tensor_tensor(by_chunk(tmp), c, mid.to_broadcast([P, PC, CH]), ALU.subtract))
            dve.tensor_tensor(ex_t, tmp, lw, ALU.subtract).then_inc(rel_ready, 1)
            dve.wait_ge(bonus_summed, 1)
            dve.tensor_tensor(flat(bonus), ps[:, 2:4, :].rearrange("p a t -> p (a t)"), flat(v_t), ALU.mult)
            dve.wait_ge(rel_done, 1)
            for j in range(2):
                r = slice(64 * j, 64 * j + 64)
                dve.tensor_tensor(r_pad[r, :, j, :], by_chunk(r_t)[r], by_chunk(e1)[r], ALU.mult)
                dve.scalar_tensor_tensor(a_pad[r, :, j, :], by_chunk(kk)[r], -1.0, by_chunk(e2)[r], ALU.mult, ALU.mult)
                dve.tensor_tensor(k_pad[r, :, j, :], by_chunk(k2)[r], by_chunk(e3)[r], ALU.mult)
                dve.tensor_tensor(b_pad[r, :, j, :], by_chunk(b_t)[r], by_chunk(e3)[r], ALU.mult)

        def rel_scalar(act):
            act.wait_ge(rel_ready, 1)
            act.activation(carry, carry_arg, ACT.Exp)
            act.activation(e1, tmp, ACT.Exp)
            act.activation(e2, ex_t, ACT.Exp)
            act.activation(e3, tmp, ACT.Exp, scale=-1.0).then_inc(rel_done, 1)
        stages.append(Stage(rel_tensor, rel_scalar, rel_vector, None))

        room = Room(work, temp_at)
        ab, inv_m, inv_t, mid_m, level = [room(PC, P) for _ in range(5)]
        ak = of_context
        ak_of = lambda i: ak[:, i // 2, (i % 2) * P:(i % 2 + 1) * P]
        rb = region(work, 0, PC, P)
        rk = region(hi_sb, 0, PC, P)
        pads = lambda a, i: a[:, i, :, :].rearrange("p h t -> p (h t)")

        def block_tiles(lhs, rhs, vector=None, scalar=None):
            tiles = []
            for g in range(PC // 4):
                products = [(lhs(4 * g + i), rhs(4 * g + i), P, i * P, P, True, True) for i in range(4)]
                tiles.append(Tile(products, None if scalar is None else scalar(slice(4 * g, 4 * g + 4)),
                                  None if vector is None else vector(slice(4 * g, 4 * g + 4))))
            return tiles

        bank4 = lambda b: b.rearrange("p (i t) -> p i t", t=P)

        def masked(dst, mask):
            return lambda g: lambda dve, b: dve.tensor_tensor(dst[:, g, :], bank4(b), each(const(mask), 4), ALU.mult)

        def masked_ak(g):
            def vector(dve, b):
                for i in range(g.start, g.stop, 2):
                    ins = dve.tensor_tensor(ak[:, i // 2, :].rearrange("p (i t) -> p i t", t=P), bank4(b)[:, i - g.start:i - g.start + 2, :],
                                            each(const("before"), 2), ALU.mult)
                return ins
            return vector

        def to(dst):
            return lambda g: lambda act, b: act.activation(dst[:, g, :], bank4(b), ACT.Copy)

        def added(dst):
            return lambda g: lambda dve, b: dve.tensor_tensor(dst[:, g, :], dst[:, g, :], bank4(b), ALU.add)

        tiles = block_tiles(lambda i: pads(b_pad, i), lambda i: pads(a_pad, i), masked(ab, "before"))
        tiles += block_tiles(lambda i: pads(a_pad, i), lambda i: pads(b_pad, i), masked(inv_m, "level1_turned"))
        tiles += block_tiles(lambda i: pads(k_pad, i), lambda i: pads(a_pad, i), masked_ak)
        tiles += block_tiles(lambda i: pads(b_pad, i), lambda i: pads(r_pad, i), masked(rb, "upto"))
        tiles += block_tiles(lambda i: pads(k_pad, i), lambda i: pads(r_pad, i), masked(rk, "upto"))
        projection("rw_chunks", tiles)

        def unit_vector(dve):
            step = steps["dve"]
            step(dve.tensor_tensor(inv_t, ab, each(const("level1"), PC), ALU.mult))
            dve.tensor_tensor(inv_t, inv_t, each(const("ident"), PC), ALU.add)

        def level_scalar(b):
            def gpsimd(pool):
                pool.tensor_tensor(level, ab, each(const(f"level{b}"), PC), ALU.mult)
            return gpsimd

        def unit_pool(pool):
            steps["pool"](pool.tensor_tensor(inv_m, inv_m, each(const("ident"), PC), ALU.add))
            level_scalar(2)(pool)
        stages.append(Stage(None, None, unit_vector, unit_pool))
        for b in range(2, 7):
            projection(f"rw_join{b}", block_tiles(lambda i: level[:, i, :], lambda i: inv_m[:, i, :], scalar=to(mid_m)))
            t_tiles = block_tiles(lambda i: mid_m[:, i, :], lambda i: inv_t[:, i, :], added(inv_t))
            m_tiles = block_tiles(lambda i: inv_t[:, i, :], lambda i: mid_m[:, i, :], added(inv_m))
            tiles = []
            for g in range(PC // 4):
                tiles += [m_tiles[g], t_tiles[g]] if b < 6 else [t_tiles[g]]
            level_update(f"rw_inv{b}", tiles, 2 if b < 6 else 1, level_scalar(b + 1) if b < 6 else None)

        room = Room(work, temp_at)
        ab_, k_tok, inv_t_, b_tok, v_low = [room(PC, P) for _ in range(5)]
        v_pad = ab
        v_tok = region(work, temp_at + 4 * PC * P, PC, CH)
        scratch = Room(work, temp_at + 4 * PC * P + PC * CH)
        w_s, u_s, g_s, h_s = scratch(4, CH), scratch(2, 4, CH), scratch(4, CH), region(hi_sb, 3 * 4 * T, 4, CH)
        y_s = region(hi_sb, PC * P, PC, CH)

        def v_pad_gpsimd(pool):
            steps["pool"](pool.memset(v_pad[0:64, :, 64:P], 0.0))
            pool.memset(v_pad[64:P, :, 0:64], 0.0)

        def v_pad_vector(dve):
            for j in range(2):
                r = slice(64 * j, 64 * j + 64)
                dve.tensor_copy(v_pad[r, :, 64 * j:64 * j + 64], by_chunk(v_t)[r])
        k_turned = sem("k_turned")
        k_took = [sem("k_act_took"), sem("k_dve_took")]

        def turn_tensor(pe):
            for n in range(8):
                src = (k_pad, b_pad)[n // 4]
                for i in range(4):
                    mm = pe.transpose(ps[:, n, i * P:(i + 1) * P], pads(src, 4 * (n % 4) + i), const("ident"))
                mm.then_inc(k_turned, 1)

        def turn_scalar(act):
            for n in range(4):
                act.wait_ge(k_turned, n + 1)
                act.activation(k_tok[:, 4 * n:4 * n + 4, :], bank4(ps[:, n, :]), ACT.Copy)

        def turn_vector(dve):
            v_pad_vector(dve)
            for n in range(4):
                dve.wait_ge(k_turned, n + 5)
                dve.tensor_copy(b_tok[:, 4 * n:4 * n + 4, :], bank4(ps[:, 4 + n, :]))
        stages.append(Stage(turn_tensor, turn_scalar, turn_vector, v_pad_gpsimd))

        tiles = []
        for g in range(2):
            tiles.append(Tile([(v_pad[:, 8 * g + i, :], const("ident2"), P, i * CH, CH, True, True) for i in range(8)], None,
                              lambda dve, b, g=g: dve.tensor_copy(v_tok[:, 8 * g:8 * g + 8, :],
                                                                  b.rearrange("p (i t) -> p i t", t=CH))))
        projection("rw_values", tiles)

        at_chunk = lambda a, c: a.rearrange("p (a c) t -> p a c t", c=NC)[:, :, c, :]
        bank_of = lambda n: ps[:, n, 0:4 * CH].rearrange("p (a t) -> p a t", t=CH)
        w_filled, w_taken, u_filled, u_taken = sem("w_filled"), sem("w_taken"), sem("u_filled"), sem("u_taken")
        h_filled, g_ready, y_filled, y_taken = sem("h_filled"), sem("g_ready"), sem("y_filled"), sem("y_taken")

        def seq_tensor(pe):
            for c in range(NC):
                o = lambda n, a: ps[:, n, a * CH:(a + 1) * CH]
                if c:
                    pe.wait_ge(w_taken, c)
                    pe.wait_ge(g_ready, c)
                for a in range(4):
                    i = a * NC + c
                    blocks.product(pe, o(0, a), ak_of(i), v_tok[:, i, :], True, c == 0,
                                   w_filled if c == 0 and a == 3 else None)
                    if c:
                        blocks.product(pe, o(0, a), pads(a_pad, i), g_s[:, a, :], False, True, w_filled if a == 3 else None)
                pe.wait_ge(w_taken, c + 1)
                if c:
                    pe.wait_ge(u_taken, c)
                for a in range(4):
                    blocks.product(pe, o(1, a), inv_t[:, a * NC + c, :], w_s[:, a, :], True, True, u_filled if a == 3 else None)
                pe.wait_ge(u_taken, c + 1)
                if c < NC - 1:
                    for a in range(4):
                        i = a * NC + c
                        blocks.product(pe, o(2, a), k_tok[:, i, :], v_tok[:, i, :], True, False)
                        blocks.product(pe, o(2, a), b_tok[:, i, :], u_s[:, c % 2, a, :], False, True, h_filled if a == 3 else None)
                if c >= 2:
                    pe.wait_ge(y_taken, c - 1)
                for a in range(4):
                    i = a * NC + c
                    blocks.product(pe, o(3 + c % 2, a), rk[:, i, :], v_tok[:, i, :], True, False)
                    if c:
                        blocks.product(pe, o(3 + c % 2, a), pads(r_pad, i), g_s[:, a, :], False, False)
                    blocks.product(pe, o(3 + c % 2, a), rb[:, i, :], u_s[:, c % 2, a, :], False, True, y_filled if a == 3 else None)

        def seq_vector(dve):
            step = steps["dve"]
            for c in range(NC):
                dve.wait_ge(w_filled, c + 1)
                dve.tensor_copy(w_s, bank_of(0)).then_inc(w_taken, 1)
                if c < NC - 1:
                    dve.wait_ge(h_filled, c + 1)
                    if c == 0:
                        src = bank_of(2)
                    else:
                        step(dve.tensor_tensor(h_s, bank_of(2), g_s, ALU.add))
                        src = h_s
                        dve.wait_ge(y_filled, c + 1)
                    dve.tensor_tensor(g_s, src, wide(carry[:, :, c], CH), ALU.mult).then_inc(g_ready, 1)

        def seq_scalar(act):
            for c in range(NC):
                act.wait_ge(u_filled, c + 1)
                if c >= 2:
                    act.wait_ge(y_filled, c - 1)
                act.activation(u_s[:, c % 2, :, :], bank_of(1), ACT.Copy).then_inc(u_taken, 1)
                act.wait_ge(y_filled, c + 1)
                act.activation(at_chunk(y_s, c), bank_of(3 + c % 2), ACT.Copy).then_inc(y_taken, 1)
        stages.append(Stage(seq_tensor, seq_scalar, seq_vector, None))

        y_bd, y_sq = k_pad.rearrange("p i h t -> p i (h t)"), region(work, temp_at, PC, CH)
        mean, var = region(small, 380, PC), region(small, 400, PC)
        var_ready, var_rooted = sem("var_ready"), sem("var_rooted")

        def norm_gpsimd(pool):
            pool.memset(y_bd, 0.0).then_inc(var_ready, 1)

        def norm_vector(dve):
            step = steps["dve"]
            step(dve.tensor_reduce(mean, y_s, AX.X, ALU.add))
            step(dve.tensor_scalar(mean, mean, 1.0 / CH, None, ALU.mult))
            step(dve.tensor_tensor(y_s, y_s, wide(mean, CH), ALU.subtract))
            step(dve.tensor_tensor(y_sq, y_s, y_s, ALU.mult))
            dve.tensor_reduce(var, y_sq, AX.X, ALU.add).then_inc(var_ready, 1)
            dve.wait_ge(var_rooted, 1)
            step(dve.reciprocal(mean, var))
            for j in range(2):
                r = slice(64 * j, 64 * j + 64)
                dve.tensor_tensor(y_bd[r, :, 64 * j:64 * j + 64], y_s[r], wide(mean[r], CH), ALU.mult)

        def norm_scalar(act):
            act.wait_ge(var_ready, 2)
            act.activation(var, var, ACT.Sqrt, bias=eps_col[:, 1:2], scale=1.0 / CH).then_inc(var_rooted, 1)
        stages.append(Stage(None, norm_scalar, norm_vector, norm_gpsimd))

        def y_out(g):
            def vector(dve, b):
                step = steps["dve"]
                for m in (2 * g, 2 * g + 1):
                    src = b[:, (m % 2) * T:(m % 2 + 1) * T]
                    step(dve.tensor_scalar(y_rw[:, m, :], src, vec("lnx_w")[:, m:m + 1], vec("lnx_b")[:, m:m + 1],
                                           ALU.mult, ALU.add))
                two = slice(2 * g, 2 * g + 2)
                step(dve.tensor_tensor(y_rw[:, two, :], y_rw[:, two, :], bonus[:, two, :], ALU.add))
                return dve.tensor_tensor(y_rw[:, two, :], y_rw[:, two, :], g_t[:, two, :], ALU.mult)
            return vector
        tiles = [Tile([(y_bd[:, 8 * g + i, :], const("ident2"), P, i * CH, CH, True, True) for i in range(8)], None, y_out(g))
                 for g in range(2)]
        projection("rw_y", tiles)

        room = Room(work)
        merged, sig, tmp2 = room(KD, T), room(4, T), room(T)
        merged_split = Pair(region(work_r, room.at, KD, T), region(work_r, 0, KD, T))
        rw_at, hi_at2 = 14 * T + 2 * 4 * T, 14 * T + 3 * 4 * T
        s5_at = hi_at2 + 2 * 4 * T
        parts = [Pair(region(work_r, hi_at2 + b * 4 * T, 4, T), region(work_r, lo, 4, T)) for b, lo in enumerate((rw_at, s5_at))]
        merge("merge2", plan["merge2"], list(zip([y_rw, y_s5], parts)), h2_split, merged, merged_split, T, sig, tmp2,
              bias=vec("b_gate"))
        o2, inverse2 = residual("out2", plan["out2"], [merged_split[:, k, :] for k in range(KD)], T,
                                [(0, T, lambda m: vec("mix_post")[:, m:m + 1])], hi_at2)

        stages.append(norm(T, xS, h2, h2_split, scaled_by(vec("ffn_pre")), 0, add=(o2, inverse2)))
        room = Room(work)
        hidden, hidden_hi_at = room(FT, T), room.at
        room(FT, T)
        hidden_split = Pair(region(work_r, hidden_hi_at, FT, T), region(work_r, 0, FT, T))
        down_at = room.at
        conv = room(2, 2, T)
        gelu = room(2, T)
        up_filled, affine, convolved = sem("up_filled"), sem("affine"), sem("convolved")
        gelud, hidden_done = sem("gelud"), sem("hidden_done")
        tap = lambda j, m: vec("conv_w")[:, j * 2 * FT + m:j * 2 * FT + m + 1]

        def up_tensor(pe):
            for i in range(2 * FT):
                if i >= 8:
                    pe.wait_ge(convolved, i - 7)
                for k in range(KD):
                    blocks.product(pe, ps[:, i % 8, 0:T], blocks.lhs(pe, plan["ff_up"] + KD * i + k), hk[k], k == 0, k == KD - 1,
                                   up_filled if k == KD - 1 else None)
                blocks.mark("up", i)

        def up_scalar(act):
            for j in range(FT):
                for v in range(2):
                    i, m = 2 * j + v, j + v * FT
                    rounding.before(act, "up", i)
                    act.wait_ge(up_filled, i + 1)
                    if j >= 2:
                        act.wait_ge(hidden_done, j - 1)
                    act.activation(conv[:, j % 2, v, :], ps[:, i % 8, 0:T], ACT.Identity, bias=vec("conv_b")[:, m:m + 1],
                                   scale=tap(2, m)).then_inc(affine, 1)
                act.wait_ge(convolved, 2 * j + 1)
                act.activation(gelu[:, j % 2, :], conv[:, j % 2, 0, :], ACT.Gelu_apprx_tanh).then_inc(gelud, 1)

        def up_vector(dve):
            step = steps["dve"]
            for j in range(FT):
                for v in range(2):
                    i, m = 2 * j + v, j + v * FT
                    dve.wait_ge(affine, i + 1)
                    z = conv[:, j % 2, v, :]
                    step(dve.scalar_tensor_tensor(z[:, 1:T], ps[:, i % 8, 0:T - 1], tap(1, m), z[:, 1:T], ALU.mult, ALU.add))
                    dve.scalar_tensor_tensor(z[:, 2:T], ps[:, i % 8, 0:T - 2], tap(0, m), z[:, 2:T], ALU.mult,
                                             ALU.add).then_inc(convolved, 1)
                dve.wait_ge(gelud, j + 1)
                dve.wait_ge(convolved, 2 * j + 2)
                dve.tensor_tensor(hidden[:, j, :], gelu[:, j % 2, :], conv[:, j % 2, 1, :], ALU.mult).then_inc(hidden_done, 1)
                dve.wait_ge(hidden_done, j + 1)
                step(dve.tensor_copy(hidden_split.hi[:, j, :], hidden[:, j, :]))
                dve.tensor_tensor(hidden_split.lo[:, j, :], hidden[:, j, :], hidden_split.hi[:, j, :], ALU.subtract)
        stages.append(Stage(up_tensor, up_scalar, up_vector, None))
        residual("ff_down", plan["ff_down"], [hidden_split[:, j, :] for j in range(FT)], T,
                 [(0, T, lambda m: vec("ffn_post")[:, m:m + 1])], down_at, last_x=xS)

        pool_stages = [n for n, stage in enumerate(stages, 1) if stage.gpsimd is not None]

        def rejoin(eng, n):
            eng.drain().then_inc(stage_done, 1)
            eng.wait_ge(stage_done, 3 * n)
            if n in pool_stages:
                eng.wait_ge(pool_done, pool_stages.index(n) + 1)

        block = ctx.enter_context(nc.Block())

        @block.sync
        def _(sp):
            sp.dma_start(c_sb, c_in.rearrange("p (k c) -> p k c", c=2)).then_inc(c_loaded, 16)
            for i in range(n_panels):
                if i >= SLOTS:
                    sp.wait_ge(panel_used, i - SLOTS + 1)
                n = PANEL * P
                s = i % SLOTS
                sp.dma_start(panels[:, s * n:(s + 1) * n], weights[i]).then_inc(panel_loaded[s], 16)
                if i == 3:
                    sp.dma_start(const_sb[:, :], constants).then_inc(constants_loaded, 16)
                    sp.dma_start(vec_sb[:, :], vectors).then_inc(vectors_loaded, 16)
                if i == 2 * SLOTS:
                    sp.dma_start(x_sb[:, :], x_in).then_inc(x_loaded, 16)
            sp.wait_ge(stage_done, 3 * len(stages))
            sp.dma_start(out, xS).then_inc(out_stored, 16)
            sp.wait_ge(out_stored, 16)

        @block.tensor
        def _(pe):
            for n, stage in enumerate(stages, 1):
                if stage.tensor is not None:
                    stage.tensor(pe)
                blocks.mark("stage", n)
                rejoin(pe, n)

        @block.scalar
        def _(act):
            steps["act"] = Steps(act, act_step)
            for n, stage in enumerate(stages, 1):
                if stage.scalar is not None:
                    stage.scalar(act)
                rounding.before(act, "stage", n)
                rounding.after_stage.append(rounding.n)
                rejoin(act, n)

        @block.vector
        def _(dve):
            steps["dve"] = Steps(dve, dve_step)
            for n, stage in enumerate(stages, 1):
                if stage.vector is not None:
                    stage.vector(dve)
                rejoin(dve, n)

        @block.gpsimd
        def _(pool):
            steps["pool"] = Steps(pool, pool_step)
            taken = 0
            for n in pool_stages:
                while taken < rounding.after_stage[n - 1]:
                    take_rest(pool, taken)
                    taken += 1
                if n > 1:
                    pool.wait_ge(stage_done, 3 * (n - 1))
                stages[n - 1].gpsimd(pool)
                pool.drain().then_inc(pool_done, 1)
            while taken < len(to_split):
                take_rest(pool, taken)
                taken += 1


def by_partition(a, cols):
    return np.asarray(a).reshape(cols, P).T


def lay_out(inputs):
    _, order, _ = stream_plan()
    w = np.zeros((-(-len(order) // PANEL) * PANEL, P, P), np.float32)
    for n, pieces in enumerate(order):
        for piece in pieces:
            a = inputs[piece.array][piece.index]
            a = a.T if piece.turned else a
            w[n, piece.row:piece.row + a.shape[0], piece.col:piece.col + a.shape[1]] = a
    w = np.ascontiguousarray(w.reshape(-1, PANEL, P, P).transpose(0, 2, 1, 3)).reshape(-1, P, PANEL * P)
    vec_at, sources, n_vec = vector_plan()
    v = np.zeros((P, n_vec), np.float32)
    for at, cols, array, l in sources:
        v[:, at:at + cols] = by_partition(inputs[array][l], cols)
    at, cols = vec_at["log_step"]
    v[:, at:at + cols] = by_partition(np.repeat(inputs["s5_log_step_2"][0], 64), cols)
    for name, array in (("c_re", "s5_c_re_2"), ("c_im", "s5_c_im_2")):
        at, cols = vec_at[name]
        c = np.zeros((P, S5T, 32), np.float32)
        pairs = inputs[array][0].reshape(S5T, 2, 16, 64)
        for j in range(2):
            c[64 * j:64 * j + 64, :, 16 * j:16 * j + 16] = pairs[:, j].transpose(2, 0, 1)
        v[:, at:at + cols] = c.reshape(P, cols)
    tokens = np.concatenate([inputs["x"][0], inputs["ctx"][0]], 0)
    x = np.ascontiguousarray(tokens.T.reshape(KD, P, TOK).transpose(1, 0, 2)).reshape(P, KD * TOK)
    conds = np.stack([inputs["c"][0], inputs["c_ctx"]], -1)
    c = np.ascontiguousarray(conds.reshape(KD, P, 2).transpose(1, 0, 2)).reshape(P, KD * 2)
    constants = np.ascontiguousarray(np.concatenate(list(constant_plan().values()), 1)).astype(np.float32)
    return dict(weights=w, vectors=v, constants=constants, x_in=x, c_in=c)


def kernel(**inputs):
    import concourse.bacc as bacc
    from concourse.bass_utils import run_bass_kernel_spmd

    arrays = lay_out({k: np.asarray(v) for k, v in inputs.items()})
    nc = bacc.Bacc("TRN2", target_bir_lowering=False, num_devices=1)
    args = {k: nc.dram_tensor(k, a.shape, F32, kind="ExternalInput").ap() for k, a in arrays.items()}
    out = nc.dram_tensor("out", (P, KD, SEQ), F32, kind="ExternalOutput").ap()
    build(nc, out=out, **args)
    r = run_bass_kernel_spmd(nc, [arrays], core_ids=[0])
    y = np.asarray(r.results[0]["out"])
    return np.ascontiguousarray(y.transpose(1, 0, 2).reshape(D, SEQ).T)[None]
```
